# Optimizing a Trainium2 kernel written in Bass

```python
import jax, jax.numpy as jnp
from jax import lax
import numpy as np

D_MODEL = 2048
BATCH = 1
SEQ = 256
DEPTH = 1

EPS = 1e-6
HEAD_DIM = 64
ATTN_WIDTH = D_MODEL // 2
N_HEADS_A = ATTN_WIDTH // HEAD_DIM
N_KV_HEADS = 4
GROUP_SIZE = N_HEADS_A // N_KV_HEADS
KV_WIDTH = N_KV_HEADS * HEAD_DIM
IDX_HEADS = 16
IDX_DIM = 64
TOPK_MAX = 256
Q_BLOCK = 128
CONV_WIDTH = D_MODEL // 2
CONV_K = 3
N_GROUPS = 4
EXPERTS_PER_GROUP = 8
N_EXPERTS = N_GROUPS * EXPERTS_PER_GROUP
TOP_K_IN_GROUP = 2
EXPERT_FF = 512
TOKEN_CHUNK = 128
N_MOD = 6
PROJ_SIZES = (ATTN_WIDTH, KV_WIDTH, KV_WIDTH, IDX_HEADS * IDX_DIM, IDX_DIM, IDX_HEADS,
              CONV_WIDTH, CONV_WIDTH, CONV_WIDTH, D_MODEL, D_MODEL)
PROJ_WIDTH = sum(PROJ_SIZES)

kernel_name = 'hybrid_dsa_shortconv_hmoe_block'

def _rmsnorm(x, g):
    xf = x.astype(jnp.float32)
    r = lax.rsqrt(jnp.mean(xf * xf, axis=-1, keepdims=True) + EPS)
    return (xf * r).astype(x.dtype) * g

def _sparse_attention(q, k, v, iq, ik, iw):
    b, s = q.shape[0], q.shape[1]
    k_top = min(TOPK_MAX, s // 4)
    nb = s // Q_BLOCK
    neg = jnp.finfo(jnp.float32).min
    key_pos = jnp.arange(s)
    ik32 = ik.astype(jnp.float32)

    def to_blocks(a):
        return jnp.moveaxis(a.reshape((b, nb, Q_BLOCK) + a.shape[2:]), 1, 0)

    def block(args):
        qb, iqb, iwb, t0 = args
        q_pos = t0 + jnp.arange(Q_BLOCK)
        rel = jax.nn.relu(jnp.einsum('bqhd,bsd->bqhs', iqb.astype(jnp.float32), ik32) * (IDX_DIM ** -0.5))
        score = jnp.einsum('bqhs,bqh->bqs', rel, iwb.astype(jnp.float32) * (IDX_HEADS ** -0.5))
        causal = key_pos[None, :] <= q_pos[:, None]
        score = jnp.where(causal[None], score, neg)
        _, sel = lax.top_k(score, k_top)
        k_sel = jax.vmap(lambda kb, ib: kb[ib])(k, sel)
        v_sel = jax.vmap(lambda vb, ib: vb[ib])(v, sel)
        qg = qb.reshape(b, Q_BLOCK, N_KV_HEADS, GROUP_SIZE, HEAD_DIM)
        logits = jnp.einsum('bqgrd,bqkgd->bqgrk', qg, k_sel).astype(jnp.float32) * (HEAD_DIM ** -0.5)
        valid = (sel <= q_pos[None, :, None])[:, :, None, None, :]
        p = jax.nn.softmax(jnp.where(valid, logits, neg), axis=-1).astype(v.dtype)
        o = jnp.einsum('bqgrk,bqkgd->bqgrd', p, v_sel)
        return o.reshape(b, Q_BLOCK, N_HEADS_A * HEAD_DIM)

    starts = jnp.arange(nb) * Q_BLOCK
    out = lax.map(block, (to_blocks(q), to_blocks(iq), to_blocks(iw), starts))
    return jnp.moveaxis(out, 0, 1).reshape(b, s, N_HEADS_A * HEAD_DIM)

def _short_conv(u, w):
    s = u.shape[1]
    pad = jnp.pad(u, ((0, 0), (CONV_K - 1, 0), (0, 0)))
    y = w[0] * pad[:, 0:s]
    for j in range(1, CONV_K):
        y = y + w[j] * pad[:, j:j + s]
    return y

def _hybrid_mixer(h, w_in, conv_w, w_a_up, w_b_out, w_o):
    b, s, _ = h.shape
    proj = h @ w_in
    points = np.cumsum(PROJ_SIZES)[:-1].tolist()
    q, k, v, iq, ik, iw, bg, cg, xc, gate_a, gate_b = jnp.split(proj, points, axis=-1)
    o_a = _sparse_attention(q.reshape(b, s, N_HEADS_A, HEAD_DIM),
                            k.reshape(b, s, N_KV_HEADS, HEAD_DIM),
                            v.reshape(b, s, N_KV_HEADS, HEAD_DIM),
                            iq.reshape(b, s, IDX_HEADS, IDX_DIM), ik, iw)
    y_a = o_a @ w_a_up
    y_b = (bg * _short_conv(cg * xc, conv_w)) @ w_b_out
    merged = jax.nn.sigmoid(gate_a) * y_a + jax.nn.sigmoid(gate_b) * y_b
    return merged @ w_o

def _hier_moe(h, w_rg, b_rg, w_re, b_re, w_gate, w_up, w_down):
    b, s, d = h.shape
    t = h.reshape(b * s, d)
    g_logits = (t @ w_rg + b_rg).astype(jnp.float32)
    p_group = jax.nn.softmax(g_logits, axis=-1)
    g_sel = jnp.argmax(g_logits, axis=-1)
    e_logits = (t @ w_re + b_re).astype(jnp.float32).reshape(-1, N_GROUPS, EXPERTS_PER_GROUP)
    within = jnp.take_along_axis(e_logits, g_sel[:, None, None], axis=1)[:, 0]
    top_v, top_e = lax.top_k(within, TOP_K_IN_GROUP)
    p_in = jax.nn.softmax(top_v, axis=-1)
    p_g = jnp.take_along_axis(p_group, g_sel[:, None], axis=1)
    weights = p_g * p_in
    eid = g_sel[:, None] * EXPERTS_PER_GROUP + top_e
    combine = jnp.einsum('nk,nke->ne', weights,
                         jax.nn.one_hot(eid, N_EXPERTS, dtype=jnp.float32)).astype(h.dtype)
    nc = t.shape[0] // TOKEN_CHUNK

    def chunk(args):
        tc, cc = args
        a = jnp.einsum('nd,edf->nef', tc, w_gate)
        u = jnp.einsum('nd,edf->nef', tc, w_up)
        act = jax.nn.silu(a) * u * cc[:, :, None]
        return jnp.einsum('nef,efd->nd', act, w_down)

    out = lax.map(chunk, (t.reshape(nc, TOKEN_CHUNK, d), combine.reshape(nc, TOKEN_CHUNK, N_EXPERTS)))
    return out.reshape(b, s, d)

def _normal(key, shape, scale):
    return jax.random.normal(key, shape, jnp.float32) * scale

def setup_inputs(seed: int = 0) -> dict:
    key = jax.random.key(seed)
    ks = jax.random.split(key, 19)
    D = D_MODEL
    return {
        'x': _normal(ks[0], (BATCH, SEQ, D), 1.0),
        'c': _normal(ks[1], (BATCH, D), 1.0),
        'w_ada': _normal(ks[2], (DEPTH, D, N_MOD * D), D ** -0.5),
        'b_ada': _normal(ks[3], (DEPTH, N_MOD * D), 0.02),
        'g_norm_mix': 1.0 + _normal(ks[4], (DEPTH, D), 0.05),
        'w_in': _normal(ks[5], (DEPTH, D, PROJ_WIDTH), D ** -0.5),
        'conv_w': _normal(ks[6], (DEPTH, CONV_K, CONV_WIDTH), CONV_K ** -0.5),
        'w_a_up': _normal(ks[7], (DEPTH, ATTN_WIDTH, D), ATTN_WIDTH ** -0.5),
        'w_b_out': _normal(ks[8], (DEPTH, CONV_WIDTH, D), CONV_WIDTH ** -0.5),
        'w_o': _normal(ks[9], (DEPTH, D, D), D ** -0.5),
        'g_norm_ffn': 1.0 + _normal(ks[10], (DEPTH, D), 0.05),
        'w_rg': _normal(ks[11], (DEPTH, D, N_GROUPS), D ** -0.5),
        'b_rg': _normal(ks[12], (DEPTH, N_GROUPS), 0.01),
        'w_re': _normal(ks[13], (DEPTH, D, N_EXPERTS), D ** -0.5),
        'b_re': _normal(ks[14], (DEPTH, N_EXPERTS), 0.01),
        'w_e_gate': _normal(ks[15], (DEPTH, N_EXPERTS, D, EXPERT_FF), D ** -0.5),
        'w_e_up': _normal(ks[16], (DEPTH, N_EXPERTS, D, EXPERT_FF), D ** -0.5),
        'w_e_down': _normal(ks[17], (DEPTH, N_EXPERTS, EXPERT_FF, D), EXPERT_FF ** -0.5),
        'g_norm_final': 1.0 + _normal(ks[18], (D,), 0.05),
    }

def reference(x, c, w_ada, b_ada, g_norm_mix, w_in, conv_w, w_a_up, w_b_out, w_o,
              g_norm_ffn, w_rg, b_rg, w_re, b_re, w_e_gate, w_e_up, w_e_down, g_norm_final):
    c_act = jax.nn.silu(c)
    for l in range(DEPTH):
        mod = (c_act @ w_ada[l] + b_ada[l])[:, None, :]
        sh1, sc1, g1, sh2, sc2, g2 = jnp.split(mod, N_MOD, axis=-1)
        h = _rmsnorm(x, g_norm_mix[l]) * (1.0 + sc1) + sh1
        x = x + g1 * _hybrid_mixer(h, w_in[l], conv_w[l], w_a_up[l], w_b_out[l], w_o[l])
        h = _rmsnorm(x, g_norm_ffn[l]) * (1.0 + sc2) + sh2
        x = x + g2 * _hier_moe(h, w_rg[l], b_rg[l], w_re[l], b_re[l],
                               w_e_gate[l], w_e_up[l], w_e_down[l])
    return _rmsnorm(x, g_norm_final)


_drawn_inputs = setup_inputs


def setup_inputs(seed=0):
    import zlib

    import numpy as np

    out = dict(_drawn_inputs(seed))
    spreads = {}
    factors = {'b_rg': 3.628, 'b_re': 3.882}
    for name, (base, spread) in spreads.items():
        noise = np.random.default_rng([zlib.crc32(name.encode()), seed]).standard_normal(out[name].shape)
        drawn = base * np.exp(spread * noise) if base else spread * noise
        out[name] = __import__('jax').numpy.asarray(drawn.astype(out[name].dtype))
    for name, factor in factors.items():
        out[name] = (out[name] * factor).astype(out[name].dtype)
    return out
```

```python
from contextlib import ExitStack

import concourse.bass as bass
from concourse import mybir


P = 128
D = 2048
S = 256
HALVES = S // P
KC = D // P
N_MOD = 6
HEAD = 64
KV = 4
ATTN = 1024
CONV = 1024
TAPS = 3
IDX_HEADS = 16
TOPK = 64
GROUPS = 4
EPG = 8
EXPERTS = 32
FF = 512
FC = FF // P
TILE = 64
OVER = (2 * S - 1) // TILE
EPS = 1e-6
NEG = -3.0e38

COL_Q = 0
COL_K = COL_Q + ATTN
COL_V = COL_K + KV * HEAD
COL_IQ = COL_V + KV * HEAD
COL_IK = COL_IQ + IDX_HEADS * HEAD
COL_IW = COL_IK + HEAD
COL_BG = COL_IW + IDX_HEADS
COL_CG = COL_BG + CONV
COL_XC = COL_CG + CONV
COL_GA = COL_XC + CONV
COL_GB = COL_GA + D

SLOTS = 6
UNIT = 256
HC = KC // 2
QC = KC // 4

F32 = mybir.dt.float32
I32 = mybir.dt.int32
ALU = mybir.AluOpType
ACT = mybir.ActivationFunctionType
AX = mybir.AxisListType.X

PLAN = [
    ("norm1", 1, dict(L0=1, L1=1, T0=1, T1=1, A0=1, A1=1, O=1, M=1, v=5)),
    ("mod", 4, dict(w0=1, w1=1, w2=1, w3=1, A0=1, A1=1, acc=2, v=14)),
    ("kv", 1, dict(w4=1, w5=1, w0=1, A0=3, A1=3, v=3)),
    ("idx", 2, dict(w1=1, w2=1, A0=2, A1=2, L0=4, L1=4, qs0=2, qs1=2, rel0=4, rel1=4, v=8)),
    ("topk", 1, dict(v=38)),
    ("main", 4, dict(w3=1, w0=1, w1=1, w2=1, w4=1, w5=1, A0=4, A1=4, L0=2, L1=2, T0=2, T1=2, O=1, M=2,
                     qs0=1, qs1=1, cg0=1, cg1=1, pb0=1, pb1=1, pb2=1, pb3=1, pT0=2, pT1=2, vst=1, acc=2, v=42)),
    ("gate", 8, dict(w0=1, w1=1, w2=1, w3=1, w4=1, w5=1, A0=2, A1=2, L0=2, L1=2, M=3, sg0=2, sg1=2, acc=3, v=45)),
    ("spread", 1, dict(L0=4, L1=4, T0=4, T1=4)),
    ("out", 2, dict(w0=1, w1=1, w2=1, w3=1, A0=4, A1=4)),
    ("norm2", 1, dict(L0=1, L1=1, T0=1, T1=1, A0=1, A1=1, O=1, M=1, v=6)),
    ("route", 1, dict(A0=1, A1=1, v=59)),
    ("expert", EXPERTS + OVER, dict(w0=1, w1=1, w2=1, w3=1, w4=1, w5=1)),
    ("last", 1, dict(v=5)),
]
DMAS = {("gate", "w2"): 3, ("expert", "w0"): 2, ("expert", "w1"): 2, ("expert", "w2"): 2, ("expert", "w3"): 2}
BUFFERS = ("qs0", "qs1", "rel0", "rel1", "cg0", "cg1", "pb0", "pb1", "pb2", "pb3", "pT0", "pT1", "vst", "sg0", "sg1")


def before(name, phase, i=0, pos=0):
    n = 0
    for other, runs, events in PLAN:
        if other == phase:
            return n + i * events.get(name, 0) + pos
        n += runs * events.get(name, 0)


def landed(slot, phase, i=0):
    n = 0
    for other, runs, events in PLAN:
        per = 16 * DMAS.get((other, slot), 1) * events.get(slot, 0)
        if other == phase:
            return n + i * per + per
        n += runs * per


def block_kernel(nc, x, c, w_ada, b_ada, g_norm_mix, w_in, conv_w, w_a_up, w_b_out, w_o, g_norm_ffn,
                 w_rg, b_rg, w_re, b_re, w_e_gate, w_e_up, w_e_down, g_norm_final, out):
    ada_v = w_ada[0].rearrange("(p k) n -> p k n", p=P)
    in_v = w_in[0].rearrange("(p k) n -> p k n", p=P)
    a_up_v = w_a_up[0].rearrange("(j p) n -> p j n", p=P)
    b_out_v = w_b_out[0].rearrange("(j p) n -> p j n", p=P)
    o_v = w_o[0].rearrange("(j p) n -> p j n", p=P)
    gate_v = w_e_gate[0].rearrange("e (p k) f -> e p k f", p=P)
    up_v = w_e_up[0].rearrange("e (p k) f -> e p k f", p=P)
    down_v = w_e_down[0].rearrange("e (p j) d -> e p j d", p=P)
    x_v = x[0].rearrange("(h p) d -> p h d", p=P)
    out_v = out[0].rearrange("(h p) d -> p h d", p=P)

    with ExitStack() as ctx:
        def sb(name, shape, dt=F32):
            return ctx.enter_context(nc.sbuf_tensor(name, shape, dt))

        def sem(name):
            return ctx.enter_context(nc.semaphore(name))

        W = sb("weight_slots", [P, SLOTS, 4096])
        xr = sb("x_resid", [P, HALVES, D])
        RA = sb("region_a", [P, 4096])
        RB = sb("region_b", [P, 4096])
        RM = sb("region_m", [P, 4096])
        RH = sb("region_h", [P, 4096])
        ikd = sb("ik_diag", [P, 2 * S])
        vtok = sb("v_tok", [P, HALVES, KV * HEAD])
        vst = sb("v_stage", [P, HALVES, HEAD])
        amask = sb("attn_mask", [P, HALVES, S])
        qs = sb("q_stage", [P, 2, S])
        pT = sb("probs_T", [P, 2, 512])
        modrow = sb("mod_rows", [P, D])
        acc = sb("ada_acc", [P, 2, UNIT])
        cgT = sb("cg_T", [P, 2, S])
        uT = sb("u_T", [P, 2, S + TAPS - 1])
        ident = sb("ident", [P, P])
        ones = sb("ones", [P, P])
        tri = sb("tri", [P, P])
        cT = sb("c_T", [P, 2, KC])
        modT = sb("mod_T", [P, 2, KC])
        colb = sb("col_b", [P, 3, KC])
        convc = sb("conv_c", [P, TAPS, 8])
        iw = sb("idx_w", [P, HALVES, IDX_HEADS])
        st = sb("stats", [P, 40])
        gb = sb("router_bias", [P, GROUPS + EXPERTS])
        iota = sb("iota", [P, TILE])
        eidx = sb("expert_index", [P, EXPERTS])
        cols = sb("rank_cols", [P, HALVES, 42])
        cwc = sb("weight_cols", [P, HALVES, 42])
        plan_i = sb("plan_i", [1, 16], I32)

        hT = RA[:, :].rearrange("p (k t) -> p k t", k=KC)
        xn = RB[:, :].rearrange("p (h k q) -> p h k q", h=HALVES, k=KC)
        oT = RB[:, 0:2048].rearrange("p (b t) -> p b t", b=8)
        zT = RB[:, 2048:4096].rearrange("p (b t) -> p b t", b=8)
        rows = RM[0:1, :]
        mT = RM[:, :].rearrange("p (b t) -> p b t", b=16)
        kd = RH[:, 0:2048].rearrange("p (g n) -> p g n", g=KV)
        pb = RH[:, 2048:4096].rearrange("p (n m) -> p n m", n=4)
        rel = RH[:, 2048:3072].rearrange("p (h n) -> p h n", h=2)
        score = RH[:, 3072:3584].rearrange("p (h s) -> p h s", h=2)
        work = RH[:, 3584:4096].rearrange("p (h s) -> p h s", h=2)
        acc512 = RH[:, 0:1024].rearrange("p (b n) -> p b n", b=2)
        yb = ikd[:, :].rearrange("p (b t) -> p b t", b=2)
        g1B, g2B = RA[:, 0:2048], RA[:, 2048:4096]
        A2B, B2B = RB[:, 0:2048], RB[:, 2048:4096]
        h2 = RH[:, :].rearrange("p (h k q) -> p h k q", h=HALVES, k=KC)
        h2T = RM[:, :].rearrange("p (k t) -> p k t", k=KC)
        hsel = RM[:, 0:1024].rearrange("p (k s) -> p k s", k=KC)
        gus = RM[:, 1024:1536].rearrange("p (j q) -> p j q", j=FC)
        sil = RM[:, 1536:1792].rearrange("p (j s) -> p j s", j=FC)
        actT = RM[:, 1792:2048].rearrange("p (j s) -> p j s", j=FC)
        ysb = RM[:, 2048:3072]
        pg = RM[:, 3072:3200].rearrange("p (h s) -> p h s", h=2)
        pw = RM[:, 3200:3456].rearrange("p (h s) -> p h s", h=2)
        pt_lo, pt_hi = RB[:, 0:256], RB[:, 256:512]
        g2s = RA[:, 2048:3072]
        gfin = RB[:, 2048:4096]
        wr_g = sb("w_rg_sb", [P, KC, GROUPS])
        wr = cgT[:, :, :].rearrange("p a b -> p (a b)")
        wr_e = wr.rearrange("p (k e) -> p k e", k=KC)

        scratch, at = {}, 512
        for name, shape in dict(lg=(2, 36), gsel=(2, 4), gexp=(2, 4), gm=(2,), zs=(2,), pgr=(2,), down=(32,),
                                val=(2, 32), val2=(2, 32), one=(2, 32), two=(2, 32), choice=(2, 32), m1=(2,),
                                m2=(2,), t2=(2,), t4=(4,), pexp=(2,), p1=(2,), p2=(2,), ov=(32,), incl=(32,),
                                excl=(32,), own=(OVER, 32), first=(OVER, 32), tmp7=(OVER, 32),
                                eid=(OVER,)).items():
            n = shape[0] * (shape[1] if len(shape) > 1 else 1)
            scratch[name] = RB[:, at:at + n] if len(shape) == 1 else \
                RB[:, at:at + n].rearrange("p (a b) -> p a b", a=shape[0])
            at += n
        assert at <= 2048

        def R(name):
            return scratch[name]

        bank = {n: ctx.enter_context(nc.psum_tensor(f"bank_{n}", [P, 512], F32)) for n in ("A0", "A1")}
        pairL = ctx.enter_context(nc.psum_tensor("bank_L", [P, 1024], F32))
        pairT = ctx.enter_context(nc.psum_tensor("bank_T", [P, 1024], F32))
        pairO = ctx.enter_context(nc.psum_tensor("bank_OM", [P, 1024], F32))
        bank.update(L0=pairL[:, 0:512], L1=pairL[:, 512:1024], T0=pairT[:, 0:512], T1=pairT[:, 512:1024],
                    O=pairO[:, 0:512], M=pairO[:, 512:1024], A0=bank["A0"][:, :], A1=bank["A1"][:, :])

        slot_in = {f"w{n}": sem(f"slot{n}_landed") for n in range(SLOTS)}
        slot_free = {f"w{n}": sem(f"slot{n}_free") for n in range(SLOTS)}
        full = {n: sem(f"{n}_full") for n in (*bank, *BUFFERS)}
        free = {n: sem(f"{n}_free") for n in (*bank, *BUFFERS)}
        chain = sem("vector_chain")
        acc_ready = sem("acc_ready")
        names = """c_in x_in small_in modrow_in const_ready pool_step cact_ready ssq_ready ms_ready root_ready
            xn_ready modT_in h_ready kd_ready v_ready ikd_ready iw_ready lg_ready exp_ready fgain_in mT_ready
            gain_in x2_ready h2_ready router_in logits_ready gexp_ready pexp_ready choice_in choice_ready
            gexp_in pexp_in plan_ready pg_ready pw_ready gather_done hsel_ready ptr_done pt_ready pv_done
            gus_ready gut_done sil_ready act_ready y_ready cmb_done add_done fin_ssq fin_ms fin_root
            fin_chain fin_ready stored""".split()
        (c_in, x_in, small_in, modrow_in, const_ready, pool_step, cact_ready, ssq_ready, ms_ready, root_ready,
         xn_ready, modT_in, h_ready, kd_ready, v_ready, ikd_ready, iw_ready, lg_ready, exp_ready, fgain_in, mT_ready,
         gain_in, x2_ready, h2_ready, router_in, logits_ready, gexp_ready, pexp_ready, choice_in, choice_ready,
         gexp_in, pexp_in, plan_ready, pg_ready, pw_ready, gather_done, hsel_ready, ptr_done, pt_ready, pv_done,
         gus_ready, gut_done, sil_ready, act_ready, y_ready, cmb_done, add_done, fin_ssq, fin_ms, fin_root,
         fin_chain, fin_ready, stored) = (sem(n) for n in names)

        def filled(eng, name, phase, i=0, pos=0):
            eng.wait_ge(full[name], before(name, phase, i, pos) + 1)

        def emptied(eng, name, phase, i=0, pos=0):
            eng.wait_ge(free[name], before(name, phase, i, pos) + 1)

        block = ctx.enter_context(nc.Block())

        @block.sync
        def _(sp):
            def claim(slot, phase, i=0):
                sp.wait_ge(slot_free[slot], before(slot, phase, i) + 1)

            def slot_view(n, k):
                return W[:, n, :].rearrange("p (k n) -> p k n", k=k)

            for n in range(SLOTS):
                sp.sem_inc(slot_free[f"w{n}"], 1)
            with sp.Fori(0, 4) as i:
                for n in range(4):
                    at = sp.snap(i * 1024 + (n // 2) * 512)
                    claim(f"w{n}", "mod", i)
                    sp.dma_start(slot_view(n, HC), ada_v[:, (n % 2) * HC:(n % 2 + 1) * HC, bass.ds(at, 512)])\
                        .then_inc(slot_in[f"w{n}"], 16)
            for slot, n, col in (("w4", 4, COL_K), ("w5", 5, COL_V)):
                claim(slot, "kv")
                sp.dma_start(slot_view(n, KC), in_v[:, :, col:col + UNIT]).then_inc(slot_in[slot], 16)
            claim("w0", "kv")
            sp.dma_start(slot_view(0, KC)[:, :, 0:HEAD + IDX_HEADS], in_v[:, :, COL_IK:COL_BG])\
                .then_inc(slot_in["w0"], 16)
            with sp.Fori(0, 2) as i:
                for b in range(2):
                    at = sp.snap(i * 512 + COL_IQ + b * UNIT)
                    claim(f"w{1 + b}", "idx", i)
                    sp.dma_start(slot_view(1 + b, KC), in_v[:, :, bass.ds(at, UNIT)])\
                        .then_inc(slot_in[f"w{1 + b}"], 16)
            with sp.Fori(0, KV) as i:
                for n, col in ((3, COL_Q), (0, COL_CG), (1, COL_XC), (2, COL_BG)):
                    at = sp.snap(i * UNIT + col)
                    claim(f"w{n}", "main", i)
                    sp.dma_start(slot_view(n, KC), in_v[:, :, bass.ds(at, UNIT)])\
                        .then_inc(slot_in[f"w{n}"], 16)
                for b in range(2):
                    at = sp.snap(i * 512 + 2 * D + b * UNIT)
                    claim(f"w{4 + b}", "main", i)
                    sp.dma_start(slot_view(4 + b, KC), ada_v[:, :, bass.ds(at, UNIT)])\
                        .then_inc(slot_in[f"w{4 + b}"], 16)
            with sp.Fori(0, 8) as i:
                for n, col in ((0, COL_GA), (1, COL_GB)):
                    at = sp.snap(i * UNIT + col)
                    claim(f"w{n}", "gate", i)
                    sp.dma_start(slot_view(n, KC), in_v[:, :, bass.ds(at, UNIT)])\
                        .then_inc(slot_in[f"w{n}"], 16)
                at = sp.snap(i * UNIT)
                claim("w2", "gate", i)
                for q in (4, 0):
                    sp.dma_start(slot_view(2, KC)[:, q:q + 4, :], a_up_v[:, q:q + 4, bass.ds(at, UNIT)])\
                        .then_inc(slot_in["w2"], 16)
                sp.dma_start(slot_view(2, KC)[:, 8:16, :], b_out_v[:, :, bass.ds(at, UNIT)])\
                    .then_inc(slot_in["w2"], 16)
                for n in range(3):
                    at = sp.snap(i * UNIT + (3 + n) * D)
                    claim(f"w{3 + n}", "gate", i)
                    sp.dma_start(slot_view(3 + n, KC), ada_v[:, :, bass.ds(at, UNIT)])\
                        .then_inc(slot_in[f"w{3 + n}"], 16)
            with sp.Fori(0, 2) as i:
                for b in range(4):
                    at = sp.snap(i * 1024 + b * UNIT)
                    claim(f"w{b}", "out", i)
                    sp.dma_start(slot_view(b, KC), o_v[:, :, bass.ds(at, UNIT)])\
                        .then_inc(slot_in[f"w{b}"], 16)

            def load_expert(e, t):
                for n in range(4):
                    claim(f"w{n}", "expert", t)
                    v = W[:, n, :].rearrange("p (g k f) -> p g k f", g=2, k=QC)
                    for g, src in ((0, gate_v), (1, up_v)):
                        sp.dma_start(v[:, g], src[e][:, n * QC:(n + 1) * QC, :]).then_inc(slot_in[f"w{n}"], 16)
                for n in range(2):
                    claim(f"w{4 + n}", "expert", t)
                    sp.dma_start(W[:, 4 + n, :].rearrange("p (j d) -> p j d", j=2),
                                 down_v[e][:, 2 * n:2 * n + 2, :]).then_inc(slot_in[f"w{4 + n}"], 16)

            with sp.Fori(0, EXPERTS) as e:
                load_expert(e, e)
            sp.wait_ge(plan_ready, 1)
            n_over = sp.value_load(plan_i[0:1, 8:9], min_val=0, max_val=OVER)
            with sp.Fori(0, OVER) as o:
                with sp.If(o < n_over):
                    e = sp.value_load(plan_i[0:1, bass.ds(o, 1)], min_val=0, max_val=EXPERTS - 1)
                    load_expert(e, o + EXPERTS)
            for h in range(HALVES):
                sp.wait_ge(fin_ready, h + 1)
                sp.dma_start(out_v[:, h, :], xr[:, h, :]).then_inc(stored, 16)
            sp.wait_ge(stored, 16 * HALVES)

        @block.gpsimd
        def _(pool):
            g = nc.gpsimd
            g.memset(ones[:, :], 1.0).then_inc(pool_step, 1)
            g.memset(ident[:, :], 0.0).then_inc(pool_step, 1)
            pool.wait_ge(pool_step, 2)
            g.affine_select(out=ident[:, :], in_=ident[:, :], compare_op=ALU.not_equal, fill=1.0, base=0,
                            pattern=[[-1, P]], channel_multiplier=1).then_inc(const_ready, 1)
            g.memset(modrow[:, :], 0.0).then_inc(const_ready, 1)
            g.affine_select(out=tri[:, :], in_=ones[:, :], compare_op=ALU.is_gt, fill=0.0, base=0,
                            pattern=[[1, P]], channel_multiplier=-1).then_inc(const_ready, 1)
            g.iota(iota[:, :], pattern=[[1, TILE]], base=0, channel_multiplier=0,
                   allow_small_or_imprecise_dtypes=True).then_inc(const_ready, 1)
            g.iota(eidx[:, :], pattern=[[1, EXPERTS]], base=0, channel_multiplier=0,
                   allow_small_or_imprecise_dtypes=True).then_inc(const_ready, 1)
            g.memset(amask[:, :, :], 0.0).then_inc(pool_step, 1)
            pool.wait_ge(pool_step, 3)
            g.affine_select(out=amask[:, :, :], in_=amask[:, :, :], compare_op=ALU.is_ge, fill=NEG, base=0,
                            pattern=[[P, HALVES], [-1, S]], channel_multiplier=1).then_inc(const_ready, 1)
            g.memset(ikd[:, :], 0.0).then_inc(const_ready, 1)
            g.memset(uT[:, :, 0:TAPS - 1], 0.0).then_inc(const_ready, 1)
            g.memset(cols[:, :, :], -1.0).then_inc(const_ready, 1)
            g.memset(cwc[:, :, :], 0.0).then_inc(const_ready, 1)
            g.memset(score, 0.0).then_inc(const_ready, 1)
            emptied(pool, "A0", "kv")
            emptied(pool, "A1", "kv")
            g.memset(RH[:, 0:2048], 0.0).then_inc(const_ready, 1)
            pool.wait_ge(v_ready, 2)
            with pool.Fori(0, KV) as i:
                emptied(pool, "vst", "main", i)
                g.tensor_copy(vst[:, :, :], vtok[:, :, bass.ds(i * HEAD, HEAD)]).then_inc(full["vst"], 1)

        @block.scalar
        def _(act):
            a = nc.scalar
            for name in free:
                act.sem_inc(free[name], 1)

            act.dma_start(cT[:, 0, :], c[0].rearrange("(p k) -> p k", p=P)).then_inc(c_in, 16)
            for h in range(HALVES):
                act.dma_start(xr[:, h, :], x_v[:, h, :]).then_inc(x_in, 16)
            act.dma_start(colb[:, 0, :], b_ada[0, 0:D].rearrange("(p k) -> p k", p=P)).then_inc(small_in, 16)
            act.dma_start(colb[:, 1, :], b_ada[0, D:2 * D].rearrange("(p k) -> p k", p=P)).then_inc(small_in, 16)
            act.dma_start(colb[:, 2, :], g_norm_mix[0].rearrange("(p k) -> p k", p=P)).then_inc(small_in, 16)
            for j in range(TAPS):
                act.dma_start(convc[:, j, :], conv_w[0, j].rearrange("(b p) -> p b", p=P),
                              allow_slow_non_contiguous=True).then_inc(small_in, 16)
            act.dma_start(wr_g[:, :, :], w_rg[0].rearrange("(p k) e -> p k e", p=P)).then_inc(small_in, 16)
            act.dma_start(gb[:, 0:GROUPS], b_rg[0:1, :].to_broadcast([P, GROUPS])).then_inc(small_in, 16)
            act.dma_start(gb[:, GROUPS:], b_re[0:1, :].to_broadcast([P, EXPERTS])).then_inc(small_in, 16)
            act.wait_ge(const_ready, 2)
            for v in range(4):
                act.dma_start(modrow[32 * v:32 * v + 1, :], b_ada[0:1, (2 + v) * D:(3 + v) * D])\
                    .then_inc(modrow_in, 16)

            act.wait_ge(c_in, 16)
            a.activation(cT[:, 1, :], cT[:, 0, :], ACT.Silu).then_inc(cact_ready, 1)
            act.wait_ge(x_in, 16 * HALVES)
            for h in range(HALVES):
                a.activation(RB[:, h * D:(h + 1) * D], xr[:, h, :], ACT.Square,
                             accum_out=st[:, h:h + 1]).then_inc(ssq_ready, 1)
            act.wait_ge(ms_ready, 1)
            a.activation(st[:, 4:6], st[:, 2:4], ACT.Sqrt).then_inc(root_ready, 1)
            for n, name in enumerate(("L0", "L1", "T0", "T1", "A0", "A1", "O", "M")):
                h, k = n // 4, (n % 4) * 4
                filled(act, name, "norm1")
                a.activation(hT[:, k:k + 4, h * P:(h + 1) * P],
                             bank[name].rearrange("p (k t) -> p k t", k=4), ACT.Copy).then_inc(free[name], 1)
            with act.Fori(0, 4) as i:
                for b in range(2):
                    filled(act, f"A{b}", "mod", i)
                    a.activation(rows[:, bass.ds(i * 1024 + b * 512, 512)], bank[f"A{b}"][0:1, :], ACT.Copy)\
                        .then_inc(free[f"A{b}"], 1)
            emptied(act, "A0", "kv")
            emptied(act, "A1", "kv")
            for v in range(2):
                act.dma_start(modT[:, v, :], rows[0:1, v * D:(v + 1) * D].rearrange("o (p k) -> o p k", k=KC))\
                    .then_inc(modT_in, 16)
            for h in range(HALVES):
                filled(act, f"A{h}", "kv", 0, 1)
                if h == 1:
                    act.sem_inc(slot_free["w5"], 1)
                a.activation(vtok[:, h, :], bank[f"A{h}"][:, 0:UNIT], ACT.Copy).then_inc(v_ready, 1)
                act.wait_ge(v_ready, h + 1)
                act.sem_inc(free[f"A{h}"], 1)
            filled(act, "A0", "kv", 0, 2)
            act.wait_ge(const_ready, 11)
            a.activation(ikd[0:HEAD, 0:S], bank["A0"][0:HEAD, 0:S], ACT.Copy).then_inc(ikd_ready, 1)
            a.activation(ikd[HEAD:P, S:2 * S], bank["A0"][0:HEAD, 0:S], ACT.Copy).then_inc(ikd_ready, 1)
            act.wait_ge(ikd_ready, 2)
            act.sem_inc(free["A0"], 1)

            with act.Fori(0, 2) as i:
                for b in range(2):
                    for j in range(2):
                        filled(act, f"A{j}", "idx", i, b)
                        if j == 1:
                            act.sem_inc(slot_free[f"w{1 + b}"], 1)
                        a.activation(qs[:, j, :], bank[f"A{j}"][:, 0:S], ACT.Copy).then_inc(full[f"qs{j}"], 1)
                    for j in range(2):
                        for h in range(HALVES):
                            filled(act, f"L{h}", "idx", i, 2 * b + j)
                            emptied(act, f"rel{h}", "idx", i, 2 * b + j)
                            a.activation(rel[:, h, :], bank[f"L{h}"], ACT.Relu).then_inc(full[f"rel{h}"], 1)

            with act.Fori(0, KV) as i:
                def cg(j):
                    filled(act, f"A{j}", "main", i, 1)
                    emptied(act, f"cg{j}", "main", i)
                    if j == 1:
                        act.sem_inc(slot_free["w0"], 1)
                    a.activation(cgT[:, j, :], bank[f"A{j}"][:, 0:S], ACT.Copy).then_inc(full[f"cg{j}"], 1)
                    filled(act, f"cg{j}", "main", i)
                    act.sem_inc(free[f"A{j}"], 1)

                def expo(n):
                    act.wait_ge(lg_ready, i * 4 + n + 1)
                    for h in range(2):
                        a.activation(pb[:, n, h * S:(h + 1) * S], pb[:, n, h * S:(h + 1) * S], ACT.Exp,
                                     bias=st[:, 8 + 2 * n + h:9 + 2 * n + h],
                                     accum_out=st[:, 16 + 2 * n + h:17 + 2 * n + h]).then_inc(exp_ready, 1)

                for j in range(2):
                    filled(act, f"A{j}", "main", i, 0)
                    if j == 1:
                        act.sem_inc(slot_free["w3"], 1)
                    a.activation(qs[:, j, :], bank[f"A{j}"][:, 0:S], ACT.Copy).then_inc(full[f"qs{j}"], 1)
                cg(0)
                expo(0)
                expo(1)
                cg(1)
                expo(2)
                expo(3)
                for n in range(4):
                    filled(act, f"T{n % 2}", "main", i, n // 2)
                    if n >= 2:
                        act.wait_ge(pv_done, i * 2 + n - 1)
                    a.activation(pT[:, n % 2, :], bank[f"T{n % 2}"], ACT.Copy).then_inc(full[f"pT{n % 2}"], 1)
                filled(act, "O", "main", i)
                act.sem_inc(free["vst"], 1)
                a.activation(RB[:, bass.ds(i * 512, 512)], bank["O"], ACT.Copy).then_inc(free["O"], 1)

            for j in range(2):
                emptied(act, f"cg{j}", "gate")
            act.dma_start(wr_e, w_re[0].rearrange("(p k) e -> p k e", p=P)).then_inc(router_in, 16)
            with act.Fori(0, 8) as i:
                for j in range(2):
                    for b in range(2):
                        filled(act, f"A{b}", "gate", i, j)
                        if j == 1:
                            act.sem_inc(slot_free[f"w{b}"], 1)
                        emptied(act, f"sg{b}", "gate", i, j)
                        a.activation(qs[:, b, :], bank[f"A{b}"][:, 0:S], ACT.Sigmoid).then_inc(full[f"sg{b}"], 1)
            filled(act, "L0", "spread")
            act.dma_start(A2B, g_norm_ffn[0:1, :].to_broadcast([P, D])).then_inc(fgain_in, 16)
            for turn, dst in enumerate((g1B, B2B, None)):
                for q, name in enumerate(("L0", "L1", "T0", "T1")):
                    filled(act, name, "spread", 0, turn)
                    if dst is not None:
                        o, src = dst[:, q * 512:(q + 1) * 512], bank[name]
                    else:
                        r = slice(64 * (q // 2), 64 * (q // 2) + 64)
                        o, src = g2s[r, (q % 2) * 512:(q % 2 + 1) * 512], bank[name][r, :]
                    a.activation(o, src, ACT.Copy).then_inc(free[name], 1)
            act.wait_ge(x2_ready, 16)
            for h in range(HALVES):
                a.activation(RM[:, h * D:(h + 1) * D], xr[:, h, :], ACT.Square,
                             accum_out=st[:, h:h + 1]).then_inc(ssq_ready, 1)
            act.wait_ge(ms_ready, 2)
            a.activation(st[:, 4:6], st[:, 2:4], ACT.Sqrt).then_inc(root_ready, 1)
            for n, name in enumerate(("L0", "L1", "T0", "T1", "A0", "A1", "O", "M")):
                h, k = n // 4, (n % 4) * 4
                filled(act, name, "norm2")
                a.activation(h2T[:, k:k + 4, h * P:(h + 1) * P],
                             bank[name].rearrange("p (k t) -> p k t", k=4), ACT.Copy).then_inc(free[name], 1)
            act.wait_ge(h2_ready, 2)
            act.dma_start(gfin, g_norm_final.rearrange("(o d) -> o d", o=1).to_broadcast([P, D])).then_inc(gain_in, 16)
            act.wait_ge(gexp_in, 1)
            a.activation(R("gexp"), R("gexp"), ACT.Exp).then_inc(gexp_ready, 1)
            act.wait_ge(pexp_in, 1)
            a.activation(R("pexp"), R("pexp"), ACT.Exp).then_inc(pexp_ready, 1)

            def mask_evac(t):
                act.wait_ge(ptr_done, t + 1)
                a.activation(pt_lo[0:TILE, :], bank["A1"][0:TILE, 0:S], ACT.Copy)
                a.activation(pt_hi[TILE:P, :], bank["A1"][TILE:P, 0:S], ACT.Copy).then_inc(pt_ready, 1)

            def gather_evac(t):
                act.wait_ge(gather_done, t + 1)
                a.activation(RM[:, 0:1024], pairL[:, :], ACT.Copy).then_inc(hsel_ready, 1)

            def tile(t):
                mask_evac(t)
                act.wait_ge(slot_free["w3"], before("w3", "expert", t) + 2)
                a.activation(gus, bank["A0"].rearrange("p (q j) -> p j q", j=FC), ACT.Copy).then_inc(gus_ready, 1)
                gather_evac(t + 1)
                act.wait_ge(gut_done, t + 1)
                a.activation(sil, bank["A1"].rearrange("p (j s) -> p j s", j=FC)[:, :, 0:TILE], ACT.Silu)\
                    .then_inc(sil_ready, 1)

            gather_evac(0)
            with act.Fori(0, EXPERTS) as e:
                tile(e)
            act.wait_ge(plan_ready, 1)
            n_over = act.value_load(plan_i[0:1, 8:9], min_val=0, max_val=OVER)
            with act.Fori(0, OVER) as o:
                with act.If(o < n_over):
                    tile(o + EXPERTS)
            mask_evac(n_over + EXPERTS)
            act.wait_ge(fin_chain, 1)
            for h in range(HALVES):
                a.activation(RH[:, h * D:(h + 1) * D], xr[:, h, :], ACT.Square,
                             accum_out=st[:, h:h + 1]).then_inc(fin_ssq, 1)
            act.wait_ge(fin_ms, 1)
            a.activation(st[:, 4:6], st[:, 2:4], ACT.Sqrt).then_inc(fin_root, 1)

        @block.tensor
        def _(pe):
            mm = nc.tensor.matmul
            A0, A1 = bank["A0"], bank["A1"]

            def slot(n, phase, i=0):
                pe.wait_ge(slot_in[f"w{n}"], landed(f"w{n}", phase, i))

            def unit(n):
                return W[:, n, :].rearrange("p (k n) -> p k n", k=KC)

            def project(name, phase, i, pos, n, j, first=False):
                emptied(pe, name, phase, i, pos)
                w = unit(n)
                for k in range(KC):
                    if first:
                        pe.wait_ge(h_ready, k + 1)
                    last = mm(bank[name][:, 0:S], w[:, k, j * P:(j + 1) * P], hT[:, k, :],
                              start=(k == 0), stop=(k == KC - 1))
                return last

            def transposes(src, phase):
                for n, name in enumerate(("L0", "L1", "T0", "T1", "A0", "A1", "O", "M")):
                    h, k = n // 4, (n % 4) * 4
                    emptied(pe, name, phase)
                    for q in range(4):
                        last = nc.tensor.transpose(bank[name][:, q * P:(q + 1) * P], src[:, h, k + q, :], ident[:, :])
                    last.then_inc(full[name], 1)

            pe.wait_ge(const_ready, 1)
            pe.wait_ge(xn_ready, 2)
            transposes(xn, "norm1")
            pe.wait_ge(cact_ready, 1)
            with pe.Fori(0, 4) as i:
                for b in range(2):
                    name = f"A{b}"
                    emptied(pe, name, "mod", i)
                    slot(2 * b, "mod", i)
                    w = W[:, 2 * b, :].rearrange("p (k n) -> p k n", k=HC)
                    for k in range(HC):
                        last = mm(bank[name][0:1, :], cT[:, 1, k:k + 1], w[:, k, :], start=(k == 0), stop=False,
                                  skip_group_check=True)
                    last.then_inc(slot_free[f"w{2 * b}"], 1)
                    pe.wait_ge(acc_ready, before("acc", "mod", i, b) + 1)
                    mm(bank[name][0:1, 0:256], ones[:, 0:1], acc512[:, b, 0:256], start=False, stop=False,
                       skip_group_check=True).then_inc(slot_free[f"w{2 * b + 1}"], 1)
                    mm(bank[name][0:1, 256:512], ones[:, 0:1], acc512[:, b, 256:512], start=False, stop=True,
                       skip_group_check=True).then_inc(full[name], 1)

            slot(4, "kv")
            for j in range(2):
                last = project(f"A{j}", "kv", 0, 0, 4, j, first=(j == 0))
                last.then_inc(full[f"A{j}"], 1)
            slot(5, "kv")
            for h in range(HALVES):
                emptied(pe, f"A{h}", "kv", 0, 1)
                for k in range(KC):
                    last = mm(bank[f"A{h}"][:, 0:UNIT], hT[:, k, h * P:(h + 1) * P], unit(5)[:, k, :],
                              start=(k == 0), stop=(k == KC - 1))
                last.then_inc(full[f"A{h}"], 1)
            slot(0, "kv")
            emptied(pe, "A0", "kv", 0, 2)
            for k in range(KC):
                last = mm(A0[0:HEAD, 0:S], unit(0)[:, k, 0:HEAD], hT[:, k, :], start=(k == 0), stop=(k == KC - 1))
            last.then_inc(full["A0"], 1)
            emptied(pe, "A1", "kv", 0, 2)
            for h in range(HALVES):
                for k in range(KC):
                    last = mm(A1[:, h * 16:h * 16 + 16], hT[:, k, h * P:(h + 1) * P],
                              unit(0)[:, k, HEAD:HEAD + IDX_HEADS], start=(k == 0), stop=(k == KC - 1))
            last.then_inc(full["A1"], 1)

            pe.wait_ge(ikd_ready, 2)
            with pe.Fori(0, 2) as i:
                for b in range(2):
                    slot(1 + b, "idx", i)
                    for j in range(2):
                        project(f"A{j}", "idx", i, b, 1 + b, j).then_inc(full[f"A{j}"], 1)
                    for j in range(2):
                        filled(pe, f"qs{j}", "idx", i, b)
                        pe.sem_inc(free[f"A{j}"], 1)
                        for h in range(HALVES):
                            emptied(pe, f"L{h}", "idx", i, 2 * b + j)
                            last = mm(bank[f"L{h}"], qs[:, j, h * P:(h + 1) * P], ikd[:, :], start=True, stop=True)
                            last.then_inc(full[f"L{h}"], 1)

            pe.wait_ge(kd_ready, 2)
            with pe.Fori(0, KV) as i:
                def logits(n):
                    j, h = n // 2, n % 2
                    emptied(pe, f"L{n % 2}", "main", i, n // 2)
                    mm(bank[f"L{n % 2}"], qs[:, j, h * P:(h + 1) * P], RH[:, bass.ds(i * 512, 512)],
                       start=True, stop=True).then_inc(full[f"L{n % 2}"], 1)

                def turn(n):
                    filled(pe, f"pb{n}", "main", i)
                    emptied(pe, f"T{n % 2}", "main", i, n // 2)
                    for q in range(4):
                        last = nc.tensor.transpose(bank[f"T{n % 2}"][:, q * P:(q + 1) * P],
                                                   pb[:, n, q * P:(q + 1) * P], ident[:, :])
                    last.then_inc(full[f"T{n % 2}"], 1)

                def values(n):
                    j, h = n // 2, n % 2
                    filled(pe, f"pT{n % 2}", "main", i, n // 2)
                    pe.sem_inc(free[f"T{n % 2}"], 1)
                    for s in range(HALVES):
                        for a in range(2):
                            last = mm(bank["O"][a * HEAD:(a + 1) * HEAD, j * S + h * P:j * S + (h + 1) * P],
                                      vst[:, s, :], pT[:, n % 2, (2 * a + s) * P:(2 * a + s + 1) * P],
                                      start=(s == 0), stop=(s == HALVES - 1), skip_group_check=True)
                            if a == 1 and s == 0:
                                last.then_inc(free[f"pb{n}"], 1)
                    if n == 3:
                        last.then_inc(full["O"], 1)
                    elif n < 2:
                        last.then_inc(pv_done, 1)

                def spread_sum(b, n):
                    pe.wait_ge(acc_ready, before("acc", "main", i, b) + 1)
                    emptied(pe, "M", "main", i, b)
                    mm(bank["M"][:, 0:P], ones[:, :], acc[:, b, 0:P], start=True, stop=True)\
                        .then_inc(slot_free[f"w{n}"], 1)
                    mm(bank["M"][:, P:UNIT], ones[:, :], acc[:, b, P:UNIT], start=True, stop=True)\
                        .then_inc(full["M"], 1)

                def staged(j):
                    filled(pe, f"qs{j}", "main", i)
                    pe.sem_inc(free[f"A{j}"], 1)

                def block_of(n, pos, j):
                    if j == 0:
                        slot(n, "main", i)
                    project(f"A{j}", "main", i, pos, n, j).then_inc(full[f"A{j}"], 1)

                block_of(3, 0, 0)
                block_of(3, 0, 1)
                staged(0)
                block_of(0, 1, 0)
                staged(1)
                logits(0)
                logits(1)
                block_of(0, 1, 1)
                block_of(1, 2, 0)
                logits(2)
                logits(3)
                spread_sum(0, 4)
                block_of(1, 2, 1)
                block_of(2, 3, 0)
                turn(0)
                turn(1)
                block_of(2, 3, 1)
                filled(pe, "vst", "main", i)
                emptied(pe, "O", "main", i)
                values(0)
                values(1)
                turn(2)
                turn(3)
                spread_sum(1, 5)
                values(2)
                values(3)

            emptied(pe, "O", "gate")
            with pe.Fori(0, 8) as i:
                def branch(name, j, half, src):
                    emptied(pe, name, "gate", i, j)
                    w = unit(2)
                    for q in range(8):
                        last = mm(bank[name][:, 0:S], w[:, 8 * half + q, j * P:(j + 1) * P], src[:, q, :],
                                  start=(q == 0), stop=(q == 7))
                    return last

                def spread_sum(n):
                    pe.wait_ge(acc_ready, before("acc", "gate", i, n) + 1)
                    emptied(pe, "M", "gate", i, n)
                    mm(bank["M"][:, 0:P], ones[:, :], acc[:, n % 2, 0:P], start=True, stop=True)\
                        .then_inc(slot_free[f"w{3 + n}"], 1)
                    mm(bank["M"][:, P:UNIT], ones[:, :], acc[:, n % 2, P:UNIT], start=True, stop=True)\
                        .then_inc(full["M"], 1)

                for j in range(2):
                    if j == 0:
                        slot(0, "gate", i)
                    project("A0", "gate", i, j, 0, j).then_inc(full["A0"], 1)
                    if j == 0:
                        slot(2, "gate", i)
                    branch("L0", j, 0, oT).then_inc(full["L0"], 1)
                    if j == 0:
                        slot(1, "gate", i)
                    project("A1", "gate", i, j, 1, j).then_inc(full["A1"], 1)
                    branch("L1", j, 1, zT).then_inc(full["L1"], 1)
                    if j == 0:
                        spread_sum(0)
                spread_sum(1)
                spread_sum(2)

            emptied(pe, "M", "norm2")
            for turn, v in enumerate((0, 1, 3, 2)):
                for q, name in enumerate(("L0", "L1", "T0", "T1")):
                    emptied(pe, name, "spread", 0, turn)
                    mm(bank[name], ident[:, 32 * v:32 * v + 1].to_broadcast([P, P]),
                       modrow[:, q * 512:(q + 1) * 512], start=True, stop=True).then_inc(full[name], 1)

            pe.wait_ge(mT_ready, 16)
            with pe.Fori(0, 2) as i:
                for b in range(4):
                    slot(b, "out", i)
                    for h in range(HALVES):
                        emptied(pe, f"A{h}", "out", i, b)
                        for q in range(KC):
                            last = mm(bank[f"A{h}"][:, 0:UNIT], mT[:, q, h * P:(h + 1) * P], unit(b)[:, q, :],
                                      start=(q == 0), stop=(q == KC - 1))
                        last.then_inc(full[f"A{h}"], 1)

            pe.wait_ge(h2_ready, 2)
            transposes(h2, "norm2")
            emptied(pe, "A0", "route")
            for name in ("L0", "L1", "T0", "T1"):
                emptied(pe, name, "route")
            for name in ("A1", "O", "M"):
                emptied(pe, name, "route")
            pe.wait_ge(router_in, 16)
            pe.wait_ge(small_in, 16 * 9)
            for h in range(HALVES):
                for o, n, w in ((0, GROUPS, wr_g), (GROUPS, EXPERTS, wr_e)):
                    for k in range(KC):
                        last = mm(A0[:, 64 * h + o:64 * h + o + n], h2T[:, k, h * P:(h + 1) * P], w[:, k, :],
                                  start=(k == 0), stop=(k == KC - 1))
            last.then_inc(full["A0"], 1)
            pe.wait_ge(choice_ready, 1)
            m0, m1 = R("choice")[:, 0, :], R("choice")[:, 1, :]
            mm(A1[:, 0:32], tri[:, :], m0, start=True, stop=True)
            mm(A1[:, 32:64], tri[:, :], m1, start=True, stop=False)
            mm(A1[:, 32:64], ones[:, :], m0, start=False, stop=True)
            mm(A1[:, 64:96], ones[:, :], m0, start=True, stop=False)
            mm(A1[:, 64:96], ones[:, :], m1, start=False, stop=True).then_inc(full["A1"], 1)

            def gather(t):
                pe.wait_ge(pg_ready, t + 1)
                for k in range(KC):
                    for h in range(HALVES):
                        last = mm(pairL[:, k * TILE:(k + 1) * TILE], h2[:, h, k, :], pg[:, h, :],
                                  start=(h == 0), stop=(h == HALVES - 1))
                last.then_inc(gather_done, 1)

            def combine_mask(t):
                pe.wait_ge(pw_ready, t + 1)
                pe.wait_ge(act_ready, t + 1)
                for h in range(HALVES):
                    last = nc.tensor.transpose(A1[:, h * P:(h + 1) * P], pw[:, h, :], ident[:, :])
                last.then_inc(ptr_done, 1)

            def combine(t):
                pe.wait_ge(pt_ready, t + 1)
                pe.wait_ge(y_ready, t + 1)
                for n in range(8):
                    h, q = n // 4, n % 4
                    pe.wait_ge(add_done, t * 8 + n + 1)
                    mm(bank["OM"[n % 2]], (pt_lo if q < 2 else pt_hi)[:, h * P:(h + 1) * P],
                       ysb[:, (q % 2) * 512:(q % 2 + 1) * 512], start=True, stop=True).then_inc(cmb_done, 1)

            def tile(t):
                combine_mask(t)
                pe.wait_ge(hsel_ready, t + 1)
                pe.wait_ge(gus_ready, t + 1)
                for n in range(4):
                    slot(n, "expert", t)
                    w = W[:, n, :].rearrange("p (g k f) -> p g k f", g=2, k=QC)
                    for k in range(QC):
                        ks = n * QC + k
                        for g in range(2):
                            last = mm(A0[g * TILE:(g + 1) * TILE, :], hsel[:, ks, :], w[:, g, k, :],
                                      start=(ks == 0), stop=(ks == KC - 1), skip_group_check=True)
                    last.then_inc(slot_free[f"w{n}"], 1)
                gather(t + 1)
                pe.wait_ge(gus_ready, t + 2)
                pe.wait_ge(pt_ready, t + 1)
                for j in range(FC):
                    last = nc.tensor.transpose(A1[:, j * P:(j + 1) * P], gus[:, j, :], ident[:, :])
                last.then_inc(gut_done, 1)
                combine(t)
                pe.wait_ge(act_ready, t + 2)
                for n in range(2):
                    slot(4 + n, "expert", t)
                    w = W[:, 4 + n, :].rearrange("p (j g d) -> p j g d", j=2, g=2)
                    for j in range(2):
                        js = 2 * n + j
                        for q in range(2):
                            for g in range(2):
                                last = mm(pairT[g * TILE:(g + 1) * TILE, q * 512:(q + 1) * 512], actT[:, js, :],
                                          w[:, j, g, q * 512:(q + 1) * 512], start=(js == 0), stop=(js == FC - 1),
                                          skip_group_check=True)
                    last.then_inc(slot_free[f"w{4 + n}"], 1)

            pe.wait_ge(pg_ready, 1)
            gather(0)
            with pe.Fori(0, EXPERTS) as e:
                tile(e)
            pe.wait_ge(plan_ready, 1)
            n_over = pe.value_load(plan_i[0:1, 8:9], min_val=0, max_val=OVER)
            with pe.Fori(0, OVER) as o:
                with pe.If(o < n_over):
                    tile(o + EXPERTS)
            combine_mask(n_over + EXPERTS)
            combine(n_over + EXPERTS)

        @block.vector
        def _(dve):
            v = nc.vector
            place = [None, 0]

            def enter(phase, i=0):
                place[:] = [before("v", phase, i), 0]

            def leave(phase):
                want = {n: e.get("v", 0) for n, _, e in PLAN}[phase]
                assert place[1] == want, (phase, place[1], want)

            def link(ins):
                place[1] += 1
                ins.then_inc(chain, 1)
                dve.wait_ge(chain, place[0] + place[1])

            def inverse_root(col, ms_sem, root_sem, turn):
                v.tensor_scalar(st[:, 2:4], st[:, 0:2], 1.0 / D, EPS, ALU.mult, ALU.add).then_inc(ms_sem, 1)
                dve.wait_ge(root_sem, turn)
                link(v.reciprocal(st[:, 6:8], st[:, 4:6]))
                link(v.tensor_tensor(st[:, 4:6], st[:, 6:8], st[:, 6:8], ALU.mult))
                link(v.tensor_tensor(st[:, 4:6], st[:, 4:6], st[:, 2:4], ALU.mult))
                link(v.tensor_scalar(st[:, 4:6], st[:, 4:6], -0.5, 1.5, ALU.mult, ALU.add))
                link(v.tensor_tensor(st[:, 6:8], st[:, 6:8], st[:, 4:6], ALU.mult))

            def weigh(dst, w, chunks, k0):
                n = len(chunks)
                for q, k in enumerate(chunks):
                    cs = cT[:, 1, k:k + 1]
                    if q == 0:
                        link(v.tensor_scalar(dst, w[:, k - k0, :], cs, None, ALU.mult))
                    else:
                        ins = v.scalar_tensor_tensor(out=dst, in0=w[:, k - k0, :], scalar=cs, in1=dst,
                                                     op0=ALU.mult, op1=ALU.add)
                        if q < n - 1:
                            link(ins)
                        else:
                            ins.then_inc(acc_ready, 1)

            enter("norm1")
            dve.wait_ge(ssq_ready, 2)
            inverse_root(0, ms_ready, root_ready, 1)
            for h in range(HALVES):
                v.tensor_scalar(xn[:, h, :, :], xr[:, h, :].rearrange("p (q k) -> p k q", k=KC),
                                st[:, 6 + h:7 + h], None, ALU.mult).then_inc(xn_ready, 1)
            leave("norm1")

            dve.wait_ge(cact_ready, 1)
            with dve.Fori(0, 4) as i:
                enter("mod", i)
                for b in range(2):
                    dve.wait_ge(slot_in[f"w{2 * b + 1}"], landed(f"w{2 * b + 1}", "mod", i))
                    emptied(dve, f"A{b}", "mod", i)
                    weigh(acc512[:, b, :], W[:, 2 * b + 1, :].rearrange("p (k n) -> p k n", k=HC),
                          range(HC, KC), HC)
                leave("mod")
            enter("kv")
            dve.wait_ge(modT_in, 32)
            dve.wait_ge(small_in, 16 * 9)
            for name in ("L0", "L1", "T0", "T1"):
                emptied(dve, name, "idx" if name[0] == "L" else "main")
            emptied(dve, "O", "main")
            emptied(dve, "M", "main")
            emptied(dve, "A0", "kv")
            emptied(dve, "A1", "kv")
            link(v.tensor_tensor(modT[:, :, :], modT[:, :, :], colb[:, 0:2, :], ALU.add))
            link(v.tensor_scalar(modT[:, 1, :], modT[:, 1, :], 1.0, None, ALU.add))
            link(v.tensor_tensor(modT[:, 1, :], modT[:, 1, :], colb[:, 2, :], ALU.mult))
            for k in range(KC):
                v.tensor_scalar(hT[:, k, :], hT[:, k, :], modT[:, 1, k:k + 1], modT[:, 0, k:k + 1],
                                ALU.mult, ALU.add).then_inc(h_ready, 1)
            dve.wait_ge(const_ready, 12)
            for b in range(2):
                filled(dve, f"A{b}", "kv")
                if b == 1:
                    dve.sem_inc(slot_free["w4"], 1)
                for a in range(2):
                    src = bank[f"A{b}"][a * HEAD:(a + 1) * HEAD, 0:S]
                    v.tensor_copy(kd[0:HEAD, 2 * b + a, 0:S], src)
                    last = v.tensor_copy(kd[HEAD:P, 2 * b + a, S:2 * S], src)
                last.then_inc(kd_ready, 1)
                dve.wait_ge(kd_ready, b + 1)
                dve.sem_inc(free[f"A{b}"], 1)
            filled(dve, "A1", "kv", 0, 2)
            dve.sem_inc(slot_free["w0"], 1)
            v.tensor_scalar(iw[:, :, :], bank["A1"][:, 0:32].rearrange("p (h e) -> p h e", h=2),
                            HEAD ** -0.5 * IDX_HEADS ** -0.5, None, ALU.mult).then_inc(iw_ready, 1)
            dve.wait_ge(iw_ready, 1)
            dve.sem_inc(free["A1"], 1)
            leave("kv")

            with dve.Fori(0, 2) as i:
                enter("idx", i)
                for b in range(2):
                    for j in range(2):
                        for h in range(HALVES):
                            filled(dve, f"rel{h}", "idx", i, 2 * b + j)
                            dve.sem_inc(free[f"L{h}"], 1)
                            for a in range(2):
                                ins = v.scalar_tensor_tensor(
                                    out=score[:, h, :], in0=rel[:, h, a * S:(a + 1) * S],
                                    scalar=iw[:, h, bass.ds(i * 8 + 4 * b + 2 * j + a, 1)],
                                    in1=score[:, h, :], op0=ALU.mult, op1=ALU.add)
                                if a == 0:
                                    link(ins)
                                else:
                                    ins.then_inc(free[f"rel{h}"], 1)
                                    dve.wait_ge(free[f"rel{h}"], before(f"rel{h}", "idx", i, 2 * b + j) + 2)
                leave("idx")
            enter("topk")
            for h in range(HALVES):
                link(v.tensor_tensor(work[:, h, :], score[:, h, :], amask[:, h, :], ALU.add))
            for r in range(TOPK // 8):
                for h in range(HALVES):
                    cur = work if r == 0 else score
                    link(v.max(st[:, 8 + 8 * h:16 + 8 * h], cur[:, h, :]))
                    link(v.match_replace(score[:, h, :], st[:, 8 + 8 * h:16 + 8 * h], cur[:, h, :], NEG))
            for h in range(HALVES):
                link(v.tensor_tensor(work[:, h, :], work[:, h, :], score[:, h, :], ALU.is_equal))
                link(v.tensor_scalar(amask[:, h, :], work[:, h, :], NEG, None, ALU.mult))
            leave("topk")

            def modulation(n, b, phase, i):
                dve.wait_ge(slot_in[f"w{n}"], landed(f"w{n}", phase, i))
                weigh(acc[:, b, :], W[:, n, :].rearrange("p (k n) -> p k n", k=KC), range(KC), 0)

            def mod_row(r, phase, i, pos, at):
                filled(dve, "M", phase, i, pos)
                o = modrow[r:r + 1, bass.ds(at, UNIT)]
                v.tensor_tensor(o, bank["M"][r:r + 1, 0:UNIT], o, ALU.add).then_inc(free["M"], 1)

            dve.wait_ge(modrow_in, 64)
            with dve.Fori(0, KV) as i:
                enter("main", i)

                def masked(n):
                    h = n % 2
                    filled(dve, f"L{n % 2}", "main", i, n // 2)
                    emptied(dve, f"pb{n}", "main", i)
                    p3 = pb[:, n, :].rearrange("p (a s) -> p a s", a=2)
                    v.scalar_tensor_tensor(out=p3, in0=bank[f"L{n % 2}"].rearrange("p (a s) -> p a s", a=2),
                                           scalar=HEAD ** -0.5,
                                           in1=amask[:, h, :].unsqueeze(1).to_broadcast([P, 2, S]),
                                           op0=ALU.mult, op1=ALU.add).then_inc(free[f"L{n % 2}"], 1)
                    dve.wait_ge(free[f"L{n % 2}"], before(f"L{n % 2}", "main", i, n // 2) + 2)
                    link(v.tensor_reduce(st[:, 24 + 2 * n:26 + 2 * n], p3, AX, ALU.max))
                    v.tensor_scalar(st[:, 8 + 2 * n:10 + 2 * n], st[:, 24 + 2 * n:26 + 2 * n], -1.0, None,
                                    ALU.mult).then_inc(lg_ready, 1)

                def normalise(n):
                    dve.wait_ge(exp_ready, i * 8 + 2 * n + 2)
                    link(v.reciprocal(st[:, 24 + 2 * n:26 + 2 * n], st[:, 16 + 2 * n:18 + 2 * n]))
                    for a in range(2):
                        o = pb[:, n, a * S:(a + 1) * S]
                        last = v.tensor_scalar(o, o, st[:, 24 + 2 * n + a:25 + 2 * n + a], None, ALU.mult)
                    last.then_inc(full[f"pb{n}"], 1)

                def conv(j):
                    filled(dve, f"A{j}", "main", i, 2)
                    if j == 1:
                        dve.sem_inc(slot_free["w1"], 1)
                    filled(dve, f"cg{j}", "main", i)
                    v.tensor_tensor(uT[:, j, 2:], bank[f"A{j}"][:, 0:S], cgT[:, j, :], ALU.mult)\
                        .then_inc(free[f"A{j}"], 1)
                    dve.wait_ge(free[f"A{j}"], before(f"A{j}", "main", i, 2) + 2)
                    w = [convc[:, q, bass.ds(i * 2 + j, 1)] for q in range(TAPS)]
                    v.tensor_scalar(yb[:, j, :], uT[:, j, 2:2 + S], w[2], None, ALU.mult)\
                        .then_inc(free[f"cg{j}"], 1)
                    dve.wait_ge(free[f"cg{j}"], before(f"cg{j}", "main", i) + 2)
                    for q in (1, 0):
                        link(v.scalar_tensor_tensor(out=yb[:, j, :], in0=uT[:, j, q:q + S], scalar=w[q],
                                                    in1=yb[:, j, :], op0=ALU.mult, op1=ALU.add))

                modulation(4, 0, "main", i)
                masked(0)
                masked(1)
                conv(0)
                masked(2)
                masked(3)
                mod_row(0, "main", i, 0, i * 512)
                normalise(0)
                normalise(1)
                conv(1)
                normalise(2)
                normalise(3)
                modulation(5, 1, "main", i)
                for j in range(2):
                    filled(dve, f"A{j}", "main", i, 3)
                    if j == 1:
                        dve.sem_inc(slot_free["w2"], 1)
                    v.tensor_tensor(RB[:, bass.ds(i * 512 + 2048 + j * S, S)], bank[f"A{j}"][:, 0:S],
                                    yb[:, j, :], ALU.mult).then_inc(free[f"A{j}"], 1)
                mod_row(0, "main", i, 1, i * 512 + UNIT)
                leave("main")

            with dve.Fori(0, 8) as i:
                enter("gate", i)

                def merge(j):
                    for b in range(2):
                        filled(dve, f"L{b}", "gate", i, j)
                        filled(dve, f"sg{b}", "gate", i, j)
                        dve.sem_inc(free[f"A{b}"], 1)
                        if b == 1 and j == 1:
                            dve.sem_inc(slot_free["w2"], 1)
                        v.tensor_tensor(yb[:, b, :], bank[f"L{b}"][:, 0:S], qs[:, b, :], ALU.mult)\
                            .then_inc(free[f"L{b}"], 1)
                        dve.wait_ge(free[f"L{b}"], before(f"L{b}", "gate", i, j) + 2)
                        dve.sem_inc(free[f"sg{b}"], 1)
                    v.tensor_tensor(RM[:, bass.ds(i * 512 + j * S, S)], yb[:, 0, :], yb[:, 1, :], ALU.add)\
                        .then_inc(mT_ready, 1)
                    dve.wait_ge(mT_ready, i * 2 + j + 1)

                modulation(3, 0, "gate", i)
                merge(0)
                mod_row(32, "gate", i, 0, i * UNIT)
                modulation(4, 1, "gate", i)
                merge(1)
                modulation(5, 0, "gate", i)
                mod_row(64, "gate", i, 1, i * UNIT)
                mod_row(96, "gate", i, 2, i * UNIT)
                leave("gate")

            dve.wait_ge(fgain_in, 16)
            for q, name in enumerate(("L0", "L1", "T0", "T1")):
                filled(dve, name, "spread", 0, 3)
                o = A2B[:, q * 512:(q + 1) * 512]
                v.scalar_tensor_tensor(out=o, in0=bank[name], scalar=1.0, in1=o, op0=ALU.add, op1=ALU.mult)\
                    .then_inc(free[name], 1)

            for name in ("L0", "L1", "T0", "T1"):
                emptied(dve, name, "spread", 0, 1)
            with dve.Fori(0, 2) as i:
                enter("out", i)
                for b in range(4):
                    at = i * 1024 + b * UNIT
                    for h in range(HALVES):
                        filled(dve, f"A{h}", "out", i, b)
                        if h == 1:
                            dve.sem_inc(slot_free[f"w{b}"], 1)
                        v.tensor_tensor(acc[:, h, :], bank[f"A{h}"][:, 0:UNIT], g1B[:, bass.ds(at, UNIT)],
                                        ALU.mult).then_inc(free[f"A{h}"], 1)
                        dve.wait_ge(free[f"A{h}"], before(f"A{h}", "out", i, b) + 2)
                        o = xr[:, h, bass.ds(at, UNIT)]
                        v.tensor_tensor(o, o, acc[:, h, :], ALU.add).then_inc(x2_ready, 1)
                        dve.wait_ge(x2_ready, i * 8 + 2 * b + h + 1)
                leave("out")

            enter("norm2")
            dve.wait_ge(ssq_ready, 4)
            inverse_root(0, ms_ready, root_ready, 2)
            for name in ("L0", "L1", "T0", "T1"):
                emptied(dve, name, "norm2")
            for h in range(HALVES):
                perm = "p (q k) -> p k q"
                ins = v.scalar_tensor_tensor(out=h2[:, h, :, :], in0=xr[:, h, :].rearrange(perm, k=KC),
                                             scalar=st[:, 6 + h:7 + h], in1=A2B.rearrange(perm, k=KC),
                                             op0=ALU.mult, op1=ALU.mult)
                if h == 0:
                    link(ins)
                else:
                    ins.then_inc(choice_in, 1)
                    dve.wait_ge(choice_in, 1)
                v.tensor_tensor(h2[:, h, :, :], h2[:, h, :, :], B2B.rearrange(perm, k=KC), ALU.add)\
                    .then_inc(h2_ready, 1)
            leave("norm2")

            enter("route")
            dve.wait_ge(const_ready, 12)
            filled(dve, "A0", "route")
            lg, gx, zs = R("lg"), R("gexp"), R("zs")
            A3 = bank["A0"][:, 0:P].rearrange("p (h n) -> p h n", h=2)[:, :, 0:GROUPS + EXPERTS]
            link(v.tensor_tensor(lg, A3, gb[:, :].unsqueeze(1).to_broadcast([P, 2, GROUPS + EXPERTS]), ALU.add))
            gl, el = lg[:, :, 0:GROUPS], lg[:, :, GROUPS:]

            def wide(t, n):
                return t.to_broadcast([P, 2, n])

            def first_max(dst, src, n, m):
                link(v.tensor_reduce(m, src, AX, ALU.max))
                m3 = wide(m.rearrange("p (h o) -> p h o", o=1), n)
                link(v.tensor_tensor(dst, src, m3, ALU.is_equal))
                link(v.tensor_tensor(dst, dst, R("down")[:, EXPERTS - n:].unsqueeze(1).to_broadcast([P, 2, n]),
                                     ALU.mult))
                link(v.tensor_reduce(R("t2"), dst, AX, ALU.max))
                link(v.tensor_tensor(dst, wide(R("t2").rearrange("p (h o) -> p h o", o=1), n),
                                     R("down")[:, EXPERTS - n:].unsqueeze(1).to_broadcast([P, 2, n]), ALU.is_equal))

            link(v.tensor_scalar(R("down"), eidx[:, :], -1.0, float(EXPERTS), ALU.mult, ALU.add))
            gm = R("gm")
            first_max(R("gsel"), gl, GROUPS, gm)
            v.tensor_tensor(gx, gl, wide(gm.rearrange("p (h o) -> p h o", o=1), GROUPS), ALU.subtract)\
                .then_inc(gexp_in, 1)
            dve.wait_ge(gexp_ready, 1)
            link(v.tensor_reduce(zs, gx, AX, ALU.add))
            link(v.reciprocal(R("pgr"), zs))
            e4 = el.rearrange("p h (g e) -> p h g e", g=GROUPS)
            gs4 = R("gsel")
            val = R("val")
            for h in range(HALVES):
                v4 = val[:, h, :].rearrange("p (g e) -> p g e", g=GROUPS)
                s4 = gs4[:, h, :].unsqueeze(2).to_broadcast([P, GROUPS, EPG])
                link(v.tensor_tensor(v4, e4[:, h], s4, ALU.mult))
                link(v.tensor_scalar(R("t4"), gs4[:, h, :], -1.0, -NEG, ALU.add, ALU.mult))
                link(v.tensor_tensor(v4, v4, R("t4").unsqueeze(2).to_broadcast([P, GROUPS, EPG]), ALU.add))
            first_max(R("one"), val, EXPERTS, R("m1"))
            link(v.scalar_tensor_tensor(out=R("val2"), in0=R("one"), scalar=1.1 * NEG, in1=val,
                                        op0=ALU.mult, op1=ALU.add))
            first_max(R("two"), R("val2"), EXPERTS, R("m2"))
            v.tensor_tensor(R("pexp"), R("m2"), R("m1"), ALU.subtract).then_inc(pexp_in, 1)
            link(v.tensor_tensor(R("choice"), R("one"), R("two"), ALU.add))
            v.tensor_copy(R("t2"), R("m1")).then_inc(choice_ready, 1)
            dve.wait_ge(pexp_ready, 1)
            link(v.tensor_scalar(R("p1"), R("pexp"), 1.0, None, ALU.add))
            link(v.reciprocal(R("p1"), R("p1")))
            link(v.tensor_tensor(R("p1"), R("p1"), R("pgr"), ALU.mult))
            link(v.tensor_tensor(R("p2"), R("p1"), R("pexp"), ALU.mult))
            link(v.tensor_tensor(R("val"), R("one"), wide(R("p1").rearrange("p (h o) -> p h o", o=1), EXPERTS),
                                 ALU.mult))
            link(v.tensor_tensor(R("val2"), R("two"), wide(R("p2").rearrange("p (h o) -> p h o", o=1), EXPERTS),
                                 ALU.mult))
            link(v.tensor_tensor(cwc[:, :, 1:1 + EXPERTS], R("val"), R("val2"), ALU.add))
            filled(dve, "A1", "route")
            rk = cols[:, :, 1:1 + EXPERTS]
            link(v.scalar_tensor_tensor(out=rk, in0=bank["A1"][:, 0:64].rearrange("p (h e) -> p h e", h=2),
                                        scalar=1000.0, in1=R("choice"), op0=ALU.add, op1=ALU.mult))
            link(v.tensor_scalar(rk, rk, -1000.0, None, ALU.add))
            cnt = bank["A1"][:, 64:96]
            link(v.tensor_scalar(R("ov"), cnt, float(TILE), None, ALU.is_gt))
            for b in range(2, S // TILE):
                link(v.scalar_tensor_tensor(out=R("ov"), in0=cnt, scalar=float(b * TILE), in1=R("ov"),
                                            op0=ALU.is_gt, op1=ALU.add))
            link(v.tensor_tensor_scan(R("incl"), ones[:, 0:EXPERTS], R("ov"), 0.0, ALU.mult, ALU.add))
            link(v.tensor_tensor(R("excl"), R("incl"), R("ov"), ALU.subtract))
            o7 = eidx[:, 0:OVER].unsqueeze(2).to_broadcast([P, OVER, EXPERTS])
            in7 = R("incl").unsqueeze(1).to_broadcast([P, OVER, EXPERTS])
            ex7 = R("excl").unsqueeze(1).to_broadcast([P, OVER, EXPERTS])
            own, first, tmp7 = R("own"), R("first"), R("tmp7")
            link(v.tensor_tensor(own, in7, o7, ALU.is_gt))
            link(v.tensor_tensor(first, ex7, o7, ALU.is_le))
            link(v.tensor_tensor(own, own, first, ALU.mult))
            link(v.tensor_tensor(first, o7, ex7, ALU.subtract))
            link(v.tensor_scalar(first, first, 1.0, float(TILE), ALU.add, ALU.mult))
            for h in range(HALVES):
                rk7 = cols[:, h, 1:1 + EXPERTS].unsqueeze(1).to_broadcast([P, OVER, EXPERTS])
                cw7 = cwc[:, h, 1:1 + EXPERTS].unsqueeze(1).to_broadcast([P, OVER, EXPERTS])
                link(v.tensor_tensor(tmp7, rk7, first, ALU.subtract))
                link(v.tensor_tensor(tmp7, tmp7, own, ALU.mult))
                link(v.tensor_reduce(cols[:, h, 1 + EXPERTS:1 + EXPERTS + OVER], tmp7, AX, ALU.add))
                link(v.tensor_tensor(tmp7, cw7, own, ALU.mult))
                link(v.tensor_reduce(cwc[:, h, 1 + EXPERTS:1 + EXPERTS + OVER], tmp7, AX, ALU.add))
            link(v.tensor_tensor(tmp7, own, eidx[:, 0:EXPERTS].unsqueeze(1).to_broadcast([P, OVER, EXPERTS]),
                                 ALU.mult))
            link(v.tensor_reduce(R("eid"), tmp7, AX, ALU.add))
            link(v.tensor_copy(plan_i[0:1, 0:OVER], R("eid")[0:1, :]))
            v.tensor_copy(plan_i[0:1, 8:9], R("incl")[0:1, EXPERTS - 1:EXPERTS]).then_inc(plan_ready, 1)
            leave("route")

            def gather_mask(t):
                for h in range(HALVES):
                    last = v.tensor_scalar(pg[:, h, :], iota[:, :], cols[:, h, bass.ds(t + 1, 1)], None, ALU.is_equal)
                last.then_inc(pg_ready, 1)

            v.memset(RB[:, 0:512], 0.0)
            v.memset(pw, 0.0).then_inc(pw_ready, 1)
            v.memset(ysb, 0.0).then_inc(y_ready, 1)
            v.memset(actT, 0.0).then_inc(act_ready, 1)
            v.memset(gus, 0.0).then_inc(gus_ready, 1)
            v.memset(st[:, 32:33], 0.0).then_inc(add_done, 1)
            v.memset(st[:, 33:34], 0.0).then_inc(add_done, 1)
            gather_mask(0)

            def adds(t):
                dve.wait_ge(add_done, t * 8 + 2)
                for n in range(8):
                    dve.wait_ge(cmb_done, t * 8 + n + 1)
                    h, q = n // 4, n % 4
                    o = xr[:, h, q * 512:(q + 1) * 512]
                    v.tensor_tensor(o, o, bank["OM"[n % 2]], ALU.add).then_inc(add_done, 1)

            def tile(t):
                dve.wait_ge(gather_done, t + 1)
                gather_mask(t + 1)
                dve.wait_ge(ptr_done, t + 1)
                for h in range(HALVES):
                    last = v.tensor_scalar(pw[:, h, :].rearrange("p (a s) -> p a s", a=2),
                                           iota[:, :].unsqueeze(1).to_broadcast([P, 2, TILE]),
                                           cols[:, h, bass.ds(t + 1, 1)], cwc[:, h, bass.ds(t + 1, 1)],
                                           ALU.is_equal, ALU.mult)
                last.then_inc(pw_ready, 1)
                dve.wait_ge(sil_ready, t + 1)
                v.tensor_tensor(actT, sil, bank["A1"].rearrange("p (j s) -> p j s", j=FC)[:, :, TILE:], ALU.mult)\
                    .then_inc(act_ready, 1)
                adds(t)
                dve.wait_ge(slot_free["w5"], before("w5", "expert", t) + 2)
                v.tensor_tensor(ysb, pairT[:, :], g2s, ALU.mult).then_inc(y_ready, 1)

            with dve.Fori(0, EXPERTS) as e:
                tile(e)
            dve.wait_ge(plan_ready, 1)
            n_over = dve.value_load(plan_i[0:1, 8:9], min_val=0, max_val=OVER)
            with dve.Fori(0, OVER) as o:
                with dve.If(o < n_over):
                    tile(o + EXPERTS)
            adds(n_over + EXPERTS)

            dve.wait_ge(add_done, (n_over + EXPERTS) * 8 + 10)
            v.memset(st[:, 34:35], 0.0).then_inc(fin_chain, 1)
            dve.wait_ge(fin_ssq, 2)
            enter("last")
            inverse_root(0, fin_ms, fin_root, 1)
            leave("last")
            dve.wait_ge(gain_in, 16)
            for h in range(HALVES):
                v.scalar_tensor_tensor(out=xr[:, h, :], in0=xr[:, h, :], scalar=st[:, 6 + h:7 + h], in1=gfin,
                                       op0=ALU.mult, op1=ALU.mult).then_inc(fin_ready, 1)


NAMES = ["x", "c", "w_ada", "b_ada", "g_norm_mix", "w_in", "conv_w", "w_a_up", "w_b_out", "w_o", "g_norm_ffn",
         "w_rg", "b_rg", "w_re", "b_re", "w_e_gate", "w_e_up", "w_e_down", "g_norm_final"]


def kernel(**inputs):
    import numpy as np
    import concourse.bacc as bacc
    from concourse.bass_utils import run_bass_kernel_spmd

    nc = bacc.Bacc("TRN2", target_bir_lowering=False, num_devices=1)
    arrays, args = {}, []
    for name in NAMES:
        a = np.ascontiguousarray(inputs[name])
        arrays[f"in_{name}"] = a
        args.append(nc.dram_tensor(f"in_{name}", a.shape, mybir.dt.from_np(a.dtype), kind="ExternalInput").ap())
    args.append(nc.dram_tensor("out_x", (1, S, D), F32, kind="ExternalOutput").ap())
    block_kernel(nc, *args)
    r = run_bass_kernel_spmd(nc, [arrays], core_ids=[0])
    return r.results[0]["out_x"]
```

```python
from contextlib import ExitStack

import concourse.bass as bass
from concourse import mybir


P = 128
D = 2048
S = 256
HALVES = S // P
KC = D // P
N_MOD = 6
HEAD = 64
KV = 4
ATTN = 1024
CONV = 1024
TAPS = 3
IDX_HEADS = 16
TOPK = 64
GROUPS = 4
EPG = 8
EXPERTS = 32
FF = 512
FC = FF // P
TILE = 64
OVER = (2 * S - 1) // TILE
EPS = 1e-6
NEG = -3.0e38

COL_Q = 0
COL_K = COL_Q + ATTN
COL_V = COL_K + KV * HEAD
COL_IQ = COL_V + KV * HEAD
COL_IK = COL_IQ + IDX_HEADS * HEAD
COL_IW = COL_IK + HEAD
COL_BG = COL_IW + IDX_HEADS
COL_CG = COL_BG + CONV
COL_XC = COL_CG + CONV
COL_GA = COL_XC + CONV
COL_GB = COL_GA + D

SLOTS = 6
UNIT = 256
HC = KC // 2
QC = KC // 4

F32 = mybir.dt.float32
I32 = mybir.dt.int32
ALU = mybir.AluOpType
ACT = mybir.ActivationFunctionType
AX = mybir.AxisListType.X

PLAN = [
    ("mod", 2, dict(w0=1, w1=1, w2=1, w3=1, A0=1, A1=1, acc=2, v=14)),
    ("norm1", 1, dict(L0=1, L1=1, T0=1, T1=1, A0=1, A1=1, O=2, M=1, v=5)),
    ("mod2", 2, dict(w0=1, w1=1, w2=1, w3=1, A0=1, A1=1, acc=2, v=14)),
    ("kv", 1, dict(w4=1, w5=1, w0=1, A0=3, A1=3, M=1, v=2)),
    ("idx", 2, dict(w1=1, w2=1, A0=2, A1=2, L0=4, L1=4, qs0=2, qs1=2, rel0=4, rel1=4, v=8)),
    ("topk", 1, dict(v=38)),
    ("main", 4, dict(w3=1, w0=1, w1=1, w2=1, w4=1, w5=1, A0=4, A1=4, L0=2, L1=2, T0=2, T1=2, O=1, M=2,
                     qs0=1, qs1=1, cg0=1, cg1=1, pb0=1, pb1=1, pb2=1, pb3=1, pT0=2, pT1=2, vst=1, acc=2, v=42)),
    ("gate", 8, dict(w0=1, w1=1, w2=1, w3=1, w4=1, A0=2, A1=2, L0=2, L1=2, M=2, sg0=2, sg1=2, acc=2, v=30)),
    ("spread", 1, dict(L0=3, L1=3, T0=3, T1=3)),
    ("out", 4, dict(w0=1, w1=1, w4=1, w5=1, A0=2, A1=2, M=2, acc=2, v=30)),
    ("spread2", 1, dict(L0=1, L1=1, T0=1, T1=1)),
    ("norm2", 1, dict(L0=1, L1=1, T0=1, T1=1, A0=1, A1=1, O=1, M=1, v=7)),
    ("route", 1, dict(A0=1, A1=1, v=58)),
    ("expert", EXPERTS + OVER, dict(w0=1, w1=1, w2=1, w3=1, w4=1, w5=1)),
    ("last", 1, dict(v=5)),
]
DMAS = {("gate", "w2"): 3, ("expert", "w0"): 2, ("expert", "w1"): 2, ("expert", "w2"): 2, ("expert", "w3"): 2}
BUFFERS = ("qs0", "qs1", "rel0", "rel1", "cg0", "cg1", "pb0", "pb1", "pb2", "pb3", "pT0", "pT1", "vst", "sg0", "sg1")


def before(name, phase, i=0, pos=0):
    n = 0
    for other, runs, events in PLAN:
        if other == phase:
            return n + i * events.get(name, 0) + pos
        n += runs * events.get(name, 0)


def landed(slot, phase, i=0):
    n = 0
    for other, runs, events in PLAN:
        per = 16 * DMAS.get((other, slot), 1) * events.get(slot, 0)
        if other == phase:
            return n + i * per + per
        n += runs * per


def block_kernel(nc, x, c, w_ada, b_ada, g_norm_mix, w_in, conv_w, w_a_up, w_b_out, w_o, g_norm_ffn,
                 w_rg, b_rg, w_re, b_re, w_e_gate, w_e_up, w_e_down, g_norm_final, out):
    ada_v = w_ada[0].rearrange("(p k) n -> p k n", p=P)
    in_v = w_in[0].rearrange("(p k) n -> p k n", p=P)
    a_up_v = w_a_up[0].rearrange("(j p) n -> p j n", p=P)
    b_out_v = w_b_out[0].rearrange("(j p) n -> p j n", p=P)
    o_v = w_o[0].rearrange("(j p) n -> p j n", p=P)
    gate_v = w_e_gate[0].rearrange("e (p k) f -> e p k f", p=P)
    up_v = w_e_up[0].rearrange("e (p k) f -> e p k f", p=P)
    down_v = w_e_down[0].rearrange("e (p j) d -> e p j d", p=P)
    x_v = x[0].rearrange("(h p) d -> p h d", p=P)
    out_v = out[0].rearrange("(h p) d -> p h d", p=P)

    with ExitStack() as ctx:
        def sb(name, shape, dt=F32):
            return ctx.enter_context(nc.sbuf_tensor(name, shape, dt))

        def sem(name):
            return ctx.enter_context(nc.semaphore(name))

        W = sb("weight_slots", [P, SLOTS, 4096])
        xr = sb("x_resid", [P, HALVES, D])
        RA = sb("region_a", [P, 4096])
        RB = sb("region_b", [P, 4096])
        RM = sb("region_m", [P, 4096])
        RH = sb("region_h", [P, 4096])
        ikd = sb("ik_diag", [P, 2 * S])
        amask = sb("attn_mask", [P, HALVES, S])
        qs = sb("q_stage", [P, 2, S])
        pT = sb("probs_T", [P, 2, 512])
        modrow = sb("mod_rows", [P, D])
        acc = sb("ada_acc", [P, 2, UNIT])
        cgT = sb("cg_T", [P, 2, S])
        uT = sb("u_T", [P, 2, S + TAPS - 1])
        ident = sb("ident", [P, P])
        ones = sb("ones", [P, P])
        tri = sb("tri", [P, P])
        cT = sb("c_T", [P, 2, KC])
        modT = sb("mod_T", [P, 2, KC])
        colb = sb("col_b", [P, 3, KC])
        convc = sb("conv_c", [P, TAPS, 8])
        iw = sb("idx_w", [P, HALVES, IDX_HEADS])
        st = sb("stats", [P, 40])
        gb = sb("router_bias", [P, GROUPS + EXPERTS])
        iota = sb("iota", [P, TILE])
        eidx = sb("expert_index", [P, EXPERTS])
        cols = sb("rank_cols", [P, HALVES, 42])
        cwc = sb("weight_cols", [P, HALVES, 42])
        plan_i = sb("plan_i", [1, 16], I32)

        hT = RA[:, :].rearrange("p (k t) -> p k t", k=KC)
        xn = RB[:, :].rearrange("p (h k q) -> p h k q", h=HALVES, k=KC)
        oT = RB[:, 0:2048].rearrange("p (b t) -> p b t", b=8)
        zT = RB[:, 2048:4096].rearrange("p (b t) -> p b t", b=8)
        rows = RM[0:1, :]
        vtok = RM[:, 0:512].rearrange("p (h n) -> p h n", h=HALVES)
        vst = RM[:, 512:640].rearrange("p (h n) -> p h n", h=HALVES)
        mT = RM[:, :].rearrange("p (b t) -> p b t", b=16)
        kd = RH[:, 0:2048].rearrange("p (g n) -> p g n", g=KV)
        pb = RH[:, 2048:4096].rearrange("p (n m) -> p n m", n=4)
        rel = RH[:, 2048:3072].rearrange("p (h n) -> p h n", h=2)
        score = RH[:, 3072:3584].rearrange("p (h s) -> p h s", h=2)
        work = RH[:, 3584:4096].rearrange("p (h s) -> p h s", h=2)
        acc512 = RH[:, 0:1024].rearrange("p (b n) -> p b n", b=2)
        yb = ikd[:, :].rearrange("p (b t) -> p b t", b=2)
        g1B = RA[:, 0:2048]
        fgain = RH[:, 2048:4096]
        A2B, B2B = RB[:, 0:2048], RB[:, 2048:4096]
        h2 = RH[:, :].rearrange("p (h k q) -> p h k q", h=HALVES, k=KC)
        h2T = RM[:, :].rearrange("p (k t) -> p k t", k=KC)
        hsel = RM[:, 0:1024].rearrange("p (k s) -> p k s", k=KC)
        gus = RM[:, 1024:1536].rearrange("p (j q) -> p j q", j=FC)
        sil = RM[:, 1536:1792].rearrange("p (j s) -> p j s", j=FC)
        actT = RM[:, 1792:2048].rearrange("p (j s) -> p j s", j=FC)
        ysb = RM[:, 2048:3072]
        pg = RM[:, 3072:3200].rearrange("p (h s) -> p h s", h=2)
        pw = RM[:, 3200:3456].rearrange("p (h s) -> p h s", h=2)
        pt_lo, pt_hi = RB[:, 0:256], RB[:, 256:512]
        g2s = pT[:, :, :].rearrange("p a b -> p (a b)")
        cstage = qs[0:TAPS * 8, 0, 0:P]
        gfin = RB[:, 2048:4096]
        wr = sb("router_w", [P, KC, GROUPS + EXPERTS])
        sq = sb("square_sums", [P, HALVES, 8])

        scratch, at = {}, 512
        for name, shape in dict(lg=(2, 36), gsel=(2, 4), gexp=(2, 4), gm=(2,), zs=(2,), pgr=(2,), down=(32,),
                                val=(2, 32), val2=(2, 32), one=(2, 32), two=(2, 32), choice=(2, 32), m1=(2,),
                                m2=(2,), t2=(2,), t4=(4,), pexp=(2,), p1=(2,), p2=(2,), ov=(32,), incl=(32,),
                                excl=(32,), own=(OVER, 32), first=(OVER, 32), tmp7=(OVER, 32),
                                eid=(OVER,)).items():
            n = shape[0] * (shape[1] if len(shape) > 1 else 1)
            scratch[name] = RB[:, at:at + n] if len(shape) == 1 else \
                RB[:, at:at + n].rearrange("p (a b) -> p a b", a=shape[0])
            at += n
        assert at <= 2048

        def R(name):
            return scratch[name]

        bank = {n: ctx.enter_context(nc.psum_tensor(f"bank_{n}", [P, 512], F32)) for n in ("A0", "A1")}
        pairL = ctx.enter_context(nc.psum_tensor("bank_L", [P, 1024], F32))
        pairT = ctx.enter_context(nc.psum_tensor("bank_T", [P, 1024], F32))
        pairO = ctx.enter_context(nc.psum_tensor("bank_OM", [P, 1024], F32))
        bank.update(L0=pairL[:, 0:512], L1=pairL[:, 512:1024], T0=pairT[:, 0:512], T1=pairT[:, 512:1024],
                    O=pairO[:, 0:512], M=pairO[:, 512:1024], A0=bank["A0"][:, :], A1=bank["A1"][:, :])

        slot_in = {f"w{n}": sem(f"slot{n}_landed") for n in range(SLOTS)}
        slot_free = {f"w{n}": sem(f"slot{n}_free") for n in range(SLOTS)}
        full = {n: sem(f"{n}_full") for n in (*bank, *BUFFERS)}
        free = {n: sem(f"{n}_free") for n in (*bank, *BUFFERS)}
        chain = sem("vector_chain")
        acc_ready = sem("acc_ready")
        names = """c_in x_in small_in conv_in modrow_in const_ready pool_step cact_ready ssq_ready ms_ready root_ready
            xn_ready h_ready kd_ready v_ready ikd_ready iw_ready lg_ready exp_ready fgain_in mT_ready
            gain_in x2_ready h2_ready router_in logits_ready gexp_ready pexp_ready choice_in choice_ready
            gexp_in pexp_in plan_ready pg_ready pw_ready gather_done hsel_ready ptr_done pt_ready pv_done
            gus_ready gut_done sil_ready act_ready y_ready cmb_done add_done fin_ssq fin_ms fin_root
            fin_chain fin_ready stored""".split()
        (c_in, x_in, small_in, conv_in, modrow_in, const_ready, pool_step, cact_ready, ssq_ready, ms_ready, root_ready,
         xn_ready, h_ready, kd_ready, v_ready, ikd_ready, iw_ready, lg_ready, exp_ready, fgain_in, mT_ready,
         gain_in, x2_ready, h2_ready, router_in, logits_ready, gexp_ready, pexp_ready, choice_in, choice_ready,
         gexp_in, pexp_in, plan_ready, pg_ready, pw_ready, gather_done, hsel_ready, ptr_done, pt_ready, pv_done,
         gus_ready, gut_done, sil_ready, act_ready, y_ready, cmb_done, add_done, fin_ssq, fin_ms, fin_root,
         fin_chain, fin_ready, stored) = (sem(n) for n in names)

        def filled(eng, name, phase, i=0, pos=0):
            eng.wait_ge(full[name], before(name, phase, i, pos) + 1)

        def emptied(eng, name, phase, i=0, pos=0):
            eng.wait_ge(free[name], before(name, phase, i, pos) + 1)

        block = ctx.enter_context(nc.Block())

        @block.sync
        def _(sp):
            def claim(slot, phase, i=0):
                sp.wait_ge(slot_free[slot], before(slot, phase, i) + 1)

            def slot_view(n, k):
                return W[:, n, :].rearrange("p (k n) -> p k n", k=k)

            for n in range(SLOTS):
                sp.sem_inc(slot_free[f"w{n}"], 1)
            for phase, start in (("mod", 0), ("mod2", 2)):
              with sp.Fori(0, 2) as i:
                for n in range(4):
                    at = sp.snap(i * 1024 + start * 1024 + (n // 2) * 512)
                    claim(f"w{n}", phase, i)
                    sp.dma_start(slot_view(n, HC), ada_v[:, (n % 2) * HC:(n % 2 + 1) * HC, bass.ds(at, 512)])\
                        .then_inc(slot_in[f"w{n}"], 16)
            for slot, n, col in (("w4", 4, COL_K), ("w5", 5, COL_V)):
                claim(slot, "kv")
                sp.dma_start(slot_view(n, KC), in_v[:, :, col:col + UNIT]).then_inc(slot_in[slot], 16)
            claim("w0", "kv")
            sp.dma_start(slot_view(0, KC)[:, :, 0:HEAD + IDX_HEADS], in_v[:, :, COL_IK:COL_BG])\
                .then_inc(slot_in["w0"], 16)
            with sp.Fori(0, 2) as i:
                for b in range(2):
                    at = sp.snap(i * 512 + COL_IQ + b * UNIT)
                    claim(f"w{1 + b}", "idx", i)
                    sp.dma_start(slot_view(1 + b, KC), in_v[:, :, bass.ds(at, UNIT)])\
                        .then_inc(slot_in[f"w{1 + b}"], 16)
            with sp.Fori(0, KV) as i:
                for n, col in ((3, COL_Q), (0, COL_CG), (1, COL_XC), (2, COL_BG)):
                    at = sp.snap(i * UNIT + col)
                    claim(f"w{n}", "main", i)
                    sp.dma_start(slot_view(n, KC), in_v[:, :, bass.ds(at, UNIT)])\
                        .then_inc(slot_in[f"w{n}"], 16)
                for b in range(2):
                    at = sp.snap(i * 512 + 2 * D + b * UNIT)
                    claim(f"w{4 + b}", "main", i)
                    sp.dma_start(slot_view(4 + b, KC), ada_v[:, :, bass.ds(at, UNIT)])\
                        .then_inc(slot_in[f"w{4 + b}"], 16)
            with sp.Fori(0, 8) as i:
                for n, col in ((0, COL_GA), (1, COL_GB)):
                    at = sp.snap(i * UNIT + col)
                    claim(f"w{n}", "gate", i)
                    sp.dma_start(slot_view(n, KC), in_v[:, :, bass.ds(at, UNIT)])\
                        .then_inc(slot_in[f"w{n}"], 16)
                at = sp.snap(i * UNIT)
                claim("w2", "gate", i)
                for q in (4, 0):
                    sp.dma_start(slot_view(2, KC)[:, q:q + 4, :], a_up_v[:, q:q + 4, bass.ds(at, UNIT)])\
                        .then_inc(slot_in["w2"], 16)
                sp.dma_start(slot_view(2, KC)[:, 8:16, :], b_out_v[:, :, bass.ds(at, UNIT)])\
                    .then_inc(slot_in["w2"], 16)
                for n in range(2):
                    at = sp.snap(i * UNIT + (3 + n) * D)
                    claim(f"w{3 + n}", "gate", i)
                    sp.dma_start(slot_view(3 + n, KC), ada_v[:, :, bass.ds(at, UNIT)])\
                        .then_inc(slot_in[f"w{3 + n}"], 16)
            with sp.Fori(0, 4) as i:
                for b in range(2):
                    at = sp.snap(i * 512 + b * UNIT)
                    claim(f"w{b}", "out", i)
                    sp.dma_start(slot_view(b, KC), o_v[:, :, bass.ds(at, UNIT)])\
                        .then_inc(slot_in[f"w{b}"], 16)
                    at = sp.snap(i * 512 + 5 * D + b * UNIT)
                    claim(f"w{4 + b}", "out", i)
                    sp.dma_start(slot_view(4 + b, KC), ada_v[:, :, bass.ds(at, UNIT)])\
                        .then_inc(slot_in[f"w{4 + b}"], 16)

            def load_expert(e, t):
                for n in range(4):
                    claim(f"w{n}", "expert", t)
                    v = W[:, n, :].rearrange("p (g k f) -> p g k f", g=2, k=QC)
                    for g, src in ((0, gate_v), (1, up_v)):
                        sp.dma_start(v[:, g], src[e][:, n * QC:(n + 1) * QC, :]).then_inc(slot_in[f"w{n}"], 16)
                for n in range(2):
                    claim(f"w{4 + n}", "expert", t)
                    sp.dma_start(W[:, 4 + n, :].rearrange("p (j d) -> p j d", j=2),
                                 down_v[e][:, 2 * n:2 * n + 2, :]).then_inc(slot_in[f"w{4 + n}"], 16)

            with sp.Fori(0, EXPERTS) as e:
                load_expert(e, e)
            sp.wait_ge(plan_ready, 1)
            n_over = sp.value_load(plan_i[0:1, 8:9], min_val=0, max_val=OVER)
            with sp.Fori(0, OVER) as o:
                with sp.If(o < n_over):
                    e = sp.value_load(plan_i[0:1, bass.ds(o, 1)], min_val=0, max_val=EXPERTS - 1)
                    load_expert(e, o + EXPERTS)
            for h in range(HALVES):
                sp.wait_ge(fin_ready, h + 1)
                sp.dma_start(out_v[:, h, :], xr[:, h, :]).then_inc(stored, 16)
            sp.wait_ge(stored, 16 * HALVES)

        @block.gpsimd
        def _(pool):
            g = nc.gpsimd
            g.memset(ones[:, :], 1.0).then_inc(pool_step, 1)
            g.memset(ident[:, :], 0.0).then_inc(pool_step, 1)
            pool.wait_ge(pool_step, 2)
            g.affine_select(out=ident[:, :], in_=ident[:, :], compare_op=ALU.not_equal, fill=1.0, base=0,
                            pattern=[[-1, P]], channel_multiplier=1).then_inc(const_ready, 1)
            g.memset(modrow[:, :], 0.0).then_inc(const_ready, 1)
            g.affine_select(out=tri[:, :], in_=ones[:, :], compare_op=ALU.is_gt, fill=0.0, base=0,
                            pattern=[[1, P]], channel_multiplier=-1).then_inc(const_ready, 1)
            g.iota(iota[:, :], pattern=[[1, TILE]], base=0, channel_multiplier=0,
                   allow_small_or_imprecise_dtypes=True).then_inc(const_ready, 1)
            g.iota(eidx[:, :], pattern=[[1, EXPERTS]], base=0, channel_multiplier=0,
                   allow_small_or_imprecise_dtypes=True).then_inc(const_ready, 1)
            g.memset(amask[:, :, :], 0.0).then_inc(pool_step, 1)
            pool.wait_ge(pool_step, 3)
            g.affine_select(out=amask[:, :, :], in_=amask[:, :, :], compare_op=ALU.is_ge, fill=NEG, base=0,
                            pattern=[[P, HALVES], [-1, S]], channel_multiplier=1).then_inc(const_ready, 1)
            g.memset(ikd[:, :], 0.0).then_inc(const_ready, 1)
            g.memset(uT[:, :, 0:TAPS - 1], 0.0).then_inc(const_ready, 1)
            g.memset(cols[:, :, :], -1.0).then_inc(const_ready, 1)
            g.memset(cwc[:, :, :], 0.0).then_inc(const_ready, 1)
            g.memset(score, 0.0).then_inc(const_ready, 1)
            emptied(pool, "A0", "kv")
            emptied(pool, "A1", "kv")
            g.memset(RH[:, 0:2048], 0.0).then_inc(const_ready, 1)
            pool.wait_ge(v_ready, 2)
            with pool.Fori(0, KV) as i:
                emptied(pool, "vst", "main", i)
                g.tensor_copy(vst[:, :, :], vtok[:, :, bass.ds(i * HEAD, HEAD)]).then_inc(full["vst"], 1)
            filled(pool, "A0", "route")
            g.memset(RB[:, 0:512], 0.0)
            g.memset(pw, 0.0).then_inc(pw_ready, 1)
            g.memset(ysb, 0.0).then_inc(y_ready, 1)
            g.memset(actT, 0.0).then_inc(act_ready, 1)
            g.memset(gus, 0.0).then_inc(gus_ready, 1)

        @block.scalar
        def _(act):
            a = nc.scalar
            for name in free:
                act.sem_inc(free[name], 1)

            act.dma_start(cT[:, 0, :], c[0].rearrange("(p k) -> p k", p=P)).then_inc(c_in, 16)
            for h in range(HALVES):
                act.dma_start(xr[:, h, :], x_v[:, h, :]).then_inc(x_in, 16)
            act.dma_start(colb[:, 0, :], b_ada[0, 0:D].rearrange("(p k) -> p k", p=P)).then_inc(small_in, 16)
            act.dma_start(colb[:, 1, :], b_ada[0, D:2 * D].rearrange("(p k) -> p k", p=P)).then_inc(small_in, 16)
            act.dma_start(colb[:, 2, :], g_norm_mix[0].rearrange("(p k) -> p k", p=P)).then_inc(small_in, 16)
            act.dma_start(cstage, conv_w[0].rearrange("j (b p) -> (j b) p", p=P)).then_inc(conv_in, 16)
            act.wait_ge(c_in, 16)
            a.activation(cT[:, 1, :], cT[:, 0, :], ACT.Silu).then_inc(cact_ready, 1)
            act.wait_ge(x_in, 16 * HALVES)
            for h in range(HALVES):
                a.activation(RB[:, h * D:(h + 1) * D], xr[:, h, :], ACT.Square,
                             accum_out=st[:, h:h + 1]).then_inc(ssq_ready, 1)
            act.dma_start(wr[:, :, 0:GROUPS], w_rg[0].rearrange("(p k) e -> p k e", p=P)).then_inc(router_in, 16)
            act.dma_start(wr[:, :, GROUPS:], w_re[0].rearrange("(p k) e -> p k e", p=P)).then_inc(router_in, 16)
            act.dma_start(gb[:, 0:GROUPS], b_rg[0:1, :].to_broadcast([P, GROUPS])).then_inc(router_in, 16)
            act.dma_start(gb[:, GROUPS:], b_re[0:1, :].to_broadcast([P, EXPERTS])).then_inc(router_in, 16)
            act.wait_ge(const_ready, 2)
            for v in range(4):
                act.dma_start(modrow[32 * v:32 * v + 1, :], b_ada[0:1, (2 + v) * D:(3 + v) * D])\
                    .then_inc(modrow_in, 16)

            def mod_rows(phase, start):
                with act.Fori(0, 2) as i:
                    for b in range(2):
                        filled(act, f"A{b}", phase, i)
                        a.activation(rows[:, bass.ds(i * 1024 + start * 1024 + b * 512, 512)],
                                     bank[f"A{b}"][0:1, :], ACT.Copy).then_inc(free[f"A{b}"], 1)

            mod_rows("mod", 0)
            act.wait_ge(ms_ready, 1)
            a.activation(st[:, 4:6], st[:, 2:4], ACT.Sqrt).then_inc(root_ready, 1)
            for n, name in enumerate(("L0", "L1", "T0", "T1", "A0", "A1", "O", "M")):
                h, k = n // 4, (n % 4) * 4
                filled(act, name, "norm1")
                a.activation(hT[:, k:k + 4, h * P:(h + 1) * P],
                             bank[name].rearrange("p (k t) -> p k t", k=4), ACT.Copy).then_inc(free[name], 1)
            filled(act, "O", "norm1", 0, 1)
            a.activation(convc[:, :, :], bank["O"][:, 0:TAPS * 8].rearrange("p (j b) -> p j b", j=TAPS),
                         ACT.Copy).then_inc(free["O"], 1)
            mod_rows("mod2", 2)
            for h in range(HALVES):
                filled(act, f"A{h}", "kv", 0, 1)
                if h == 1:
                    act.sem_inc(slot_free["w5"], 1)
                a.activation(vtok[:, h, :], bank[f"A{h}"][:, 0:UNIT], ACT.Copy).then_inc(v_ready, 1)
                act.wait_ge(v_ready, h + 1)
                act.sem_inc(free[f"A{h}"], 1)
            filled(act, "A0", "kv", 0, 2)
            act.wait_ge(const_ready, 11)
            a.activation(ikd[0:HEAD, 0:S], bank["A0"][0:HEAD, 0:S], ACT.Copy).then_inc(ikd_ready, 1)
            a.activation(ikd[HEAD:P, S:2 * S], bank["A0"][0:HEAD, 0:S], ACT.Copy).then_inc(ikd_ready, 1)
            act.wait_ge(ikd_ready, 2)
            act.sem_inc(free["A0"], 1)

            with act.Fori(0, 2) as i:
                for b in range(2):
                    for j in range(2):
                        filled(act, f"A{j}", "idx", i, b)
                        if j == 1:
                            act.sem_inc(slot_free[f"w{1 + b}"], 1)
                        a.activation(qs[:, j, :], bank[f"A{j}"][:, 0:S], ACT.Copy).then_inc(full[f"qs{j}"], 1)
                    for j in range(2):
                        for h in range(HALVES):
                            filled(act, f"L{h}", "idx", i, 2 * b + j)
                            emptied(act, f"rel{h}", "idx", i, 2 * b + j)
                            a.activation(rel[:, h, :], bank[f"L{h}"], ACT.Relu).then_inc(full[f"rel{h}"], 1)

            with act.Fori(0, KV) as i:
                def cg(j):
                    filled(act, f"A{j}", "main", i, 1)
                    emptied(act, f"cg{j}", "main", i)
                    if j == 1:
                        act.sem_inc(slot_free["w0"], 1)
                    a.activation(cgT[:, j, :], bank[f"A{j}"][:, 0:S], ACT.Copy).then_inc(full[f"cg{j}"], 1)
                    filled(act, f"cg{j}", "main", i)
                    act.sem_inc(free[f"A{j}"], 1)

                def expo(n):
                    act.wait_ge(lg_ready, i * 4 + n + 1)
                    for h in range(2):
                        a.activation(pb[:, n, h * S:(h + 1) * S], pb[:, n, h * S:(h + 1) * S], ACT.Exp,
                                     bias=st[:, 8 + 2 * n + h:9 + 2 * n + h],
                                     accum_out=st[:, 16 + 2 * n + h:17 + 2 * n + h]).then_inc(exp_ready, 1)

                for j in range(2):
                    filled(act, f"A{j}", "main", i, 0)
                    if j == 1:
                        act.sem_inc(slot_free["w3"], 1)
                    a.activation(qs[:, j, :], bank[f"A{j}"][:, 0:S], ACT.Copy).then_inc(full[f"qs{j}"], 1)
                cg(0)
                expo(0)
                expo(1)
                cg(1)
                expo(2)
                expo(3)
                for n in range(4):
                    filled(act, f"T{n % 2}", "main", i, n // 2)
                    if n >= 2:
                        act.wait_ge(pv_done, i * 2 + n - 1)
                    a.activation(pT[:, n % 2, :], bank[f"T{n % 2}"], ACT.Copy).then_inc(full[f"pT{n % 2}"], 1)
                filled(act, "O", "main", i)
                act.sem_inc(free["vst"], 1)
                a.activation(RB[:, bass.ds(i * 512, 512)], bank["O"], ACT.Copy).then_inc(free["O"], 1)

            for n in range(4):
                emptied(act, f"pb{n}", "gate")
            act.dma_start(fgain, g_norm_ffn[0:1, :].to_broadcast([P, D])).then_inc(fgain_in, 16)
            with act.Fori(0, 8) as i:
                for j in range(2):
                    for b in range(2):
                        filled(act, f"A{b}", "gate", i, j)
                        if j == 1:
                            act.sem_inc(slot_free[f"w{b}"], 1)
                        emptied(act, f"sg{b}", "gate", i, j)
                        a.activation(qs[:, b, :], bank[f"A{b}"][:, 0:S], ACT.Sigmoid).then_inc(full[f"sg{b}"], 1)
            for turn, dst in enumerate((g1B, B2B)):
                for q, name in enumerate(("L0", "L1", "T0", "T1")):
                    filled(act, name, "spread", 0, turn)
                    a.activation(dst[:, q * 512:(q + 1) * 512], bank[name], ACT.Copy).then_inc(free[name], 1)
            with act.Fori(0, 4) as i:
                act.wait_ge(ssq_ready, i * 4 + 2)
                for b in range(2):
                    for h in range(HALVES):
                        act.wait_ge(x2_ready, i * 4 + 2 * b + h + 1)
                        a.activation(RH[:, (2 * b + h) * UNIT:(2 * b + h + 1) * UNIT],
                                     xr[:, h, bass.ds(i * 512 + b * UNIT, UNIT)], ACT.Square,
                                     accum_out=sq[:, h, bass.ds(i * 2 + b, 1)]).then_inc(ssq_ready, 1)
            act.wait_ge(ms_ready, 2)
            a.activation(st[:, 4:6], st[:, 2:4], ACT.Sqrt).then_inc(root_ready, 1)
            for q, name in enumerate(("L0", "L1", "T0", "T1")):
                filled(act, name, "spread2")
                r = slice(64 * (q // 2), 64 * (q // 2) + 64)
                a.activation(g2s[r, (q % 2) * 512:(q % 2 + 1) * 512], bank[name][r, :], ACT.Copy)\
                    .then_inc(free[name], 1)
            for n, name in enumerate(("L0", "L1", "T0", "T1", "A0", "A1", "O", "M")):
                h, k = n // 4, (n % 4) * 4
                filled(act, name, "norm2")
                a.activation(h2T[:, k:k + 4, h * P:(h + 1) * P],
                             bank[name].rearrange("p (k t) -> p k t", k=4), ACT.Copy).then_inc(free[name], 1)
            act.wait_ge(h2_ready, 2)
            act.dma_start(gfin, g_norm_final.rearrange("(o d) -> o d", o=1).to_broadcast([P, D])).then_inc(gain_in, 16)
            act.wait_ge(gexp_in, 1)
            a.activation(R("gexp"), R("gexp"), ACT.Exp).then_inc(gexp_ready, 1)
            act.wait_ge(pexp_in, 1)
            a.activation(R("pexp"), R("pexp"), ACT.Exp).then_inc(pexp_ready, 1)

            def mask_evac(t):
                act.wait_ge(ptr_done, t + 1)
                a.activation(pt_lo[0:TILE, :], bank["A1"][0:TILE, 0:S], ACT.Copy)
                a.activation(pt_hi[TILE:P, :], bank["A1"][TILE:P, 0:S], ACT.Copy).then_inc(pt_ready, 1)

            def gather_evac(t):
                act.wait_ge(gather_done, t + 1)
                a.activation(RM[:, 0:1024], pairL[:, :], ACT.Copy).then_inc(hsel_ready, 1)

            def tile(t):
                mask_evac(t)
                act.wait_ge(slot_free["w3"], before("w3", "expert", t) + 2)
                a.activation(gus, bank["A0"].rearrange("p (q j) -> p j q", j=FC), ACT.Copy).then_inc(gus_ready, 1)
                gather_evac(t + 1)
                act.wait_ge(gut_done, t + 1)
                a.activation(sil, bank["A1"].rearrange("p (j s) -> p j s", j=FC)[:, :, 0:TILE], ACT.Silu)\
                    .then_inc(sil_ready, 1)

            gather_evac(0)
            with act.Fori(0, EXPERTS) as e:
                tile(e)
            act.wait_ge(plan_ready, 1)
            n_over = act.value_load(plan_i[0:1, 8:9], min_val=0, max_val=OVER)
            with act.Fori(0, OVER) as o:
                with act.If(o < n_over):
                    tile(o + EXPERTS)
            mask_evac(n_over + EXPERTS)
            act.wait_ge(fin_chain, 1)
            for h in range(HALVES):
                a.activation(RH[:, h * D:(h + 1) * D], xr[:, h, :], ACT.Square,
                             accum_out=st[:, h:h + 1]).then_inc(fin_ssq, 1)
            act.wait_ge(fin_ms, 1)
            a.activation(st[:, 4:6], st[:, 2:4], ACT.Sqrt).then_inc(fin_root, 1)

        @block.tensor
        def _(pe):
            mm = nc.tensor.matmul
            A0, A1 = bank["A0"], bank["A1"]

            def slot(n, phase, i=0):
                pe.wait_ge(slot_in[f"w{n}"], landed(f"w{n}", phase, i))

            def unit(n):
                return W[:, n, :].rearrange("p (k n) -> p k n", k=KC)

            def project(name, phase, i, pos, n, j, first=False):
                emptied(pe, name, phase, i, pos)
                w = unit(n)
                for k in range(KC):
                    if first:
                        pe.wait_ge(h_ready, k + 1)
                    last = mm(bank[name][:, 0:S], w[:, k, j * P:(j + 1) * P], hT[:, k, :],
                              start=(k == 0), stop=(k == KC - 1))
                return last

            def transposes(src, phase, ready=None):
                for n, name in enumerate(("L0", "L1", "T0", "T1", "A0", "A1", "O", "M")):
                    h, k = n // 4, (n % 4) * 4
                    if ready is not None and k == 0:
                        pe.wait_ge(ready, h + 1)
                    emptied(pe, name, phase)
                    for q in range(4):
                        last = nc.tensor.transpose(bank[name][:, q * P:(q + 1) * P], src[:, h, k + q, :], ident[:, :])
                    last.then_inc(full[name], 1)

            def mod_sums(phase):
                with pe.Fori(0, 2) as i:
                    for b in range(2):
                        name = f"A{b}"
                        emptied(pe, name, phase, i)
                        slot(2 * b, phase, i)
                        w = W[:, 2 * b, :].rearrange("p (k n) -> p k n", k=HC)
                        for k in range(HC):
                            last = mm(bank[name][0:1, :], cT[:, 1, k:k + 1], w[:, k, :], start=(k == 0), stop=False,
                                      skip_group_check=True)
                        last.then_inc(slot_free[f"w{2 * b}"], 1)
                        pe.wait_ge(acc_ready, before("acc", phase, i, b) + 1)
                        mm(bank[name][0:1, 0:256], ones[:, 0:1], acc512[:, b, 0:256], start=False, stop=False,
                           skip_group_check=True).then_inc(slot_free[f"w{2 * b + 1}"], 1)
                        mm(bank[name][0:1, 256:512], ones[:, 0:1], acc512[:, b, 256:512], start=False, stop=True,
                           skip_group_check=True).then_inc(full[name], 1)

            pe.wait_ge(cact_ready, 1)
            pe.wait_ge(const_ready, 1)
            mod_sums("mod")
            pe.wait_ge(xn_ready, 2)
            transposes(xn, "norm1")
            pe.wait_ge(conv_in, 16)
            emptied(pe, "O", "norm1", 0, 1)
            nc.tensor.transpose(bank["O"][:, 0:TAPS * 8], cstage, ident[0:TAPS * 8, 0:TAPS * 8])\
                .then_inc(full["O"], 1)
            mod_sums("mod2")

            emptied(pe, "A0", "kv")
            emptied(pe, "A1", "kv")
            emptied(pe, "M", "kv")
            for n in range(2 * KC):
                at = (n // KC) * D + n % KC
                last = mm(bank["M"][:, n:n + 1], RM[0:1, at:at + D - KC + 1:KC], ones[0:1, 0:1],
                          start=True, stop=True)
            last.then_inc(full["M"], 1)

            slot(4, "kv")
            for j in range(2):
                last = project(f"A{j}", "kv", 0, 0, 4, j, first=(j == 0))
                last.then_inc(full[f"A{j}"], 1)
            slot(5, "kv")
            for h in range(HALVES):
                emptied(pe, f"A{h}", "kv", 0, 1)
                for k in range(KC):
                    last = mm(bank[f"A{h}"][:, 0:UNIT], hT[:, k, h * P:(h + 1) * P], unit(5)[:, k, :],
                              start=(k == 0), stop=(k == KC - 1))
                last.then_inc(full[f"A{h}"], 1)
            slot(0, "kv")
            emptied(pe, "A0", "kv", 0, 2)
            for k in range(KC):
                last = mm(A0[0:HEAD, 0:S], unit(0)[:, k, 0:HEAD], hT[:, k, :], start=(k == 0), stop=(k == KC - 1))
            last.then_inc(full["A0"], 1)
            emptied(pe, "A1", "kv", 0, 2)
            for h in range(HALVES):
                for k in range(KC):
                    last = mm(A1[:, h * 16:h * 16 + 16], hT[:, k, h * P:(h + 1) * P],
                              unit(0)[:, k, HEAD:HEAD + IDX_HEADS], start=(k == 0), stop=(k == KC - 1))
            last.then_inc(full["A1"], 1)

            pe.wait_ge(ikd_ready, 2)
            with pe.Fori(0, 2) as i:
                for b in range(2):
                    slot(1 + b, "idx", i)
                    for j in range(2):
                        project(f"A{j}", "idx", i, b, 1 + b, j).then_inc(full[f"A{j}"], 1)
                    for j in range(2):
                        filled(pe, f"qs{j}", "idx", i, b)
                        pe.sem_inc(free[f"A{j}"], 1)
                        for h in range(HALVES):
                            emptied(pe, f"L{h}", "idx", i, 2 * b + j)
                            last = mm(bank[f"L{h}"], qs[:, j, h * P:(h + 1) * P], ikd[:, :], start=True, stop=True)
                            last.then_inc(full[f"L{h}"], 1)

            pe.wait_ge(kd_ready, 2)
            with pe.Fori(0, KV) as i:
                def logits(n):
                    j, h = n // 2, n % 2
                    emptied(pe, f"L{n % 2}", "main", i, n // 2)
                    mm(bank[f"L{n % 2}"], qs[:, j, h * P:(h + 1) * P], RH[:, bass.ds(i * 512, 512)],
                       start=True, stop=True).then_inc(full[f"L{n % 2}"], 1)

                def turn(n):
                    filled(pe, f"pb{n}", "main", i)
                    emptied(pe, f"T{n % 2}", "main", i, n // 2)
                    for q in range(4):
                        last = nc.tensor.transpose(bank[f"T{n % 2}"][:, q * P:(q + 1) * P],
                                                   pb[:, n, q * P:(q + 1) * P], ident[:, :])
                    last.then_inc(full[f"T{n % 2}"], 1)

                def values(n):
                    j, h = n // 2, n % 2
                    filled(pe, f"pT{n % 2}", "main", i, n // 2)
                    pe.sem_inc(free[f"T{n % 2}"], 1)
                    for s in range(HALVES):
                        for a in range(2):
                            last = mm(bank["O"][a * HEAD:(a + 1) * HEAD, j * S + h * P:j * S + (h + 1) * P],
                                      vst[:, s, :], pT[:, n % 2, (2 * a + s) * P:(2 * a + s + 1) * P],
                                      start=(s == 0), stop=(s == HALVES - 1), skip_group_check=True)
                            if a == 1 and s == 0:
                                last.then_inc(free[f"pb{n}"], 1)
                    if n == 3:
                        last.then_inc(full["O"], 1)
                    elif n < 2:
                        last.then_inc(pv_done, 1)

                def spread_sum(b, n):
                    pe.wait_ge(acc_ready, before("acc", "main", i, b) + 1)
                    emptied(pe, "M", "main", i, b)
                    mm(bank["M"][:, 0:P], ones[:, :], acc[:, b, 0:P], start=True, stop=True)\
                        .then_inc(slot_free[f"w{n}"], 1)
                    mm(bank["M"][:, P:UNIT], ones[:, :], acc[:, b, P:UNIT], start=True, stop=True)\
                        .then_inc(full["M"], 1)

                def staged(j):
                    filled(pe, f"qs{j}", "main", i)
                    pe.sem_inc(free[f"A{j}"], 1)

                def block_of(n, pos, j):
                    if j == 0:
                        slot(n, "main", i)
                    project(f"A{j}", "main", i, pos, n, j).then_inc(full[f"A{j}"], 1)

                block_of(3, 0, 0)
                block_of(3, 0, 1)
                staged(0)
                block_of(0, 1, 0)
                staged(1)
                logits(0)
                logits(1)
                block_of(0, 1, 1)
                block_of(1, 2, 0)
                logits(2)
                logits(3)
                spread_sum(0, 4)
                block_of(1, 2, 1)
                block_of(2, 3, 0)
                turn(0)
                turn(1)
                block_of(2, 3, 1)
                filled(pe, "vst", "main", i)
                emptied(pe, "O", "main", i)
                values(0)
                values(1)
                turn(2)
                turn(3)
                spread_sum(1, 5)
                values(2)
                values(3)

            emptied(pe, "O", "gate")
            with pe.Fori(0, 8) as i:
                def branch(name, j, half, src):
                    emptied(pe, name, "gate", i, j)
                    w = unit(2)
                    for q in range(8):
                        last = mm(bank[name][:, 0:S], w[:, 8 * half + q, j * P:(j + 1) * P], src[:, q, :],
                                  start=(q == 0), stop=(q == 7))
                    return last

                def spread_sum(n):
                    pe.wait_ge(acc_ready, before("acc", "gate", i, n) + 1)
                    emptied(pe, "M", "gate", i, n)
                    mm(bank["M"][:, 0:P], ones[:, :], acc[:, n % 2, 0:P], start=True, stop=True)\
                        .then_inc(slot_free[f"w{3 + n}"], 1)
                    mm(bank["M"][:, P:UNIT], ones[:, :], acc[:, n % 2, P:UNIT], start=True, stop=True)\
                        .then_inc(full["M"], 1)

                for j in range(2):
                    for b in range(2):
                        if j == 0:
                            slot(b, "gate", i)
                        project(f"A{b}", "gate", i, j, b, j).then_inc(full[f"A{b}"], 1)
                    if j == 0:
                        slot(2, "gate", i)
                    branch("L0", j, 0, oT).then_inc(full["L0"], 1)
                    branch("L1", j, 1, zT).then_inc(full["L1"], 1)
                    spread_sum(j)

            def spread_rows(v, phase, turn):
                for q, name in enumerate(("L0", "L1", "T0", "T1")):
                    emptied(pe, name, phase, 0, turn)
                    mm(bank[name], ident[:, 32 * v:32 * v + 1].to_broadcast([P, P]),
                       modrow[:, q * 512:(q + 1) * 512], start=True, stop=True).then_inc(full[name], 1)

            emptied(pe, "M", "out")
            for turn, v in enumerate((0, 1, 2)):
                spread_rows(v, "spread", turn)

            pe.wait_ge(mT_ready, 16)
            with pe.Fori(0, 4) as i:
                for b in range(2):
                    slot(b, "out", i)
                    for h in range(HALVES):
                        emptied(pe, f"A{h}", "out", i, b)
                        for q in range(KC):
                            last = mm(bank[f"A{h}"][:, 0:UNIT], mT[:, q, h * P:(h + 1) * P], unit(b)[:, q, :],
                                      start=(q == 0), stop=(q == KC - 1))
                        last.then_inc(full[f"A{h}"], 1)
                    pe.wait_ge(acc_ready, before("acc", "out", i, b) + 1)
                    emptied(pe, "M", "out", i, b)
                    mm(bank["M"][:, 0:P], ones[:, :], acc[:, b, 0:P], start=True, stop=True)\
                        .then_inc(slot_free[f"w{4 + b}"], 1)
                    mm(bank["M"][:, P:UNIT], ones[:, :], acc[:, b, P:UNIT], start=True, stop=True)\
                        .then_inc(full["M"], 1)
            emptied(pe, "M", "norm2")
            spread_rows(3, "spread2", 0)

            transposes(h2, "norm2", h2_ready)
            emptied(pe, "A0", "route")
            for name in ("L0", "L1", "T0", "T1"):
                emptied(pe, name, "route")
            for name in ("A1", "O", "M"):
                emptied(pe, name, "route")
            pe.wait_ge(router_in, 16 * 4)
            for h in range(HALVES):
                for k in range(KC):
                    last = mm(A0[:, 64 * h:64 * h + GROUPS + EXPERTS], h2T[:, k, h * P:(h + 1) * P], wr[:, k, :],
                              start=(k == 0), stop=(k == KC - 1))
            last.then_inc(full["A0"], 1)
            pe.wait_ge(choice_ready, 1)
            m0, m1 = R("choice")[:, 0, :], R("choice")[:, 1, :]
            mm(A1[:, 0:32], tri[:, :], m0, start=True, stop=True)
            mm(A1[:, 32:64], tri[:, :], m1, start=True, stop=False)
            mm(A1[:, 32:64], ones[:, :], m0, start=False, stop=True)
            mm(A1[:, 64:96], ones[:, :], m0, start=True, stop=False)
            mm(A1[:, 64:96], ones[:, :], m1, start=False, stop=True).then_inc(full["A1"], 1)

            def gather(t):
                pe.wait_ge(pg_ready, t + 1)
                for k in range(KC):
                    for h in range(HALVES):
                        last = mm(pairL[:, k * TILE:(k + 1) * TILE], h2[:, h, k, :], pg[:, h, :],
                                  start=(h == 0), stop=(h == HALVES - 1))
                last.then_inc(gather_done, 1)

            def combine_mask(t):
                pe.wait_ge(pw_ready, t + 1)
                pe.wait_ge(act_ready, t + 1)
                for h in range(HALVES):
                    last = nc.tensor.transpose(A1[:, h * P:(h + 1) * P], pw[:, h, :], ident[:, :])
                last.then_inc(ptr_done, 1)

            def combine(t):
                pe.wait_ge(pt_ready, t + 1)
                pe.wait_ge(y_ready, t + 1)
                for n in range(8):
                    h, q = n // 4, n % 4
                    pe.wait_ge(add_done, t * 8 + n + 1)
                    mm(bank["OM"[n % 2]], (pt_lo if q < 2 else pt_hi)[:, h * P:(h + 1) * P],
                       ysb[:, (q % 2) * 512:(q % 2 + 1) * 512], start=True, stop=True).then_inc(cmb_done, 1)

            def tile(t):
                combine_mask(t)
                pe.wait_ge(hsel_ready, t + 1)
                pe.wait_ge(gus_ready, t + 1)
                for n in range(4):
                    slot(n, "expert", t)
                    w = W[:, n, :].rearrange("p (g k f) -> p g k f", g=2, k=QC)
                    for k in range(QC):
                        ks = n * QC + k
                        for g in range(2):
                            last = mm(A0[g * TILE:(g + 1) * TILE, :], hsel[:, ks, :], w[:, g, k, :],
                                      start=(ks == 0), stop=(ks == KC - 1), skip_group_check=True)
                    last.then_inc(slot_free[f"w{n}"], 1)
                gather(t + 1)
                pe.wait_ge(gus_ready, t + 2)
                pe.wait_ge(pt_ready, t + 1)
                for j in range(FC):
                    last = nc.tensor.transpose(A1[:, j * P:(j + 1) * P], gus[:, j, :], ident[:, :])
                last.then_inc(gut_done, 1)
                combine(t)
                pe.wait_ge(act_ready, t + 2)
                for n in range(2):
                    slot(4 + n, "expert", t)
                    w = W[:, 4 + n, :].rearrange("p (j g d) -> p j g d", j=2, g=2)
                    for j in range(2):
                        js = 2 * n + j
                        for q in range(2):
                            for g in range(2):
                                last = mm(pairT[g * TILE:(g + 1) * TILE, q * 512:(q + 1) * 512], actT[:, js, :],
                                          w[:, j, g, q * 512:(q + 1) * 512], start=(js == 0), stop=(js == FC - 1),
                                          skip_group_check=True)
                    last.then_inc(slot_free[f"w{4 + n}"], 1)

            pe.wait_ge(pg_ready, 1)
            gather(0)
            emptied(pe, "A1", "expert")
            with pe.Fori(0, EXPERTS) as e:
                tile(e)
            pe.wait_ge(plan_ready, 1)
            n_over = pe.value_load(plan_i[0:1, 8:9], min_val=0, max_val=OVER)
            with pe.Fori(0, OVER) as o:
                with pe.If(o < n_over):
                    tile(o + EXPERTS)
            combine_mask(n_over + EXPERTS)
            combine(n_over + EXPERTS)

        @block.vector
        def _(dve):
            v = nc.vector
            place = [None, 0]

            def enter(phase, i=0):
                place[:] = [before("v", phase, i), 0]

            def leave(phase):
                want = {n: e.get("v", 0) for n, _, e in PLAN}[phase]
                assert place[1] == want, (phase, place[1], want)

            def link(ins):
                place[1] += 1
                ins.then_inc(chain, 1)
                dve.wait_ge(chain, place[0] + place[1])

            def inverse_root(col, ms_sem, root_sem, turn):
                v.tensor_scalar(st[:, 2:4], st[:, 0:2], 1.0 / D, EPS, ALU.mult, ALU.add).then_inc(ms_sem, 1)
                dve.wait_ge(root_sem, turn)
                link(v.reciprocal(st[:, 6:8], st[:, 4:6]))
                link(v.tensor_tensor(st[:, 4:6], st[:, 6:8], st[:, 6:8], ALU.mult))
                link(v.tensor_tensor(st[:, 4:6], st[:, 4:6], st[:, 2:4], ALU.mult))
                link(v.tensor_scalar(st[:, 4:6], st[:, 4:6], -0.5, 1.5, ALU.mult, ALU.add))
                link(v.tensor_tensor(st[:, 6:8], st[:, 6:8], st[:, 4:6], ALU.mult))

            def weigh(dst, w, chunks, k0):
                n = len(chunks)
                for q, k in enumerate(chunks):
                    cs = cT[:, 1, k:k + 1]
                    if q == 0:
                        link(v.tensor_scalar(dst, w[:, k - k0, :], cs, None, ALU.mult))
                    else:
                        ins = v.scalar_tensor_tensor(out=dst, in0=w[:, k - k0, :], scalar=cs, in1=dst,
                                                     op0=ALU.mult, op1=ALU.add)
                        if q < n - 1:
                            link(ins)
                        else:
                            ins.then_inc(acc_ready, 1)

            def mod_part(phase):
                with dve.Fori(0, 2) as i:
                    enter(phase, i)
                    for b in range(2):
                        dve.wait_ge(slot_in[f"w{2 * b + 1}"], landed(f"w{2 * b + 1}", phase, i))
                        emptied(dve, f"A{b}", phase, i)
                        weigh(acc512[:, b, :], W[:, 2 * b + 1, :].rearrange("p (k n) -> p k n", k=HC),
                              range(HC, KC), HC)
                    leave(phase)

            dve.wait_ge(cact_ready, 1)
            mod_part("mod")
            enter("norm1")
            dve.wait_ge(ssq_ready, 2)
            inverse_root(0, ms_ready, root_ready, 1)
            for h in range(HALVES):
                v.tensor_scalar(xn[:, h, :, :], xr[:, h, :].rearrange("p (q k) -> p k q", k=KC),
                                st[:, 6 + h:7 + h], None, ALU.mult).then_inc(xn_ready, 1)
            leave("norm1")

            mod_part("mod2")
            enter("kv")
            dve.wait_ge(small_in, 16 * 3)
            for name in ("L0", "L1", "T0", "T1"):
                emptied(dve, name, "idx" if name[0] == "L" else "main")
            emptied(dve, "O", "main")
            filled(dve, "M", "kv")
            v.tensor_tensor(modT[:, :, :], bank["M"][:, 0:2 * KC].rearrange("p (v k) -> p v k", v=2),
                            colb[:, 0:2, :], ALU.add).then_inc(free["M"], 1)
            dve.wait_ge(free["M"], before("M", "kv") + 2)
            link(v.tensor_scalar(modT[:, 1, :], modT[:, 1, :], 1.0, None, ALU.add))
            link(v.tensor_tensor(modT[:, 1, :], modT[:, 1, :], colb[:, 2, :], ALU.mult))
            for k in range(KC):
                v.tensor_scalar(hT[:, k, :], hT[:, k, :], modT[:, 1, k:k + 1], modT[:, 0, k:k + 1],
                                ALU.mult, ALU.add).then_inc(h_ready, 1)
            dve.wait_ge(const_ready, 12)
            for b in range(2):
                filled(dve, f"A{b}", "kv")
                if b == 1:
                    dve.sem_inc(slot_free["w4"], 1)
                for a in range(2):
                    src = bank[f"A{b}"][a * HEAD:(a + 1) * HEAD, 0:S]
                    v.tensor_copy(kd[0:HEAD, 2 * b + a, 0:S], src)
                    last = v.tensor_copy(kd[HEAD:P, 2 * b + a, S:2 * S], src)
                last.then_inc(kd_ready, 1)
                dve.wait_ge(kd_ready, b + 1)
                dve.sem_inc(free[f"A{b}"], 1)
            filled(dve, "A1", "kv", 0, 2)
            dve.sem_inc(slot_free["w0"], 1)
            v.tensor_scalar(iw[:, :, :], bank["A1"][:, 0:32].rearrange("p (h e) -> p h e", h=2),
                            HEAD ** -0.5 * IDX_HEADS ** -0.5, None, ALU.mult).then_inc(iw_ready, 1)
            dve.wait_ge(iw_ready, 1)
            dve.sem_inc(free["A1"], 1)
            leave("kv")

            with dve.Fori(0, 2) as i:
                enter("idx", i)
                for b in range(2):
                    for j in range(2):
                        for h in range(HALVES):
                            filled(dve, f"rel{h}", "idx", i, 2 * b + j)
                            dve.sem_inc(free[f"L{h}"], 1)
                            for a in range(2):
                                ins = v.scalar_tensor_tensor(
                                    out=score[:, h, :], in0=rel[:, h, a * S:(a + 1) * S],
                                    scalar=iw[:, h, bass.ds(i * 8 + 4 * b + 2 * j + a, 1)],
                                    in1=score[:, h, :], op0=ALU.mult, op1=ALU.add)
                                if a == 0:
                                    link(ins)
                                else:
                                    ins.then_inc(free[f"rel{h}"], 1)
                                    dve.wait_ge(free[f"rel{h}"], before(f"rel{h}", "idx", i, 2 * b + j) + 2)
                leave("idx")
            enter("topk")
            for h in range(HALVES):
                link(v.tensor_tensor(work[:, h, :], score[:, h, :], amask[:, h, :], ALU.add))
            for r in range(TOPK // 8):
                for h in range(HALVES):
                    cur = work if r == 0 else score
                    link(v.max(st[:, 8 + 8 * h:16 + 8 * h], cur[:, h, :]))
                    link(v.match_replace(score[:, h, :], st[:, 8 + 8 * h:16 + 8 * h], cur[:, h, :], NEG))
            for h in range(HALVES):
                link(v.tensor_tensor(work[:, h, :], work[:, h, :], score[:, h, :], ALU.is_equal))
                link(v.tensor_scalar(amask[:, h, :], work[:, h, :], NEG, None, ALU.mult))
            leave("topk")

            def modulation(n, b, phase, i):
                dve.wait_ge(slot_in[f"w{n}"], landed(f"w{n}", phase, i))
                weigh(acc[:, b, :], W[:, n, :].rearrange("p (k n) -> p k n", k=KC), range(KC), 0)

            def mod_row(r, phase, i, pos, at):
                filled(dve, "M", phase, i, pos)
                o = modrow[r:r + 1, bass.ds(at, UNIT)]
                v.tensor_tensor(o, bank["M"][r:r + 1, 0:UNIT], o, ALU.add).then_inc(free["M"], 1)

            dve.wait_ge(modrow_in, 64)
            with dve.Fori(0, KV) as i:
                enter("main", i)

                def masked(n):
                    h = n % 2
                    filled(dve, f"L{n % 2}", "main", i, n // 2)
                    emptied(dve, f"pb{n}", "main", i)
                    p3 = pb[:, n, :].rearrange("p (a s) -> p a s", a=2)
                    v.scalar_tensor_tensor(out=p3, in0=bank[f"L{n % 2}"].rearrange("p (a s) -> p a s", a=2),
                                           scalar=HEAD ** -0.5,
                                           in1=amask[:, h, :].unsqueeze(1).to_broadcast([P, 2, S]),
                                           op0=ALU.mult, op1=ALU.add).then_inc(free[f"L{n % 2}"], 1)
                    dve.wait_ge(free[f"L{n % 2}"], before(f"L{n % 2}", "main", i, n // 2) + 2)
                    link(v.tensor_reduce(st[:, 24 + 2 * n:26 + 2 * n], p3, AX, ALU.max))
                    v.tensor_scalar(st[:, 8 + 2 * n:10 + 2 * n], st[:, 24 + 2 * n:26 + 2 * n], -1.0, None,
                                    ALU.mult).then_inc(lg_ready, 1)

                def normalise(n):
                    dve.wait_ge(exp_ready, i * 8 + 2 * n + 2)
                    link(v.reciprocal(st[:, 24 + 2 * n:26 + 2 * n], st[:, 16 + 2 * n:18 + 2 * n]))
                    for a in range(2):
                        o = pb[:, n, a * S:(a + 1) * S]
                        last = v.tensor_scalar(o, o, st[:, 24 + 2 * n + a:25 + 2 * n + a], None, ALU.mult)
                    last.then_inc(full[f"pb{n}"], 1)

                def conv(j):
                    filled(dve, f"A{j}", "main", i, 2)
                    if j == 1:
                        dve.sem_inc(slot_free["w1"], 1)
                    filled(dve, f"cg{j}", "main", i)
                    v.tensor_tensor(uT[:, j, 2:], bank[f"A{j}"][:, 0:S], cgT[:, j, :], ALU.mult)\
                        .then_inc(free[f"A{j}"], 1)
                    dve.wait_ge(free[f"A{j}"], before(f"A{j}", "main", i, 2) + 2)
                    w = [convc[:, q, bass.ds(i * 2 + j, 1)] for q in range(TAPS)]
                    v.tensor_scalar(yb[:, j, :], uT[:, j, 2:2 + S], w[2], None, ALU.mult)\
                        .then_inc(free[f"cg{j}"], 1)
                    dve.wait_ge(free[f"cg{j}"], before(f"cg{j}", "main", i) + 2)
                    for q in (1, 0):
                        link(v.scalar_tensor_tensor(out=yb[:, j, :], in0=uT[:, j, q:q + S], scalar=w[q],
                                                    in1=yb[:, j, :], op0=ALU.mult, op1=ALU.add))

                modulation(4, 0, "main", i)
                masked(0)
                masked(1)
                conv(0)
                masked(2)
                masked(3)
                mod_row(0, "main", i, 0, i * 512)
                normalise(0)
                normalise(1)
                conv(1)
                normalise(2)
                normalise(3)
                modulation(5, 1, "main", i)
                for j in range(2):
                    filled(dve, f"A{j}", "main", i, 3)
                    if j == 1:
                        dve.sem_inc(slot_free["w2"], 1)
                    v.tensor_tensor(RB[:, bass.ds(i * 512 + 2048 + j * S, S)], bank[f"A{j}"][:, 0:S],
                                    yb[:, j, :], ALU.mult).then_inc(free[f"A{j}"], 1)
                mod_row(0, "main", i, 1, i * 512 + UNIT)
                leave("main")

            with dve.Fori(0, 8) as i:
                enter("gate", i)

                def merge(j):
                    for b in range(2):
                        filled(dve, f"L{b}", "gate", i, j)
                        filled(dve, f"sg{b}", "gate", i, j)
                        dve.sem_inc(free[f"A{b}"], 1)
                        if b == 1 and j == 1:
                            dve.sem_inc(slot_free["w2"], 1)
                        v.tensor_tensor(yb[:, b, :], bank[f"L{b}"][:, 0:S], qs[:, b, :], ALU.mult)\
                            .then_inc(free[f"L{b}"], 1)
                        dve.wait_ge(free[f"L{b}"], before(f"L{b}", "gate", i, j) + 2)
                        dve.sem_inc(free[f"sg{b}"], 1)
                    v.tensor_tensor(RM[:, bass.ds(i * 512 + j * S, S)], yb[:, 0, :], yb[:, 1, :], ALU.add)\
                        .then_inc(mT_ready, 1)
                    dve.wait_ge(mT_ready, i * 2 + j + 1)

                modulation(3, 0, "gate", i)
                merge(0)
                mod_row(32, "gate", i, 0, i * UNIT)
                modulation(4, 1, "gate", i)
                merge(1)
                mod_row(64, "gate", i, 1, i * UNIT)
                leave("gate")

            dve.wait_ge(fgain_in, 16)
            for q, name in enumerate(("L0", "L1", "T0", "T1")):
                filled(dve, name, "spread", 0, 2)
                o = A2B[:, q * 512:(q + 1) * 512]
                v.scalar_tensor_tensor(out=o, in0=bank[name], scalar=1.0, in1=fgain[:, q * 512:(q + 1) * 512],
                                       op0=ALU.add, op1=ALU.mult)\
                    .then_inc(free[name], 1)

            for name in ("L0", "L1", "T0", "T1"):
                emptied(dve, name, "spread", 0, 1)
            with dve.Fori(0, 4) as i:
                enter("out", i)
                for b in range(2):
                    modulation(4 + b, b, "out", i)
                    at = i * 512 + b * UNIT
                    for h in range(HALVES):
                        filled(dve, f"A{h}", "out", i, b)
                        if h == 1:
                            dve.sem_inc(slot_free[f"w{b}"], 1)
                        v.tensor_tensor(yb[:, h, :], bank[f"A{h}"][:, 0:UNIT], g1B[:, bass.ds(at, UNIT)],
                                        ALU.mult).then_inc(free[f"A{h}"], 1)
                        dve.wait_ge(free[f"A{h}"], before(f"A{h}", "out", i, b) + 2)
                        o = xr[:, h, bass.ds(at, UNIT)]
                        v.tensor_tensor(o, o, yb[:, h, :], ALU.add).then_inc(x2_ready, 1)
                        dve.wait_ge(x2_ready, i * 4 + 2 * b + h + 1)
                    mod_row(96, "out", i, b, at)
                leave("out")

            enter("norm2")
            dve.wait_ge(ssq_ready, 2 + 16)
            link(v.tensor_reduce(st[:, 0:2], sq[:, :, :], AX, ALU.add))
            inverse_root(0, ms_ready, root_ready, 2)
            for name in ("L0", "L1", "T0", "T1"):
                emptied(dve, name, "norm2")
            for h in range(HALVES):
                perm = "p (q k) -> p k q"
                ins = v.scalar_tensor_tensor(out=h2[:, h, :, :], in0=xr[:, h, :].rearrange(perm, k=KC),
                                             scalar=st[:, 6 + h:7 + h], in1=A2B.rearrange(perm, k=KC),
                                             op0=ALU.mult, op1=ALU.mult)
                if h == 0:
                    link(ins)
                else:
                    ins.then_inc(choice_in, 1)
                    dve.wait_ge(choice_in, 1)
                v.tensor_tensor(h2[:, h, :, :], h2[:, h, :, :], B2B.rearrange(perm, k=KC), ALU.add)\
                    .then_inc(h2_ready, 1)
            leave("norm2")

            def gather_mask(t):
                for h in range(HALVES):
                    last = v.tensor_scalar(pg[:, h, :], iota[:, :], cols[:, h, bass.ds(t + 1, 1)], None, ALU.is_equal)
                last.then_inc(pg_ready, 1)

            enter("route")
            dve.wait_ge(const_ready, 12)
            filled(dve, "A0", "route")
            lg, gx, zs = R("lg"), R("gexp"), R("zs")
            A3 = bank["A0"][:, 0:P].rearrange("p (h n) -> p h n", h=2)[:, :, 0:GROUPS + EXPERTS]
            link(v.tensor_tensor(lg, A3, gb[:, :].unsqueeze(1).to_broadcast([P, 2, GROUPS + EXPERTS]), ALU.add))
            gl, el = lg[:, :, 0:GROUPS], lg[:, :, GROUPS:]

            def wide(t, n):
                return t.to_broadcast([P, 2, n])

            def first_max(dst, src, n, m):
                link(v.tensor_reduce(m, src, AX, ALU.max))
                m3 = wide(m.rearrange("p (h o) -> p h o", o=1), n)
                link(v.tensor_tensor(dst, src, m3, ALU.is_equal))
                link(v.tensor_tensor(dst, dst, R("down")[:, EXPERTS - n:].unsqueeze(1).to_broadcast([P, 2, n]),
                                     ALU.mult))
                link(v.tensor_reduce(R("t2"), dst, AX, ALU.max))
                link(v.tensor_tensor(dst, wide(R("t2").rearrange("p (h o) -> p h o", o=1), n),
                                     R("down")[:, EXPERTS - n:].unsqueeze(1).to_broadcast([P, 2, n]), ALU.is_equal))

            link(v.tensor_scalar(R("down"), eidx[:, :], -1.0, float(EXPERTS), ALU.mult, ALU.add))
            gm = R("gm")
            first_max(R("gsel"), gl, GROUPS, gm)
            v.tensor_tensor(gx, gl, wide(gm.rearrange("p (h o) -> p h o", o=1), GROUPS), ALU.subtract)\
                .then_inc(gexp_in, 1)
            dve.wait_ge(gexp_ready, 1)
            link(v.tensor_reduce(zs, gx, AX, ALU.add))
            link(v.reciprocal(R("pgr"), zs))
            e4 = el.rearrange("p h (g e) -> p h g e", g=GROUPS)
            gs4 = R("gsel")
            val = R("val")
            for h in range(HALVES):
                v4 = val[:, h, :].rearrange("p (g e) -> p g e", g=GROUPS)
                s4 = gs4[:, h, :].unsqueeze(2).to_broadcast([P, GROUPS, EPG])
                link(v.tensor_tensor(v4, e4[:, h], s4, ALU.mult))
                link(v.tensor_scalar(R("t4"), gs4[:, h, :], -1.0, -NEG, ALU.add, ALU.mult))
                link(v.tensor_tensor(v4, v4, R("t4").unsqueeze(2).to_broadcast([P, GROUPS, EPG]), ALU.add))
            first_max(R("one"), val, EXPERTS, R("m1"))
            link(v.scalar_tensor_tensor(out=R("val2"), in0=R("one"), scalar=1.1 * NEG, in1=val,
                                        op0=ALU.mult, op1=ALU.add))
            first_max(R("two"), R("val2"), EXPERTS, R("m2"))
            v.tensor_tensor(R("pexp"), R("m2"), R("m1"), ALU.subtract).then_inc(pexp_in, 1)
            link(v.tensor_tensor(R("choice"), R("one"), R("two"), ALU.add))
            v.tensor_copy(R("t2"), R("m1")).then_inc(choice_ready, 1)
            dve.wait_ge(pexp_ready, 1)
            link(v.tensor_scalar(R("p1"), R("pexp"), 1.0, None, ALU.add))
            link(v.reciprocal(R("p1"), R("p1")))
            link(v.tensor_tensor(R("p1"), R("p1"), R("pgr"), ALU.mult))
            link(v.tensor_tensor(R("p2"), R("p1"), R("pexp"), ALU.mult))
            link(v.tensor_tensor(R("val"), R("one"), wide(R("p1").rearrange("p (h o) -> p h o", o=1), EXPERTS),
                                 ALU.mult))
            link(v.tensor_tensor(R("val2"), R("two"), wide(R("p2").rearrange("p (h o) -> p h o", o=1), EXPERTS),
                                 ALU.mult))
            link(v.tensor_tensor(cwc[:, :, 1:1 + EXPERTS], R("val"), R("val2"), ALU.add))
            filled(dve, "A1", "route")
            rk = cols[:, :, 1:1 + EXPERTS]
            link(v.scalar_tensor_tensor(out=rk, in0=bank["A1"][:, 0:64].rearrange("p (h e) -> p h e", h=2),
                                        scalar=1000.0, in1=R("choice"), op0=ALU.add, op1=ALU.mult))
            link(v.tensor_scalar(rk, rk, -1000.0, None, ALU.add))
            gather_mask(0)
            dve.sem_inc(add_done, 2)
            cnt = bank["A1"][:, 64:96]
            link(v.tensor_scalar(R("ov"), cnt, float(TILE), None, ALU.is_gt))
            for b in range(2, S // TILE):
                ins = v.scalar_tensor_tensor(out=R("ov"), in0=cnt, scalar=float(b * TILE), in1=R("ov"),
                                             op0=ALU.is_gt, op1=ALU.add)
                if b < S // TILE - 1:
                    link(ins)
                else:
                    ins.then_inc(free["A1"], 1)
                    dve.wait_ge(free["A1"], before("A1", "expert") + 1)
            link(v.tensor_tensor_scan(R("incl"), ones[:, 0:EXPERTS], R("ov"), 0.0, ALU.mult, ALU.add))
            link(v.tensor_tensor(R("excl"), R("incl"), R("ov"), ALU.subtract))
            o7 = eidx[:, 0:OVER].unsqueeze(2).to_broadcast([P, OVER, EXPERTS])
            in7 = R("incl").unsqueeze(1).to_broadcast([P, OVER, EXPERTS])
            ex7 = R("excl").unsqueeze(1).to_broadcast([P, OVER, EXPERTS])
            own, first, tmp7 = R("own"), R("first"), R("tmp7")
            link(v.tensor_tensor(own, in7, o7, ALU.is_gt))
            link(v.tensor_tensor(first, ex7, o7, ALU.is_le))
            link(v.tensor_tensor(own, own, first, ALU.mult))
            link(v.tensor_tensor(first, o7, ex7, ALU.subtract))
            link(v.tensor_scalar(first, first, 1.0, float(TILE), ALU.add, ALU.mult))
            for h in range(HALVES):
                rk7 = cols[:, h, 1:1 + EXPERTS].unsqueeze(1).to_broadcast([P, OVER, EXPERTS])
                cw7 = cwc[:, h, 1:1 + EXPERTS].unsqueeze(1).to_broadcast([P, OVER, EXPERTS])
                link(v.tensor_tensor(tmp7, rk7, first, ALU.subtract))
                link(v.tensor_tensor(tmp7, tmp7, own, ALU.mult))
                link(v.tensor_reduce(cols[:, h, 1 + EXPERTS:1 + EXPERTS + OVER], tmp7, AX, ALU.add))
                link(v.tensor_tensor(tmp7, cw7, own, ALU.mult))
                link(v.tensor_reduce(cwc[:, h, 1 + EXPERTS:1 + EXPERTS + OVER], tmp7, AX, ALU.add))
            link(v.tensor_tensor(tmp7, own, eidx[:, 0:EXPERTS].unsqueeze(1).to_broadcast([P, OVER, EXPERTS]),
                                 ALU.mult))
            link(v.tensor_reduce(R("eid"), tmp7, AX, ALU.add))
            link(v.tensor_copy(plan_i[0:1, 0:OVER], R("eid")[0:1, :]))
            v.tensor_copy(plan_i[0:1, 8:9], R("incl")[0:1, EXPERTS - 1:EXPERTS]).then_inc(plan_ready, 1)
            leave("route")

            def adds(t, turns=range(8)):
                if 0 in turns:
                    dve.wait_ge(add_done, t * 8 + 2)
                for n in turns:
                    dve.wait_ge(cmb_done, t * 8 + n + 1)
                    h, q = n // 4, n % 4
                    o = xr[:, h, q * 512:(q + 1) * 512]
                    v.tensor_tensor(o, o, bank["OM"[n % 2]], ALU.add).then_inc(add_done, 1)

            def tile(t):
                dve.wait_ge(gather_done, t + 1)
                gather_mask(t + 1)
                dve.wait_ge(ptr_done, t + 1)
                for h in range(HALVES):
                    last = v.tensor_scalar(pw[:, h, :].rearrange("p (a s) -> p a s", a=2),
                                           iota[:, :].unsqueeze(1).to_broadcast([P, 2, TILE]),
                                           cols[:, h, bass.ds(t + 1, 1)], cwc[:, h, bass.ds(t + 1, 1)],
                                           ALU.is_equal, ALU.mult)
                last.then_inc(pw_ready, 1)
                adds(t, range(0, 2))
                dve.wait_ge(sil_ready, t + 1)
                v.tensor_tensor(actT, sil, bank["A1"].rearrange("p (j s) -> p j s", j=FC)[:, :, TILE:], ALU.mult)\
                    .then_inc(act_ready, 1)
                adds(t, range(2, 8))
                dve.wait_ge(slot_free["w5"], before("w5", "expert", t) + 2)
                v.tensor_tensor(ysb, pairT[:, :], g2s, ALU.mult).then_inc(y_ready, 1)

            with dve.Fori(0, EXPERTS) as e:
                tile(e)
            dve.wait_ge(plan_ready, 1)
            n_over = dve.value_load(plan_i[0:1, 8:9], min_val=0, max_val=OVER)
            with dve.Fori(0, OVER) as o:
                with dve.If(o < n_over):
                    tile(o + EXPERTS)
            adds(n_over + EXPERTS)

            dve.wait_ge(add_done, (n_over + EXPERTS) * 8 + 10)
            v.memset(st[:, 34:35], 0.0).then_inc(fin_chain, 1)
            dve.wait_ge(fin_ssq, 2)
            enter("last")
            inverse_root(0, fin_ms, fin_root, 1)
            leave("last")
            dve.wait_ge(gain_in, 16)
            for h in range(HALVES):
                v.scalar_tensor_tensor(out=xr[:, h, :], in0=xr[:, h, :], scalar=st[:, 6 + h:7 + h], in1=gfin,
                                       op0=ALU.mult, op1=ALU.mult).then_inc(fin_ready, 1)


NAMES = ["x", "c", "w_ada", "b_ada", "g_norm_mix", "w_in", "conv_w", "w_a_up", "w_b_out", "w_o", "g_norm_ffn",
         "w_rg", "b_rg", "w_re", "b_re", "w_e_gate", "w_e_up", "w_e_down", "g_norm_final"]


def kernel(**inputs):
    import numpy as np
    import concourse.bacc as bacc
    from concourse.bass_utils import run_bass_kernel_spmd

    nc = bacc.Bacc("TRN2", target_bir_lowering=False, num_devices=1)
    arrays, args = {}, []
    for name in NAMES:
        a = np.ascontiguousarray(inputs[name])
        arrays[f"in_{name}"] = a
        args.append(nc.dram_tensor(f"in_{name}", a.shape, mybir.dt.from_np(a.dtype), kind="ExternalInput").ap())
    args.append(nc.dram_tensor("out_x", (1, S, D), F32, kind="ExternalOutput").ap())
    block_kernel(nc, *args)
    r = run_bass_kernel_spmd(nc, [arrays], core_ids=[0])
    return r.results[0]["out_x"]
```

```python
from contextlib import ExitStack

import concourse.bass as bass
from concourse import mybir


P = 128
D = 2048
S = 256
HALVES = S // P
KC = D // P
N_MOD = 6
HEAD = 64
KV = 4
ATTN = 1024
CONV = 1024
TAPS = 3
IDX_HEADS = 16
TOPK = 64
GROUPS = 4
EPG = 8
EXPERTS = 32
FF = 512
FC = FF // P
TILE = 64
OVER = (2 * S - 1) // TILE
EPS = 1e-6
NEG = -3.0e38

COL_Q = 0
COL_K = COL_Q + ATTN
COL_V = COL_K + KV * HEAD
COL_IQ = COL_V + KV * HEAD
COL_IK = COL_IQ + IDX_HEADS * HEAD
COL_IW = COL_IK + HEAD
COL_BG = COL_IW + IDX_HEADS
COL_CG = COL_BG + CONV
COL_XC = COL_CG + CONV
COL_GA = COL_XC + CONV
COL_GB = COL_GA + D

SLOTS = 6
UNIT = 256
HC = KC // 2
QC = KC // 4

F32 = mybir.dt.float32
F32R = mybir.dt.float32r
I32 = mybir.dt.int32
ALU = mybir.AluOpType
ACT = mybir.ActivationFunctionType
AX = mybir.AxisListType.X

PLAN = [
    ("mod", 2, dict(w0=1, w1=1, w2=1, w3=1, A0=1, A1=1, acc=2, v=14)),
    ("norm1", 1, dict(L0=1, L1=1, T0=1, T1=1, A0=1, A1=1, O=2, M=1, v=5)),
    ("mod2", 2, dict(w0=1, w1=1, w2=1, w3=1, A0=1, A1=1, acc=2, v=14)),
    ("kv", 1, dict(w4=1, w5=1, w0=1, A0=3, A1=3, M=1, v=2)),
    ("idx", 2, dict(w1=1, w2=1, A0=2, A1=2, L0=4, L1=4, qs0=2, qs1=2, rel0=4, rel1=4, v=8)),
    ("topk", 1, dict(v=38)),
    ("main", 4, dict(w3=1, w0=1, w1=1, w2=1, w4=2, w5=2, A0=4, A1=4, L0=2, L1=2, T0=2, T1=2, O=1, M=4,
                     qs0=1, qs1=1, cg0=1, cg1=1, pb0=1, pb1=1, pb2=1, pb3=1, pT0=2, pT1=2, vst=1, acc=4, v=72)),
    ("gate", 8, dict(w0=1, w1=1, w2=1, w3=1, A0=2, A1=2, L0=2, L1=2, M=1, sg0=2, sg1=2, acc=1, v=15)),
    ("spread", 1, dict(L0=3, L1=3, T0=3, T1=3)),
    ("out", 4, dict(w0=1, w1=1, w2=1, w3=1, A0=1, A1=1, T0=1, T1=1, M=2, acc=2, v=30)),
    ("spread2", 1, dict(L0=1, L1=1, T0=1, T1=1)),
    ("norm2", 1, dict(L0=1, L1=1, T0=1, T1=1, A0=1, A1=1, O=1, M=1, v=10)),
    ("route", 1, dict(A0=1, A1=1, v=58)),
    ("expert", EXPERTS + OVER, dict(w0=1, w1=1, w2=1, w3=1, w4=1, w5=1)),
    ("last", 1, dict(v=5)),
]
DMAS = {("gate", "w2"): 3, ("expert", "w0"): 2, ("expert", "w1"): 2, ("expert", "w2"): 2, ("expert", "w3"): 2}
BUFFERS = ("qs0", "qs1", "rel0", "rel1", "cg0", "cg1", "pb0", "pb1", "pb2", "pb3", "pT0", "pT1", "vst", "sg0", "sg1")


def before(name, phase, i=0, pos=0):
    n = 0
    for other, runs, events in PLAN:
        if other == phase:
            return n + i * events.get(name, 0) + pos
        n += runs * events.get(name, 0)


def landed(slot, phase, i=0, pos=None):
    n = 0
    for other, runs, events in PLAN:
        per = 16 * DMAS.get((other, slot), 1) * events.get(slot, 0)
        if other == phase:
            return n + i * per + (per if pos is None else 16 * (pos + 1))
        n += runs * per


def block_kernel(nc, x, c, w_ada, b_ada, g_norm_mix, w_in, conv_w, w_a_up, w_b_out, w_o, g_norm_ffn,
                 w_rg, b_rg, w_re, b_re, w_e_gate, w_e_up, w_e_down, g_norm_final, out):
    ada_v = w_ada[0].rearrange("(p k) n -> p k n", p=P)
    in_v = w_in[0].rearrange("(p k) n -> p k n", p=P)
    a_up_v = w_a_up[0].rearrange("(j p) n -> p j n", p=P)
    b_out_v = w_b_out[0].rearrange("(j p) n -> p j n", p=P)
    o_v = w_o[0].rearrange("(j p) n -> p j n", p=P)
    gate_v = w_e_gate[0].rearrange("e (p k) f -> e p k f", p=P)
    up_v = w_e_up[0].rearrange("e (p k) f -> e p k f", p=P)
    down_v = w_e_down[0].rearrange("e (p j) d -> e p j d", p=P)
    x_v = x[0].rearrange("(h p) d -> p h d", p=P)
    out_v = out[0].rearrange("(h p) d -> p h d", p=P)

    with ExitStack() as ctx:
        def sb(name, shape, dt=F32):
            return ctx.enter_context(nc.sbuf_tensor(name, shape, dt))

        def sem(name):
            return ctx.enter_context(nc.semaphore(name))

        base = (nc.sbuf_base + 31) // 32 * 32
        W = sb("weight_slots", [P, SLOTS, 4096])
        xr = sb("x_resid", [P, HALVES, D])
        RA = sb("region_a", [P, 4096])
        RB = sb("region_b", [P, 4096])
        RM = sb("region_m", [P, 4096])
        RH = sb("region_h", [P, 4096])
        ikd = sb("ik_diag", [P, 2 * S])
        amask = sb("attn_mask", [P, HALVES, S])
        qs = sb("q_stage", [P, 2, S])
        pT = sb("probs_T", [P, 2, 512])
        modrow = sb("mod_rows", [P, D])
        acc = sb("ada_acc", [P, 2, UNIT])
        cgT = sb("cg_T", [P, 2, S])
        uT = sb("u_T", [P, 2, S + TAPS - 1])
        ident = sb("ident", [P, P])
        ones = sb("ones", [P, P])
        tri = sb("tri", [P, P])
        cT = sb("c_T", [P, 2, KC])
        modT = sb("mod_T", [P, 2, KC])
        colb = sb("col_b", [P, 3, KC])
        convc = sb("conv_c", [P, TAPS, 8])
        iw = sb("idx_w", [P, HALVES, IDX_HEADS])
        st = sb("stats", [P, 40])
        gb = sb("router_bias", [P, GROUPS + EXPERTS])
        iota = sb("iota", [P, TILE])
        eidx = sb("expert_index", [P, EXPERTS])
        cols = sb("rank_cols", [P, HALVES, 42])
        cwc = sb("weight_cols", [P, HALVES, 42])
        plan_i = sb("plan_i", [1, 16], I32)

        hT = RA[:, :].rearrange("p (k t) -> p k t", k=KC)
        xn = RB[:, :].rearrange("p (h k q) -> p h k q", h=HALVES, k=KC)
        oT = RB[:, 0:2048].rearrange("p (b t) -> p b t", b=8)
        zT = RB[:, 2048:4096].rearrange("p (b t) -> p b t", b=8)
        rows = RM[0:1, :]
        vtok = RM[:, 0:512].rearrange("p (h n) -> p h n", h=HALVES)
        vst = RM[:, 512:640].rearrange("p (h n) -> p h n", h=HALVES)
        mT = RM[:, :].rearrange("p (b t) -> p b t", b=16)
        kd = RH[:, 0:2048].rearrange("p (g n) -> p g n", g=KV)
        pb = RH[:, 2048:4096].rearrange("p (n m) -> p n m", n=4)
        rel = RH[:, 2048:3072].rearrange("p (h n) -> p h n", h=2)
        score = RH[:, 3072:3584].rearrange("p (h s) -> p h s", h=2)
        work = RH[:, 3584:4096].rearrange("p (h s) -> p h s", h=2)
        acc512 = RH[:, 0:1024].rearrange("p (b n) -> p b n", b=2)
        yb = ikd[:, :].rearrange("p (b t) -> p b t", b=2)
        g1B = RH[:, 0:2048]
        fgain = RH[:, 2048:4096]
        slot_off = [base + 4 * 4096 * n for n in range(SLOTS)]
        a_off = base + 4 * (SLOTS * 4096 + HALVES * D)
        hL = nc.alloc_sbuf_tensor_at("h_low", [P, KC, S], F32R, offset=a_off)
        hH = nc.alloc_sbuf_tensor_at("h_high", [P, KC, S], F32R, offset=a_off + 3 * 4 * 4096)
        mH = nc.alloc_sbuf_tensor_at("merged_high", [P, KC, S], F32R, offset=a_off)
        mL = nc.alloc_sbuf_tensor_at("merged_low", [P, KC, S], F32R, offset=a_off + 2 * 4 * 4096)
        ringL = nc.alloc_sbuf_tensor_at("weights_low", [P, 4, HC, P], F32R, offset=slot_off[4])
        ringH = nc.alloc_sbuf_tensor_at("weights_high", [P, 4, HC, P], F32R, offset=slot_off[5])
        quarterL = nc.alloc_sbuf_tensor_at("out_weights_low", [P, 4, QC, UNIT], F32R, offset=slot_off[4])
        quarterH = nc.alloc_sbuf_tensor_at("out_weights_high", [P, 4, QC, UNIT], F32R, offset=slot_off[5])
        A2B, B2B = RB[:, 0:2048], RB[:, 2048:4096]
        h2 = RH[:, :].rearrange("p (h k q) -> p h k q", h=HALVES, k=KC)
        h2T = RM[:, :].rearrange("p (k t) -> p k t", k=KC)
        hsel = RM[:, 0:1024].rearrange("p (k s) -> p k s", k=KC)
        gus = RM[:, 1024:1536].rearrange("p (j q) -> p j q", j=FC)
        sil = RM[:, 1536:1792].rearrange("p (j s) -> p j s", j=FC)
        actT = RM[:, 1792:2048].rearrange("p (j s) -> p j s", j=FC)
        ysb = RM[:, 2048:3072]
        pg = RM[:, 3072:3200].rearrange("p (h s) -> p h s", h=2)
        pw = RM[:, 3200:3456].rearrange("p (h s) -> p h s", h=2)
        pt_lo, pt_hi = RB[:, 0:256], RB[:, 256:512]
        g2s = pT[:, :, :].rearrange("p a b -> p (a b)")
        cstage = qs[0:TAPS * 8, 0, 0:P]
        gfin = RB[:, 2048:4096]
        wr = sb("router_w", [P, KC, GROUPS + EXPERTS])
        sq = sb("square_sums", [P, HALVES, 8])

        scratch, at = {}, 512
        for name, shape in dict(lg=(2, 36), gsel=(2, 4), gexp=(2, 4), gm=(2,), zs=(2,), pgr=(2,), down=(32,),
                                val=(2, 32), val2=(2, 32), one=(2, 32), two=(2, 32), choice=(2, 32), m1=(2,),
                                m2=(2,), t2=(2,), t4=(4,), pexp=(2,), p1=(2,), p2=(2,), ov=(32,), incl=(32,),
                                excl=(32,), own=(OVER, 32), first=(OVER, 32), tmp7=(OVER, 32),
                                eid=(OVER,)).items():
            n = shape[0] * (shape[1] if len(shape) > 1 else 1)
            scratch[name] = RB[:, at:at + n] if len(shape) == 1 else \
                RB[:, at:at + n].rearrange("p (a b) -> p a b", a=shape[0])
            at += n
        assert at <= 2048

        def R(name):
            return scratch[name]

        bank = {n: ctx.enter_context(nc.psum_tensor(f"bank_{n}", [P, 512], F32)) for n in ("A0", "A1")}
        pairL = ctx.enter_context(nc.psum_tensor("bank_L", [P, 1024], F32))
        pairT = ctx.enter_context(nc.psum_tensor("bank_T", [P, 1024], F32))
        pairO = ctx.enter_context(nc.psum_tensor("bank_OM", [P, 1024], F32))
        bank.update(L0=pairL[:, 0:512], L1=pairL[:, 512:1024], T0=pairT[:, 0:512], T1=pairT[:, 512:1024],
                    O=pairO[:, 0:512], M=pairO[:, 512:1024], A0=bank["A0"][:, :], A1=bank["A1"][:, :])

        slot_in = {f"w{n}": sem(f"slot{n}_landed") for n in range(SLOTS)}
        slot_free = {f"w{n}": sem(f"slot{n}_free") for n in range(SLOTS)}
        full = {n: sem(f"{n}_full") for n in (*bank, *BUFFERS)}
        free = {n: sem(f"{n}_free") for n in (*bank, *BUFFERS)}
        chain = sem("vector_chain")
        acc_ready = sem("acc_ready")
        names = """c_in x_in small_in conv_in modrow_in const_ready pool_step cact_ready ssq_ready ms_ready root_ready
            xn_ready h_ready kd_ready v_ready ikd_ready iw_ready lg_ready exp_ready fgain_in
            hH_ready hL_ready mH_ready mL_ready gain2_ready wH_ready wL_ready ring_used mT_ready
            gain_in x2_ready h2_ready router_in gexp_ready pexp_ready choice_ready
            gexp_in pexp_in plan_ready pg_ready pw_ready gather_done hsel_ready ptr_done pt_ready pv_done
            gus_ready gut_done sil_ready act_ready y_ready cmb_done add_done fin_ssq fin_ms fin_root
            fin_ready stored""".split()
        (c_in, x_in, small_in, conv_in, modrow_in, const_ready, pool_step, cact_ready, ssq_ready, ms_ready, root_ready,
         xn_ready, h_ready, kd_ready, v_ready, ikd_ready, iw_ready, lg_ready, exp_ready, fgain_in,
         hH_ready, hL_ready, mH_ready, mL_ready, gain2_ready, wH_ready, wL_ready, ring_used, mT_ready,
         gain_in, x2_ready, h2_ready, router_in, gexp_ready, pexp_ready, choice_ready,
         gexp_in, pexp_in, plan_ready, pg_ready, pw_ready, gather_done, hsel_ready, ptr_done, pt_ready, pv_done,
         gus_ready, gut_done, sil_ready, act_ready, y_ready, cmb_done, add_done, fin_ssq, fin_ms, fin_root,
         fin_ready, stored) = (sem(n) for n in names)

        def filled(eng, name, phase, i=0, pos=0):
            eng.wait_ge(full[name], before(name, phase, i, pos) + 1)

        def emptied(eng, name, phase, i=0, pos=0):
            eng.wait_ge(free[name], before(name, phase, i, pos) + 1)

        def half_block(m):
            j, b, x = m // 4, m // 2 % 2, m % 2
            return W[:, b, :].rearrange("p (k n) -> p k n", k=KC)[:, x * HC:(x + 1) * HC, j * P:(j + 1) * P]

        def quarter(b, x):
            return W[:, b, :].rearrange("p (k n) -> p k n", k=KC)[:, x * QC:(x + 1) * QC, :]

        block = ctx.enter_context(nc.Block())

        @block.sync
        def _(sp):
            def claim(slot, phase, i=0, pos=0):
                sp.wait_ge(slot_free[slot], before(slot, phase, i, pos) + 1)

            def slot_view(n, k):
                return W[:, n, :].rearrange("p (k n) -> p k n", k=k)

            for n in range(SLOTS):
                sp.sem_inc(slot_free[f"w{n}"], 1)
            for phase, start in (("mod", 0), ("mod2", 2)):
                with sp.Fori(0, 2) as i:
                    for n in range(4):
                        at = sp.snap(i * 1024 + start * 1024 + (n // 2) * 512)
                        claim(f"w{n}", phase, i)
                        sp.dma_start(slot_view(n, HC), ada_v[:, (n % 2) * HC:(n % 2 + 1) * HC, bass.ds(at, 512)])\
                            .then_inc(slot_in[f"w{n}"], 16)
            for slot, n, col in (("w4", 4, COL_K), ("w5", 5, COL_V)):
                claim(slot, "kv")
                sp.dma_start(slot_view(n, KC), in_v[:, :, col:col + UNIT]).then_inc(slot_in[slot], 16)
            claim("w0", "kv")
            sp.dma_start(slot_view(0, KC)[:, :, 0:HEAD + IDX_HEADS], in_v[:, :, COL_IK:COL_BG])\
                .then_inc(slot_in["w0"], 16)
            with sp.Fori(0, 2) as i:
                for b in range(2):
                    at = sp.snap(i * 512 + COL_IQ + b * UNIT)
                    claim(f"w{1 + b}", "idx", i)
                    sp.dma_start(slot_view(1 + b, KC), in_v[:, :, bass.ds(at, UNIT)])\
                        .then_inc(slot_in[f"w{1 + b}"], 16)
            with sp.Fori(0, KV) as i:
                for pos, units in enumerate((((3, COL_Q), (0, COL_CG)), ((1, COL_XC), (2, COL_BG)))):
                    for n, col in units:
                        at = sp.snap(i * UNIT + col)
                        claim(f"w{n}", "main", i)
                        sp.dma_start(slot_view(n, KC), in_v[:, :, bass.ds(at, UNIT)])\
                            .then_inc(slot_in[f"w{n}"], 16)
                    for b in range(2):
                        at = sp.snap(i * 512 + (2 + pos) * D + b * UNIT)
                        claim(f"w{4 + b}", "main", i, pos)
                        sp.dma_start(slot_view(4 + b, KC), ada_v[:, :, bass.ds(at, UNIT)])\
                            .then_inc(slot_in[f"w{4 + b}"], 16)
            with sp.Fori(0, 8) as i:
                def gate_unit(n, col):
                    at = sp.snap(i * UNIT + col)
                    claim(f"w{n}", "gate", i)
                    sp.dma_start(slot_view(n, KC), in_v[:, :, bass.ds(at, UNIT)])\
                        .then_inc(slot_in[f"w{n}"], 16)

                gate_unit(0, COL_GA)
                at = sp.snap(i * UNIT)
                claim("w2", "gate", i)
                for q in (4, 0):
                    sp.dma_start(slot_view(2, KC)[:, q:q + 4, :], a_up_v[:, q:q + 4, bass.ds(at, UNIT)])\
                        .then_inc(slot_in["w2"], 16)
                sp.dma_start(slot_view(2, KC)[:, 8:16, :], b_out_v[:, :, bass.ds(at, UNIT)])\
                    .then_inc(slot_in["w2"], 16)
                gate_unit(1, COL_GB)
                at = sp.snap(i * UNIT + 4 * D)
                claim("w3", "gate", i)
                sp.dma_start(slot_view(3, KC), ada_v[:, :, bass.ds(at, UNIT)]).then_inc(slot_in["w3"], 16)
            with sp.Fori(0, 4) as i:
                for b in range(2):
                    at = sp.snap(i * 512 + b * UNIT)
                    claim(f"w{b}", "out", i)
                    sp.dma_start(slot_view(b, KC), o_v[:, :, bass.ds(at, UNIT)])\
                        .then_inc(slot_in[f"w{b}"], 16)
                    at = sp.snap(i * 512 + 5 * D + b * UNIT)
                    claim(f"w{2 + b}", "out", i)
                    sp.dma_start(slot_view(2 + b, KC), ada_v[:, :, bass.ds(at, UNIT)])\
                        .then_inc(slot_in[f"w{2 + b}"], 16)

            sp.wait_ge(full["T1"], before("T1", "spread2"))

            def load_expert(e, t):
                for n in range(4):
                    claim(f"w{n}", "expert", t)
                    v = W[:, n, :].rearrange("p (g k f) -> p g k f", g=2, k=QC)
                    for g, src in ((0, gate_v), (1, up_v)):
                        sp.dma_start(v[:, g], src[e][:, n * QC:(n + 1) * QC, :]).then_inc(slot_in[f"w{n}"], 16)
                for n in range(2):
                    claim(f"w{4 + n}", "expert", t)
                    sp.dma_start(W[:, 4 + n, :].rearrange("p (j d) -> p j d", j=2),
                                 down_v[e][:, 2 * n:2 * n + 2, :]).then_inc(slot_in[f"w{4 + n}"], 16)

            with sp.Fori(0, EXPERTS) as e:
                load_expert(e, e)
            sp.wait_ge(plan_ready, 1)
            n_over = sp.value_load(plan_i[0:1, 8:9], min_val=0, max_val=OVER)
            with sp.Fori(0, OVER) as o:
                with sp.If(o < n_over):
                    e = sp.value_load(plan_i[0:1, bass.ds(o, 1)], min_val=0, max_val=EXPERTS - 1)
                    load_expert(e, o + EXPERTS)
            for n in range(4):
                h, c = n // 2, slice(n % 2 * (D // 2), (n % 2 + 1) * (D // 2))
                sp.wait_ge(fin_ready, n + 1)
                sp.dma_start(out_v[:, h, c], xr[:, h, c]).then_inc(stored, 16)
            sp.wait_ge(stored, 16 * 4)

        @block.gpsimd
        def _(pool):
            g = nc.gpsimd
            g.memset(ones[:, :], 1.0).then_inc(pool_step, 1)
            g.memset(ident[:, :], 0.0).then_inc(pool_step, 1)
            pool.wait_ge(pool_step, 2)
            g.affine_select(out=ident[:, :], in_=ident[:, :], compare_op=ALU.not_equal, fill=1.0, base=0,
                            pattern=[[-1, P]], channel_multiplier=1).then_inc(const_ready, 1)
            g.memset(modrow[:, :], 0.0).then_inc(const_ready, 1)
            g.affine_select(out=tri[:, :], in_=ones[:, :], compare_op=ALU.is_gt, fill=0.0, base=0,
                            pattern=[[1, P]], channel_multiplier=-1).then_inc(const_ready, 1)
            g.iota(iota[:, :], pattern=[[1, TILE]], base=0, channel_multiplier=0,
                   allow_small_or_imprecise_dtypes=True).then_inc(const_ready, 1)
            g.iota(eidx[:, :], pattern=[[1, EXPERTS]], base=0, channel_multiplier=0,
                   allow_small_or_imprecise_dtypes=True).then_inc(const_ready, 1)
            g.memset(amask[:, :, :], 0.0).then_inc(pool_step, 1)
            pool.wait_ge(pool_step, 3)
            g.affine_select(out=amask[:, :, :], in_=amask[:, :, :], compare_op=ALU.is_ge, fill=NEG, base=0,
                            pattern=[[P, HALVES], [-1, S]], channel_multiplier=1).then_inc(const_ready, 1)
            g.memset(ikd[:, :], 0.0).then_inc(const_ready, 1)
            g.memset(uT[:, :, 0:TAPS - 1], 0.0).then_inc(const_ready, 1)
            g.memset(cols[:, :, :], -1.0).then_inc(const_ready, 1)
            g.memset(cwc[:, :, :], 0.0).then_inc(const_ready, 1)
            g.memset(score, 0.0).then_inc(const_ready, 1)
            emptied(pool, "A0", "kv")
            emptied(pool, "A1", "kv")
            g.memset(RH[:, 0:2048], 0.0).then_inc(const_ready, 1)
            pool.wait_ge(v_ready, 2)
            with pool.Fori(0, KV) as i:
                emptied(pool, "vst", "main", i)
                g.tensor_copy(vst[:, :, :], vtok[:, :, bass.ds(i * HEAD, HEAD)]).then_inc(full["vst"], 1)
            def low(i):
                for m in range(8):
                    pool.wait_ge(wH_ready, i * 8 + m + 1)
                    g.tensor_tensor(ringL[:, m % 4], half_block(m), ringH[:, m % 4].bitcast(F32), ALU.subtract)\
                        .then_inc(wL_ready, 1)
                    if m == 5 or m == 7:
                        pool.wait_ge(wL_ready, i * 8 + m + 1)
                        pool.sem_inc(slot_free[f"w{(m - 5) // 2}"], 1)

            with pool.Fori(0, 8) as i:
                low(i)
            with pool.Fori(0, 4) as i:
                for b in range(2):
                    for x in range(4):
                        n = 64 + 4 * b + x + 1
                        pool.wait_ge(wH_ready, i * 8 + n)
                        g.tensor_tensor(quarterL[:, x], quarter(b, x), quarterH[:, x].bitcast(F32), ALU.subtract)\
                            .then_inc(wL_ready, 1)
                    pool.wait_ge(wL_ready, i * 8 + n)
                    pool.sem_inc(slot_free[f"w{b}"], 1)
            filled(pool, "A0", "route")
            g.memset(RB[:, 0:512], 0.0)
            g.memset(pw, 0.0).then_inc(pw_ready, 1)
            g.memset(ysb, 0.0).then_inc(y_ready, 1)
            g.memset(actT, 0.0).then_inc(act_ready, 1)
            g.memset(gus, 0.0).then_inc(gus_ready, 1)

        @block.scalar
        def _(act):
            a = nc.scalar
            for name in free:
                act.sem_inc(free[name], 1)

            act.dma_start(cT[:, 0, :], c[0].rearrange("(p k) -> p k", p=P)).then_inc(c_in, 16)
            for h in range(HALVES):
                act.dma_start(xr[:, h, :], x_v[:, h, :]).then_inc(x_in, 16)
            act.dma_start(colb[:, 0, :], b_ada[0, 0:D].rearrange("(p k) -> p k", p=P)).then_inc(small_in, 16)
            act.dma_start(colb[:, 1, :], b_ada[0, D:2 * D].rearrange("(p k) -> p k", p=P)).then_inc(small_in, 16)
            act.dma_start(colb[:, 2, :], g_norm_mix[0].rearrange("(p k) -> p k", p=P)).then_inc(small_in, 16)
            act.dma_start(cstage, conv_w[0].rearrange("j (b p) -> (j b) p", p=P)).then_inc(conv_in, 16)
            act.wait_ge(c_in, 16)
            a.activation(cT[:, 1, :], cT[:, 0, :], ACT.Silu).then_inc(cact_ready, 1)
            act.wait_ge(x_in, 16 * HALVES)
            for h in range(HALVES):
                a.activation(RB[:, h * D:(h + 1) * D], xr[:, h, :], ACT.Square,
                             accum_out=st[:, h:h + 1]).then_inc(ssq_ready, 1)
            act.dma_start(wr[:, :, 0:GROUPS], w_rg[0].rearrange("(p k) e -> p k e", p=P)).then_inc(router_in, 16)
            act.dma_start(wr[:, :, GROUPS:], w_re[0].rearrange("(p k) e -> p k e", p=P)).then_inc(router_in, 16)
            act.dma_start(gb[:, 0:GROUPS], b_rg[0:1, :].to_broadcast([P, GROUPS])).then_inc(router_in, 16)
            act.dma_start(gb[:, GROUPS:], b_re[0:1, :].to_broadcast([P, EXPERTS])).then_inc(router_in, 16)
            act.wait_ge(const_ready, 2)
            for v in range(4):
                act.dma_start(modrow[32 * v:32 * v + 1, :], b_ada[0:1, (2 + v) * D:(3 + v) * D])\
                    .then_inc(modrow_in, 16)

            def mod_rows(phase, start):
                with act.Fori(0, 2) as i:
                    for b in range(2):
                        filled(act, f"A{b}", phase, i)
                        a.activation(rows[:, bass.ds(i * 1024 + start * 1024 + b * 512, 512)],
                                     bank[f"A{b}"][0:1, :], ACT.Copy).then_inc(free[f"A{b}"], 1)

            mod_rows("mod", 0)
            act.wait_ge(ms_ready, 1)
            a.activation(st[:, 4:6], st[:, 2:4], ACT.Sqrt).then_inc(root_ready, 1)
            for n, name in enumerate(("L0", "L1", "T0", "T1", "A0", "A1", "O", "M")):
                h, k = n // 4, (n % 4) * 4
                filled(act, name, "norm1")
                a.activation(hT[:, k:k + 4, h * P:(h + 1) * P],
                             bank[name].rearrange("p (k t) -> p k t", k=4), ACT.Copy).then_inc(free[name], 1)
            filled(act, "O", "norm1", 0, 1)
            a.activation(convc[:, :, :], bank["O"][:, 0:TAPS * 8].rearrange("p (j b) -> p j b", j=TAPS),
                         ACT.Copy).then_inc(free["O"], 1)
            mod_rows("mod2", 2)
            for h in range(HALVES):
                filled(act, f"A{h}", "kv", 0, 1)
                if h == 1:
                    act.sem_inc(slot_free["w5"], 1)
                a.activation(vtok[:, h, :], bank[f"A{h}"][:, 0:UNIT], ACT.Copy).then_inc(v_ready, 1)
                act.wait_ge(v_ready, h + 1)
                act.sem_inc(free[f"A{h}"], 1)
            filled(act, "A0", "kv", 0, 2)
            act.wait_ge(const_ready, 11)
            a.activation(ikd[0:HEAD, 0:S], bank["A0"][0:HEAD, 0:S], ACT.Copy).then_inc(ikd_ready, 1)
            a.activation(ikd[HEAD:P, S:2 * S], bank["A0"][0:HEAD, 0:S], ACT.Copy).then_inc(ikd_ready, 1)
            act.wait_ge(ikd_ready, 2)
            act.sem_inc(free["A0"], 1)

            with act.Fori(0, 2) as i:
                for b in range(2):
                    for j in range(2):
                        filled(act, f"A{j}", "idx", i, b)
                        if j == 1:
                            act.sem_inc(slot_free[f"w{1 + b}"], 1)
                        a.activation(qs[:, j, :], bank[f"A{j}"][:, 0:S], ACT.Copy).then_inc(full[f"qs{j}"], 1)
                    for j in range(2):
                        for h in range(HALVES):
                            filled(act, f"L{h}", "idx", i, 2 * b + j)
                            emptied(act, f"rel{h}", "idx", i, 2 * b + j)
                            a.activation(rel[:, h, :], bank[f"L{h}"], ACT.Relu).then_inc(full[f"rel{h}"], 1)

            with act.Fori(0, KV) as i:
                def cg(j):
                    filled(act, f"A{j}", "main", i, 1)
                    emptied(act, f"cg{j}", "main", i)
                    if j == 1:
                        act.sem_inc(slot_free["w0"], 1)
                    a.activation(cgT[:, j, :], bank[f"A{j}"][:, 0:S], ACT.Copy).then_inc(full[f"cg{j}"], 1)
                    filled(act, f"cg{j}", "main", i)
                    act.sem_inc(free[f"A{j}"], 1)

                def expo(n):
                    act.wait_ge(lg_ready, i * 4 + n + 1)
                    for h in range(2):
                        a.activation(pb[:, n, h * S:(h + 1) * S], pb[:, n, h * S:(h + 1) * S], ACT.Exp,
                                     bias=st[:, 8 + 2 * n + h:9 + 2 * n + h],
                                     accum_out=st[:, 16 + 2 * n + h:17 + 2 * n + h]).then_inc(exp_ready, 1)

                for j in range(2):
                    filled(act, f"A{j}", "main", i, 0)
                    if j == 1:
                        act.sem_inc(slot_free["w3"], 1)
                    a.activation(qs[:, j, :], bank[f"A{j}"][:, 0:S], ACT.Copy).then_inc(full[f"qs{j}"], 1)
                cg(0)
                expo(0)
                expo(1)
                cg(1)
                expo(2)
                expo(3)
                for n in range(4):
                    filled(act, f"T{n % 2}", "main", i, n // 2)
                    if n >= 2:
                        act.wait_ge(pv_done, i * 2 + n - 1)
                    a.activation(pT[:, n % 2, :], bank[f"T{n % 2}"], ACT.Copy).then_inc(full[f"pT{n % 2}"], 1)
                filled(act, "O", "main", i)
                act.sem_inc(free["vst"], 1)
                a.activation(RB[:, bass.ds(i * 512, 512)], bank["O"], ACT.Copy).then_inc(free["O"], 1)

            def high(i, m, used=True):
                if m % 2 == 0 and used:
                    act.wait_ge(ring_used, i * 4 + m // 2 - 1)
                if m < 4 and m % 2 == 0:
                    b = m // 2
                    act.wait_ge(slot_in[f"w{b}"], landed(f"w{b}", "gate", i))
                a.activation(ringH[:, m % 4], half_block(m), ACT.Copy).then_inc(wH_ready, 1)

            for n in (4, 5):
                act.wait_ge(slot_free[f"w{n}"], before(f"w{n}", "gate") + 1)
            high(0, 0, False)
            high(0, 1, False)
            for n in range(4):
                emptied(act, f"pb{n}", "gate")
            for q in range(4):
                a.activation(hH[:, 4 * q:4 * q + 4, :], hT[:, 4 * q:4 * q + 4, :], ACT.Copy).then_inc(hH_ready, 1)
            high(0, 2, False)
            high(0, 3, False)

            def gates(i, more=True):
                for n in range(4):
                    j, b = n // 2, n % 2
                    ahead = 2 * n + 4
                    if n == 2:
                        filled(act, "L1", "gate", i, 1)
                        act.sem_inc(slot_free["w2"], 1)
                    if n < 2 or (n < 3 and more):
                        high(i + ahead // 8 if ahead >= 8 else i, ahead % 8)
                    filled(act, f"A{b}", "gate", i, j)
                    emptied(act, f"sg{b}", "gate", i, j)
                    a.activation(qs[:, b, :], bank[f"A{b}"][:, 0:S], ACT.Sigmoid).then_inc(full[f"sg{b}"], 1)
                    if n == 3 and more:
                        high(i + 1, ahead % 8)
                    if n < 2 or more:
                        high(i + ahead // 8 if ahead >= 8 else i, ahead % 8 + 1)

            with act.Fori(0, 7) as i:
                gates(i)
            gates(7, more=False)
            act.dma_start(fgain, g_norm_ffn[0:1, :].to_broadcast([P, D])).then_inc(fgain_in, 16)
            def quarter_high(i, b, x):
                if x == 0:
                    act.wait_ge(slot_in[f"w{b}"], landed(f"w{b}", "out", i))
                a.activation(quarterH[:, x], quarter(b, x), ACT.Copy).then_inc(wH_ready, 1)

            for q in range(4):
                act.wait_ge(mT_ready, 4 * q + 4)
                a.activation(mH[:, 4 * q:4 * q + 4, :], mT[:, 4 * q:4 * q + 4, :], ACT.Copy).then_inc(mH_ready, 1)
            for x in range(4):
                quarter_high(0, 0, x)
            for turn, dst in enumerate((g1B, B2B, A2B)):
                for q, name in enumerate(("L0", "L1", "T0", "T1")):
                    filled(act, name, "spread", 0, turn)
                    a.activation(dst[:, q * 512:(q + 1) * 512], bank[name], ACT.Copy).then_inc(free[name], 1)

            def out_unit(i, b, more=True):
                if more:
                    nxt = (i, 1) if b == 0 else (i + 1, 0)
                    for x in range(4):
                        if x < 3:
                            act.wait_ge(ring_used, i * 6 + 32 + 3 * b + x + 1)
                        else:
                            filled(act, "AT"[b] + "1", "out", i)
                        quarter_high(*nxt, x)
                for h in range(HALVES):
                    act.wait_ge(x2_ready, i * 4 + 2 * b + h + 1)
                    a.activation((qs, cgT)[b][:, h, :], xr[:, h, bass.ds(i * 512 + b * UNIT, UNIT)], ACT.Square,
                                 accum_out=sq[:, h, bass.ds(i * 2 + b, 1)]).then_inc(ssq_ready, 1)

            with act.Fori(0, 3) as i:
                act.wait_ge(ssq_ready, i * 4 + 2)
                out_unit(i, 0)
                out_unit(i, 1)
            act.wait_ge(ssq_ready, 3 * 4 + 2)
            out_unit(3, 0)
            out_unit(3, 1, more=False)
            act.wait_ge(ms_ready, 2)
            a.activation(st[:, 4:6], st[:, 2:4], ACT.Sqrt).then_inc(root_ready, 1)
            for q, name in enumerate(("L0", "L1", "T0", "T1")):
                filled(act, name, "spread2")
                r = slice(64 * (q // 2), 64 * (q // 2) + 64)
                a.activation(g2s[r, (q % 2) * 512:(q % 2 + 1) * 512], bank[name][r, :], ACT.Copy)\
                    .then_inc(free[name], 1)
            for n, name in enumerate(("L0", "L1", "T0", "T1", "A0", "A1", "O", "M")):
                h, k = n // 4, (n % 4) * 4
                filled(act, name, "norm2")
                a.activation(h2T[:, k:k + 4, h * P:(h + 1) * P],
                             bank[name].rearrange("p (k t) -> p k t", k=4), ACT.Copy).then_inc(free[name], 1)
            act.wait_ge(h2_ready, 4)
            act.dma_start(gfin, g_norm_final.rearrange("(o d) -> o d", o=1).to_broadcast([P, D])).then_inc(gain_in, 16)
            act.wait_ge(gexp_in, 1)
            a.activation(R("gexp"), R("gexp"), ACT.Exp).then_inc(gexp_ready, 1)
            act.wait_ge(pexp_in, 1)
            a.activation(R("pexp"), R("pexp"), ACT.Exp).then_inc(pexp_ready, 1)

            def mask_evac(t):
                act.wait_ge(ptr_done, t + 1)
                a.activation(pt_lo[0:TILE, :], bank["A1"][0:TILE, 0:S], ACT.Copy)
                a.activation(pt_hi[TILE:P, :], bank["A1"][TILE:P, 0:S], ACT.Copy).then_inc(pt_ready, 1)

            def gather_evac(t):
                act.wait_ge(gather_done, t + 1)
                a.activation(RM[:, 0:1024], pairL[:, :], ACT.Copy).then_inc(hsel_ready, 1)

            def tile(t):
                mask_evac(t)
                act.wait_ge(slot_free["w3"], before("w3", "expert", t) + 2)
                a.activation(gus, bank["A0"].rearrange("p (q j) -> p j q", j=FC), ACT.Copy).then_inc(gus_ready, 1)
                gather_evac(t + 1)
                act.wait_ge(gut_done, t + 1)
                a.activation(sil, bank["A1"].rearrange("p (j s) -> p j s", j=FC)[:, :, 0:TILE], ACT.Silu)\
                    .then_inc(sil_ready, 1)

            gather_evac(0)
            with act.Fori(0, EXPERTS) as e:
                tile(e)
            act.wait_ge(plan_ready, 1)
            n_over = act.value_load(plan_i[0:1, 8:9], min_val=0, max_val=OVER)
            with act.Fori(0, OVER) as o:
                with act.If(o < n_over):
                    tile(o + EXPERTS)
            mask_evac(n_over + EXPERTS)
            for h in range(HALVES):
                act.wait_ge(add_done, (n_over + EXPERTS) * 8 + 6 + 4 * h)
                a.activation(RH[:, h * D:(h + 1) * D], xr[:, h, :], ACT.Square,
                             accum_out=st[:, h:h + 1]).then_inc(fin_ssq, 1)
            act.wait_ge(fin_ms, 1)
            a.activation(st[:, 4:6], st[:, 2:4], ACT.Sqrt).then_inc(fin_root, 1)

        @block.tensor
        def _(pe):
            mm = nc.tensor.matmul
            A0, A1 = bank["A0"], bank["A1"]

            def slot(n, phase, i=0):
                pe.wait_ge(slot_in[f"w{n}"], landed(f"w{n}", phase, i))

            def unit(n):
                return W[:, n, :].rearrange("p (k n) -> p k n", k=KC)

            def project(name, phase, i, pos, n, j, first=False):
                emptied(pe, name, phase, i, pos)
                w = unit(n)
                for k in range(KC):
                    if first:
                        pe.wait_ge(h_ready, k + 1)
                    last = mm(bank[name][:, 0:S], w[:, k, j * P:(j + 1) * P], hT[:, k, :],
                              start=(k == 0), stop=(k == KC - 1))
                return last

            def transposes(src, phase, ready=None):
                for n, name in enumerate(("L0", "L1", "T0", "T1", "A0", "A1", "O", "M")):
                    h, k = n // 4, (n % 4) * 4
                    if ready is not None and k % HC == 0:
                        pe.wait_ge(ready, 2 * h + k // HC + 1)
                    emptied(pe, name, phase)
                    for q in range(4):
                        last = nc.tensor.transpose(bank[name][:, q * P:(q + 1) * P], src[:, h, k + q, :], ident[:, :])
                    last.then_inc(full[name], 1)

            def mod_sums(phase):
                with pe.Fori(0, 2) as i:
                    for b in range(2):
                        name = f"A{b}"
                        emptied(pe, name, phase, i)
                        slot(2 * b, phase, i)
                        w = W[:, 2 * b, :].rearrange("p (k n) -> p k n", k=HC)
                        for k in range(HC):
                            last = mm(bank[name][0:1, :], cT[:, 1, k:k + 1], w[:, k, :], start=(k == 0), stop=False,
                                      skip_group_check=True)
                        last.then_inc(slot_free[f"w{2 * b}"], 1)
                        pe.wait_ge(acc_ready, before("acc", phase, i, b) + 1)
                        mm(bank[name][0:1, 0:256], ones[:, 0:1], acc512[:, b, 0:256], start=False, stop=False,
                           skip_group_check=True).then_inc(slot_free[f"w{2 * b + 1}"], 1)
                        mm(bank[name][0:1, 256:512], ones[:, 0:1], acc512[:, b, 256:512], start=False, stop=True,
                           skip_group_check=True).then_inc(full[name], 1)

            def row_columns(v):
                for k in range(KC):
                    n, at = v * KC + k, v * D + k
                    last = mm(bank["M"][:, n:n + 1], RM[0:1, at:at + D - KC + 1:KC], ones[0:1, 0:1],
                              start=True, stop=True)
                return last

            pe.wait_ge(cact_ready, 1)
            pe.wait_ge(const_ready, 1)
            mod_sums("mod")
            pe.wait_ge(xn_ready, 2)
            transposes(xn, "norm1")
            pe.wait_ge(conv_in, 16)
            emptied(pe, "O", "norm1", 0, 1)
            nc.tensor.transpose(bank["O"][:, 0:TAPS * 8], cstage, ident[0:TAPS * 8, 0:TAPS * 8])\
                .then_inc(full["O"], 1)
            emptied(pe, "M", "kv")
            row_columns(0)
            mod_sums("mod2")

            emptied(pe, "A0", "kv")
            emptied(pe, "A1", "kv")
            row_columns(1).then_inc(full["M"], 1)

            slot(4, "kv")
            for j in range(2):
                last = project(f"A{j}", "kv", 0, 0, 4, j, first=(j == 0))
                last.then_inc(full[f"A{j}"], 1)
            slot(5, "kv")
            for h in range(HALVES):
                emptied(pe, f"A{h}", "kv", 0, 1)
                for k in range(KC):
                    last = mm(bank[f"A{h}"][:, 0:UNIT], hT[:, k, h * P:(h + 1) * P], unit(5)[:, k, :],
                              start=(k == 0), stop=(k == KC - 1))
                last.then_inc(full[f"A{h}"], 1)
            slot(0, "kv")
            emptied(pe, "A0", "kv", 0, 2)
            for k in range(KC):
                last = mm(A0[0:HEAD, 0:S], unit(0)[:, k, 0:HEAD], hT[:, k, :], start=(k == 0), stop=(k == KC - 1))
            last.then_inc(full["A0"], 1)
            emptied(pe, "A1", "kv", 0, 2)
            for h in range(HALVES):
                for k in range(KC):
                    last = mm(A1[:, h * 16:h * 16 + 16], hT[:, k, h * P:(h + 1) * P],
                              unit(0)[:, k, HEAD:HEAD + IDX_HEADS], start=(k == 0), stop=(k == KC - 1))
            last.then_inc(full["A1"], 1)

            pe.wait_ge(ikd_ready, 2)
            with pe.Fori(0, 2) as i:
                for b in range(2):
                    slot(1 + b, "idx", i)
                    for j in range(2):
                        project(f"A{j}", "idx", i, b, 1 + b, j).then_inc(full[f"A{j}"], 1)
                    for j in range(2):
                        filled(pe, f"qs{j}", "idx", i, b)
                        pe.sem_inc(free[f"A{j}"], 1)
                        for h in range(HALVES):
                            emptied(pe, f"L{h}", "idx", i, 2 * b + j)
                            last = mm(bank[f"L{h}"], qs[:, j, h * P:(h + 1) * P], ikd[:, :], start=True, stop=True)
                            last.then_inc(full[f"L{h}"], 1)

            pe.wait_ge(kd_ready, 2)
            with pe.Fori(0, KV) as i:
                def logits(n):
                    j, h = n // 2, n % 2
                    emptied(pe, f"L{n % 2}", "main", i, n // 2)
                    mm(bank[f"L{n % 2}"], qs[:, j, h * P:(h + 1) * P], RH[:, bass.ds(i * 512, 512)],
                       start=True, stop=True).then_inc(full[f"L{n % 2}"], 1)

                def turn(n):
                    filled(pe, f"pb{n}", "main", i)
                    emptied(pe, f"T{n % 2}", "main", i, n // 2)
                    for q in range(4):
                        last = nc.tensor.transpose(bank[f"T{n % 2}"][:, q * P:(q + 1) * P],
                                                   pb[:, n, q * P:(q + 1) * P], ident[:, :])
                    last.then_inc(full[f"T{n % 2}"], 1)

                def values(n):
                    j, h = n // 2, n % 2
                    filled(pe, f"pT{n % 2}", "main", i, n // 2)
                    pe.sem_inc(free[f"T{n % 2}"], 1)
                    for s in range(HALVES):
                        for a in range(2):
                            last = mm(bank["O"][a * HEAD:(a + 1) * HEAD, j * S + h * P:j * S + (h + 1) * P],
                                      vst[:, s, :], pT[:, n % 2, (2 * a + s) * P:(2 * a + s + 1) * P],
                                      start=(s == 0), stop=(s == HALVES - 1), skip_group_check=True)
                            if a == 1 and s == 0:
                                last.then_inc(free[f"pb{n}"], 1)
                    if n == 3:
                        last.then_inc(full["O"], 1)
                    elif n < 2:
                        last.then_inc(pv_done, 1)

                def spread_sum(u):
                    b, n = u % 2, 4 + u % 2
                    pe.wait_ge(acc_ready, before("acc", "main", i, u) + 1)
                    emptied(pe, "M", "main", i, u)
                    mm(bank["M"][:, 0:P], ones[:, :], acc[:, b, 0:P], start=True, stop=True)\
                        .then_inc(slot_free[f"w{n}"], 1)
                    mm(bank["M"][:, P:UNIT], ones[:, :], acc[:, b, P:UNIT], start=True, stop=True)\
                        .then_inc(full["M"], 1)

                def staged(j):
                    filled(pe, f"qs{j}", "main", i)
                    pe.sem_inc(free[f"A{j}"], 1)

                def block_of(n, pos, j):
                    if j == 0:
                        slot(n, "main", i)
                    project(f"A{j}", "main", i, pos, n, j).then_inc(full[f"A{j}"], 1)

                block_of(3, 0, 0)
                block_of(3, 0, 1)
                staged(0)
                block_of(0, 1, 0)
                staged(1)
                logits(0)
                logits(1)
                spread_sum(0)
                block_of(0, 1, 1)
                spread_sum(1)
                block_of(1, 2, 0)
                logits(2)
                logits(3)
                spread_sum(2)
                block_of(1, 2, 1)
                block_of(2, 3, 0)
                turn(0)
                turn(1)
                block_of(2, 3, 1)
                filled(pe, "vst", "main", i)
                emptied(pe, "O", "main", i)
                values(0)
                values(1)
                turn(2)
                turn(3)
                spread_sum(3)
                values(2)
                values(3)

            emptied(pe, "O", "gate")
            for b in range(2):
                emptied(pe, f"A{b}", "gate")
            with pe.Fori(0, 8) as i:
                def branch(name, j, half, src):
                    emptied(pe, name, "gate", i, j)
                    w = unit(2)
                    for q in range(8):
                        last = mm(bank[name][:, 0:S], w[:, 8 * half + q, j * P:(j + 1) * P], src[:, q, :],
                                  start=(q == 0), stop=(q == 7))
                    return last

                def gate_block(n):
                    j, b = n // 2, n % 2
                    emptied(pe, f"A{b}", "gate", i, j)
                    o = bank[f"A{b}"][:, 0:S]
                    for x in range(2):
                        m = 2 * n + x
                        pe.wait_ge(wL_ready, i * 8 + m + 1)
                        for q in range(HC):
                            k = x * HC + q
                            wh, wl = ringH[:, m % 4, q, :], ringL[:, m % 4, q, :]
                            mm(o, wh, hH[:, k, :], start=(k == 0), stop=False)
                            mm(o, wh, hL[:, k, :], start=False, stop=False)
                            last = mm(o, wl, hH[:, k, :], start=False, stop=(k == KC - 1))
                        if x == 0:
                            last.then_inc(ring_used, 1)
                    last.then_inc(full[f"A{b}"], 1)

                slot(2, "gate", i)
                for j in range(2):
                    branch("L0", j, 0, oT).then_inc(full["L0"], 1)
                    branch("L1", j, 1, zT).then_inc(full["L1"], 1)
                    pe.wait_ge(hL_ready, 4)
                    gate_block(2 * j)
                    gate_block(2 * j + 1)
                pe.wait_ge(acc_ready, before("acc", "gate", i) + 1)
                emptied(pe, "M", "gate", i)
                mm(bank["M"][:, 0:P], ones[:, :], acc[:, 0, 0:P], start=True, stop=True)\
                    .then_inc(slot_free["w3"], 1)
                mm(bank["M"][:, P:UNIT], ones[:, :], acc[:, 0, P:UNIT], start=True, stop=True)\
                    .then_inc(full["M"], 1)

            def spread_rows(v, phase, turn):
                for q, name in enumerate(("L0", "L1", "T0", "T1")):
                    emptied(pe, name, phase, 0, turn)
                    mm(bank[name], ident[:, 32 * v:32 * v + 1].to_broadcast([P, P]),
                       modrow[:, q * 512:(q + 1) * 512], start=True, stop=True).then_inc(full[name], 1)

            emptied(pe, "M", "out")
            for turn, v in enumerate((0, 1, 2)):
                spread_rows(v, "spread", turn)

            pe.wait_ge(mT_ready, 16)
            pe.wait_ge(mL_ready, 4)
            with pe.Fori(0, 4) as i:
                for b in range(2):
                    banks = ("A0", "A1") if b == 0 else ("T0", "T1")
                    for name in banks:
                        emptied(pe, name, "out", i)
                    for x in range(4):
                        pe.wait_ge(wL_ready, i * 8 + 64 + 4 * b + x + 1)
                        for h in range(HALVES):
                            o, t = bank[banks[h]][:, 0:UNIT], slice(h * P, (h + 1) * P)
                            for q in range(QC):
                                k = x * QC + q
                                mm(o, mH[:, k, t], quarterH[:, x, q, :], start=(k == 0), stop=False)
                                mm(o, mH[:, k, t], quarterL[:, x, q, :], start=False, stop=False)
                                last = mm(o, mL[:, k, t], quarterH[:, x, q, :], start=False, stop=(k == KC - 1))
                            if x == 3:
                                last.then_inc(full[banks[h]], 1)
                        if x < 3:
                            last.then_inc(ring_used, 1)
                    pe.wait_ge(acc_ready, before("acc", "out", i, b) + 1)
                    emptied(pe, "M", "out", i, b)
                    mm(bank["M"][:, 0:P], ones[:, :], acc[:, b, 0:P], start=True, stop=True)\
                        .then_inc(slot_free[f"w{2 + b}"], 1)
                    mm(bank["M"][:, P:UNIT], ones[:, :], acc[:, b, P:UNIT], start=True, stop=True)\
                        .then_inc(full["M"], 1)
            emptied(pe, "M", "norm2")
            spread_rows(3, "spread2", 0)

            transposes(h2, "norm2", h2_ready)
            emptied(pe, "A0", "route")
            for name in ("L0", "L1", "T0", "T1"):
                emptied(pe, name, "route")
            for name in ("A1", "O", "M"):
                emptied(pe, name, "route")
            pe.wait_ge(router_in, 16 * 4)
            for h in range(HALVES):
                for k in range(KC):
                    last = mm(A0[:, 64 * h:64 * h + GROUPS + EXPERTS], h2T[:, k, h * P:(h + 1) * P], wr[:, k, :],
                              start=(k == 0), stop=(k == KC - 1))
            last.then_inc(full["A0"], 1)
            pe.wait_ge(choice_ready, 1)
            m0, m1 = R("choice")[:, 0, :], R("choice")[:, 1, :]
            mm(A1[:, 0:32], tri[:, :], m0, start=True, stop=True)
            mm(A1[:, 32:64], tri[:, :], m1, start=True, stop=False)
            mm(A1[:, 32:64], ones[:, :], m0, start=False, stop=True)
            mm(A1[:, 64:96], ones[:, :], m0, start=True, stop=False)
            mm(A1[:, 64:96], ones[:, :], m1, start=False, stop=True).then_inc(full["A1"], 1)

            def gather(t, chunks=range(KC)):
                pe.wait_ge(pg_ready, t + 1)
                for k in chunks:
                    for h in range(HALVES):
                        last = mm(pairL[:, k * TILE:(k + 1) * TILE], h2[:, h, k, :], pg[:, h, :],
                                  start=(h == 0), stop=(h == HALVES - 1))
                return last

            def combine_mask(t):
                pe.wait_ge(pw_ready, t + 1)
                pe.wait_ge(act_ready, t + 1)
                for h in range(HALVES):
                    last = nc.tensor.transpose(A1[:, h * P:(h + 1) * P], pw[:, h, :], ident[:, :])
                last.then_inc(ptr_done, 1)

            def combine(t):
                pe.wait_ge(pt_ready, t + 1)
                pe.wait_ge(y_ready, t + 1)
                for n in range(8):
                    h, q = n // 4, n % 4
                    pe.wait_ge(add_done, t * 8 + n + 1)
                    mm(bank["OM"[n % 2]], (pt_lo if q < 2 else pt_hi)[:, h * P:(h + 1) * P],
                       ysb[:, (q % 2) * 512:(q % 2 + 1) * 512], start=True, stop=True).then_inc(cmb_done, 1)

            def tile(t, more=None):
                combine_mask(t)
                pe.wait_ge(hsel_ready, t + 1)
                pe.wait_ge(gus_ready, t + 1)
                for n in range(4):
                    slot(n, "expert", t)
                    w = W[:, n, :].rearrange("p (g k f) -> p g k f", g=2, k=QC)
                    for k in range(QC):
                        ks = n * QC + k
                        for g in range(2):
                            last = mm(A0[g * TILE:(g + 1) * TILE, :], hsel[:, ks, :], w[:, g, k, :],
                                      start=(ks == 0), stop=(ks == KC - 1), skip_group_check=True)
                    last.then_inc(slot_free[f"w{n}"], 1)
                if more is None:
                    gather(t + 1).then_inc(gather_done, 1)
                else:
                    with pe.If(more):
                        gather(t + 1, range(KC - 1))
                    gather(t + 1, range(KC - 1, KC)).then_inc(gather_done, 1)
                pe.wait_ge(gus_ready, t + 2)
                pe.wait_ge(pt_ready, t + 1)
                for j in range(FC):
                    last = nc.tensor.transpose(A1[:, j * P:(j + 1) * P], gus[:, j, :], ident[:, :])
                last.then_inc(gut_done, 1)
                combine(t)
                pe.wait_ge(act_ready, t + 2)
                for n in range(2):
                    slot(4 + n, "expert", t)
                    w = W[:, 4 + n, :].rearrange("p (j g d) -> p j g d", j=2, g=2)
                    for j in range(2):
                        js = 2 * n + j
                        for q in range(2):
                            for g in range(2):
                                last = mm(pairT[g * TILE:(g + 1) * TILE, q * 512:(q + 1) * 512], actT[:, js, :],
                                          w[:, j, g, q * 512:(q + 1) * 512], start=(js == 0), stop=(js == FC - 1),
                                          skip_group_check=True)
                    last.then_inc(slot_free[f"w{4 + n}"], 1)

            pe.wait_ge(pg_ready, 1)
            gather(0).then_inc(gather_done, 1)
            emptied(pe, "A1", "expert")
            with pe.Fori(0, EXPERTS) as e:
                tile(e)
            pe.wait_ge(plan_ready, 1)
            n_over = pe.value_load(plan_i[0:1, 8:9], min_val=0, max_val=OVER)
            with pe.Fori(0, OVER) as o:
                with pe.If(o < n_over):
                    tile(o + EXPERTS, more=o + 1 < n_over)
            combine_mask(n_over + EXPERTS)
            combine(n_over + EXPERTS)

        @block.vector
        def _(dve):
            v = nc.vector
            place = [None, 0]

            def enter(phase, i=0):
                place[:] = [before("v", phase, i), 0]

            def leave(phase):
                want = {n: e.get("v", 0) for n, _, e in PLAN}[phase]
                assert place[1] == want, (phase, place[1], want)

            def link(ins):
                place[1] += 1
                ins.then_inc(chain, 1)
                dve.wait_ge(chain, place[0] + place[1])

            def inverse_root(col, ms_sem, root_sem, turn):
                v.tensor_scalar(st[:, 2:4], st[:, 0:2], 1.0 / D, EPS, ALU.mult, ALU.add).then_inc(ms_sem, 1)
                dve.wait_ge(root_sem, turn)
                link(v.reciprocal(st[:, 6:8], st[:, 4:6]))
                link(v.tensor_tensor(st[:, 4:6], st[:, 6:8], st[:, 6:8], ALU.mult))
                link(v.tensor_tensor(st[:, 4:6], st[:, 4:6], st[:, 2:4], ALU.mult))
                link(v.tensor_scalar(st[:, 4:6], st[:, 4:6], -0.5, 1.5, ALU.mult, ALU.add))
                link(v.tensor_tensor(st[:, 6:8], st[:, 6:8], st[:, 4:6], ALU.mult))

            def weigh(dst, w, chunks, k0):
                n = len(chunks)
                for q, k in enumerate(chunks):
                    cs = cT[:, 1, k:k + 1]
                    if q == 0:
                        link(v.tensor_scalar(dst, w[:, k - k0, :], cs, None, ALU.mult))
                    else:
                        ins = v.scalar_tensor_tensor(out=dst, in0=w[:, k - k0, :], scalar=cs, in1=dst,
                                                     op0=ALU.mult, op1=ALU.add)
                        if q < n - 1:
                            link(ins)
                        else:
                            ins.then_inc(acc_ready, 1)

            def mod_part(phase):
                with dve.Fori(0, 2) as i:
                    enter(phase, i)
                    for b in range(2):
                        dve.wait_ge(slot_in[f"w{2 * b + 1}"], landed(f"w{2 * b + 1}", phase, i))
                        emptied(dve, f"A{b}", phase, i)
                        weigh(acc512[:, b, :], W[:, 2 * b + 1, :].rearrange("p (k n) -> p k n", k=HC),
                              range(HC, KC), HC)
                    leave(phase)

            dve.wait_ge(cact_ready, 1)
            mod_part("mod")
            enter("norm1")
            dve.wait_ge(ssq_ready, 2)
            inverse_root(0, ms_ready, root_ready, 1)
            for h in range(HALVES):
                v.tensor_scalar(xn[:, h, :, :], xr[:, h, :].rearrange("p (q k) -> p k q", k=KC),
                                st[:, 6 + h:7 + h], None, ALU.mult).then_inc(xn_ready, 1)
            leave("norm1")

            mod_part("mod2")
            enter("kv")
            dve.wait_ge(small_in, 16 * 3)
            for name in ("L0", "L1", "T0", "T1"):
                emptied(dve, name, "idx" if name[0] == "L" else "main")
            emptied(dve, "O", "main")
            filled(dve, "M", "kv")
            v.tensor_tensor(modT[:, :, :], bank["M"][:, 0:2 * KC].rearrange("p (v k) -> p v k", v=2),
                            colb[:, 0:2, :], ALU.add).then_inc(free["M"], 1)
            dve.wait_ge(free["M"], before("M", "kv") + 2)
            link(v.tensor_scalar(modT[:, 1, :], modT[:, 1, :], 1.0, None, ALU.add))
            link(v.tensor_tensor(modT[:, 1, :], modT[:, 1, :], colb[:, 2, :], ALU.mult))
            for k in range(KC):
                v.tensor_scalar(hT[:, k, :], hT[:, k, :], modT[:, 1, k:k + 1], modT[:, 0, k:k + 1],
                                ALU.mult, ALU.add).then_inc(h_ready, 1)
            dve.wait_ge(const_ready, 12)
            for b in range(2):
                filled(dve, f"A{b}", "kv")
                if b == 1:
                    dve.sem_inc(slot_free["w4"], 1)
                for a in range(2):
                    src = bank[f"A{b}"][a * HEAD:(a + 1) * HEAD, 0:S]
                    v.tensor_copy(kd[0:HEAD, 2 * b + a, 0:S], src)
                    last = v.tensor_copy(kd[HEAD:P, 2 * b + a, S:2 * S], src)
                last.then_inc(kd_ready, 1)
                dve.wait_ge(kd_ready, b + 1)
                dve.sem_inc(free[f"A{b}"], 1)
            filled(dve, "A1", "kv", 0, 2)
            dve.sem_inc(slot_free["w0"], 1)
            v.tensor_scalar(iw[:, :, :], bank["A1"][:, 0:32].rearrange("p (h e) -> p h e", h=2),
                            HEAD ** -0.5 * IDX_HEADS ** -0.5, None, ALU.mult).then_inc(iw_ready, 1)
            dve.wait_ge(iw_ready, 1)
            dve.sem_inc(free["A1"], 1)
            leave("kv")

            with dve.Fori(0, 2) as i:
                enter("idx", i)
                for b in range(2):
                    for j in range(2):
                        for h in range(HALVES):
                            filled(dve, f"rel{h}", "idx", i, 2 * b + j)
                            dve.sem_inc(free[f"L{h}"], 1)
                            for a in range(2):
                                ins = v.scalar_tensor_tensor(
                                    out=score[:, h, :], in0=rel[:, h, a * S:(a + 1) * S],
                                    scalar=iw[:, h, bass.ds(i * 8 + 4 * b + 2 * j + a, 1)],
                                    in1=score[:, h, :], op0=ALU.mult, op1=ALU.add)
                                if a == 0:
                                    link(ins)
                                else:
                                    ins.then_inc(free[f"rel{h}"], 1)
                                    dve.wait_ge(free[f"rel{h}"], before(f"rel{h}", "idx", i, 2 * b + j) + 2)
                leave("idx")
            enter("topk")
            for h in range(HALVES):
                link(v.tensor_tensor(work[:, h, :], score[:, h, :], amask[:, h, :], ALU.add))
            for r in range(TOPK // 8):
                for h in range(HALVES):
                    cur = work if r == 0 else score
                    link(v.max(st[:, 8 + 8 * h:16 + 8 * h], cur[:, h, :]))
                    link(v.match_replace(score[:, h, :], st[:, 8 + 8 * h:16 + 8 * h], cur[:, h, :], NEG))
            for h in range(HALVES):
                link(v.tensor_tensor(work[:, h, :], work[:, h, :], score[:, h, :], ALU.is_equal))
                link(v.tensor_scalar(amask[:, h, :], work[:, h, :], NEG, None, ALU.mult))
            leave("topk")

            def modulation(n, b, phase, i, pos=None):
                dve.wait_ge(slot_in[f"w{n}"], landed(f"w{n}", phase, i, pos))
                weigh(acc[:, b, :], W[:, n, :].rearrange("p (k n) -> p k n", k=KC), range(KC), 0)

            def mod_row(r, phase, i, pos, at):
                filled(dve, "M", phase, i, pos)
                o = modrow[r:r + 1, bass.ds(at, UNIT)]
                v.tensor_tensor(o, bank["M"][r:r + 1, 0:UNIT], o, ALU.add).then_inc(free["M"], 1)

            dve.wait_ge(modrow_in, 64)
            with dve.Fori(0, KV) as i:
                enter("main", i)

                def masked(n):
                    h = n % 2
                    filled(dve, f"L{n % 2}", "main", i, n // 2)
                    emptied(dve, f"pb{n}", "main", i)
                    p3 = pb[:, n, :].rearrange("p (a s) -> p a s", a=2)
                    v.scalar_tensor_tensor(out=p3, in0=bank[f"L{n % 2}"].rearrange("p (a s) -> p a s", a=2),
                                           scalar=HEAD ** -0.5,
                                           in1=amask[:, h, :].unsqueeze(1).to_broadcast([P, 2, S]),
                                           op0=ALU.mult, op1=ALU.add).then_inc(free[f"L{n % 2}"], 1)
                    dve.wait_ge(free[f"L{n % 2}"], before(f"L{n % 2}", "main", i, n // 2) + 2)
                    link(v.tensor_reduce(st[:, 24 + 2 * n:26 + 2 * n], p3, AX, ALU.max))
                    v.tensor_scalar(st[:, 8 + 2 * n:10 + 2 * n], st[:, 24 + 2 * n:26 + 2 * n], -1.0, None,
                                    ALU.mult).then_inc(lg_ready, 1)

                def normalise(n):
                    dve.wait_ge(exp_ready, i * 8 + 2 * n + 2)
                    link(v.reciprocal(st[:, 24 + 2 * n:26 + 2 * n], st[:, 16 + 2 * n:18 + 2 * n]))
                    for a in range(2):
                        o = pb[:, n, a * S:(a + 1) * S]
                        last = v.tensor_scalar(o, o, st[:, 24 + 2 * n + a:25 + 2 * n + a], None, ALU.mult)
                    last.then_inc(full[f"pb{n}"], 1)

                def conv(j):
                    filled(dve, f"A{j}", "main", i, 2)
                    if j == 1:
                        dve.sem_inc(slot_free["w1"], 1)
                    filled(dve, f"cg{j}", "main", i)
                    v.tensor_tensor(uT[:, j, 2:], bank[f"A{j}"][:, 0:S], cgT[:, j, :], ALU.mult)\
                        .then_inc(free[f"A{j}"], 1)
                    dve.wait_ge(free[f"A{j}"], before(f"A{j}", "main", i, 2) + 2)
                    w = [convc[:, q, bass.ds(i * 2 + j, 1)] for q in range(TAPS)]
                    v.tensor_scalar(yb[:, j, :], uT[:, j, 2:2 + S], w[2], None, ALU.mult)\
                        .then_inc(free[f"cg{j}"], 1)
                    dve.wait_ge(free[f"cg{j}"], before(f"cg{j}", "main", i) + 2)
                    for q in (1, 0):
                        link(v.scalar_tensor_tensor(out=yb[:, j, :], in0=uT[:, j, q:q + S], scalar=w[q],
                                                    in1=yb[:, j, :], op0=ALU.mult, op1=ALU.add))

                modulation(4, 0, "main", i, 0)
                modulation(5, 1, "main", i, 0)
                masked(0)
                masked(1)
                mod_row(0, "main", i, 0, i * 512)
                mod_row(0, "main", i, 1, i * 512 + UNIT)
                modulation(4, 0, "main", i, 1)
                conv(0)
                masked(2)
                masked(3)
                normalise(0)
                normalise(1)
                mod_row(32, "main", i, 2, i * 512)
                conv(1)
                normalise(2)
                normalise(3)
                modulation(5, 1, "main", i, 1)
                for j in range(2):
                    filled(dve, f"A{j}", "main", i, 3)
                    if j == 1:
                        dve.sem_inc(slot_free["w2"], 1)
                    v.tensor_tensor(RB[:, bass.ds(i * 512 + 2048 + j * S, S)], bank[f"A{j}"][:, 0:S],
                                    yb[:, j, :], ALU.mult).then_inc(free[f"A{j}"], 1)
                mod_row(32, "main", i, 3, i * 512 + UNIT)
                leave("main")

            for q in range(4):
                dve.wait_ge(hH_ready, q + 1)
                v.tensor_tensor(hL[:, 4 * q:4 * q + 4, :], hT[:, 4 * q:4 * q + 4, :],
                                hH[:, 4 * q:4 * q + 4, :].bitcast(F32), ALU.subtract).then_inc(hL_ready, 1)

            with dve.Fori(0, 8) as i:
                enter("gate", i)

                def merge(j):
                    for b in range(2):
                        filled(dve, f"L{b}", "gate", i, j)
                        filled(dve, f"sg{b}", "gate", i, j)
                        dve.sem_inc(free[f"A{b}"], 1)
                        v.tensor_tensor(yb[:, b, :], bank[f"L{b}"][:, 0:S], qs[:, b, :], ALU.mult)\
                            .then_inc(free[f"L{b}"], 1)
                        dve.wait_ge(free[f"L{b}"], before(f"L{b}", "gate", i, j) + 2)
                        dve.sem_inc(free[f"sg{b}"], 1)
                    v.tensor_tensor(RM[:, bass.ds(i * 512 + j * S, S)], yb[:, 0, :], yb[:, 1, :], ALU.add)\
                        .then_inc(mT_ready, 1)
                    dve.wait_ge(mT_ready, i * 2 + j + 1)

                merge(0)
                modulation(3, 0, "gate", i)
                merge(1)
                mod_row(64, "gate", i, 0, i * UNIT)
                leave("gate")

            for q in range(4):
                dve.wait_ge(mH_ready, q + 1)
                v.tensor_tensor(mL[:, 4 * q:4 * q + 4, :], mT[:, 4 * q:4 * q + 4, :],
                                mH[:, 4 * q:4 * q + 4, :].bitcast(F32), ALU.subtract).then_inc(mL_ready, 1)

            for name in ("L0", "L1", "T0", "T1"):
                emptied(dve, name, "spread", 0, 1)
            def out_run(i):
                enter("out", i)
                for b in range(2):
                    modulation(2 + b, b, "out", i)
                    at = i * 512 + b * UNIT
                    for h in range(HALVES):
                        name = "AT"[b] + str(h)
                        filled(dve, name, "out", i)
                        v.tensor_tensor(yb[:, h, :], bank[name][:, 0:UNIT], g1B[:, bass.ds(at, UNIT)],
                                        ALU.mult).then_inc(free[name], 1)
                        dve.wait_ge(free[name], before(name, "out", i) + 2)
                        o = xr[:, h, bass.ds(at, UNIT)]
                        v.tensor_tensor(o, o, yb[:, h, :], ALU.add).then_inc(x2_ready, 1)
                        dve.wait_ge(x2_ready, i * 4 + 2 * b + h + 1)
                    mod_row(96, "out", i, b, at)
                leave("out")

            with dve.Fori(0, 3) as i:
                out_run(i)
            dve.wait_ge(fgain_in, 16)
            for name in ("L0", "L1"):
                emptied(dve, name, "spread2")
            for name in ("T0", "T1"):
                emptied(dve, name, "out")
            v.scalar_tensor_tensor(out=A2B, in0=A2B, scalar=1.0, in1=fgain, op0=ALU.add, op1=ALU.mult)\
                .then_inc(gain2_ready, 1)
            out_run(3)
            dve.wait_ge(gain2_ready, 1)

            enter("norm2")
            dve.wait_ge(ssq_ready, 2 + 16)
            link(v.tensor_reduce(st[:, 0:2], sq[:, :, :], AX, ALU.add))
            inverse_root(0, ms_ready, root_ready, 2)
            for name in ("L0", "L1"):
                emptied(dve, name, "spread2")
            for h in range(HALVES):
                for c in range(2):
                    ks = slice(c * HC, (c + 1) * HC)
                    gain2, shift2, x2 = (t.rearrange("p (q k) -> p k q", k=KC)[:, ks, :]
                                         for t in (A2B, B2B, xr[:, h, :]))
                    link(v.scalar_tensor_tensor(out=h2[:, h, ks, :], in0=x2, scalar=st[:, 6 + h:7 + h], in1=gain2,
                                                op0=ALU.mult, op1=ALU.mult))
                    v.tensor_tensor(h2[:, h, ks, :], h2[:, h, ks, :], shift2, ALU.add).then_inc(h2_ready, 1)
            leave("norm2")

            def gather_mask(t):
                for h in range(HALVES):
                    last = v.tensor_scalar(pg[:, h, :], iota[:, :], cols[:, h, bass.ds(t + 1, 1)], None, ALU.is_equal)
                last.then_inc(pg_ready, 1)

            enter("route")
            dve.wait_ge(const_ready, 12)
            filled(dve, "A0", "route")
            lg, gx, zs = R("lg"), R("gexp"), R("zs")
            A3 = bank["A0"][:, 0:P].rearrange("p (h n) -> p h n", h=2)[:, :, 0:GROUPS + EXPERTS]
            link(v.tensor_tensor(lg, A3, gb[:, :].unsqueeze(1).to_broadcast([P, 2, GROUPS + EXPERTS]), ALU.add))
            gl, el = lg[:, :, 0:GROUPS], lg[:, :, GROUPS:]

            def wide(t, n):
                return t.to_broadcast([P, 2, n])

            def first_max(dst, src, n, m):
                link(v.tensor_reduce(m, src, AX, ALU.max))
                m3 = wide(m.rearrange("p (h o) -> p h o", o=1), n)
                link(v.tensor_tensor(dst, src, m3, ALU.is_equal))
                link(v.tensor_tensor(dst, dst, R("down")[:, EXPERTS - n:].unsqueeze(1).to_broadcast([P, 2, n]),
                                     ALU.mult))
                link(v.tensor_reduce(R("t2"), dst, AX, ALU.max))
                link(v.tensor_tensor(dst, wide(R("t2").rearrange("p (h o) -> p h o", o=1), n),
                                     R("down")[:, EXPERTS - n:].unsqueeze(1).to_broadcast([P, 2, n]), ALU.is_equal))

            link(v.tensor_scalar(R("down"), eidx[:, :], -1.0, float(EXPERTS), ALU.mult, ALU.add))
            gm = R("gm")
            first_max(R("gsel"), gl, GROUPS, gm)
            v.tensor_tensor(gx, gl, wide(gm.rearrange("p (h o) -> p h o", o=1), GROUPS), ALU.subtract)\
                .then_inc(gexp_in, 1)
            dve.wait_ge(gexp_ready, 1)
            link(v.tensor_reduce(zs, gx, AX, ALU.add))
            link(v.reciprocal(R("pgr"), zs))
            e4 = el.rearrange("p h (g e) -> p h g e", g=GROUPS)
            gs4 = R("gsel")
            val = R("val")
            for h in range(HALVES):
                v4 = val[:, h, :].rearrange("p (g e) -> p g e", g=GROUPS)
                s4 = gs4[:, h, :].unsqueeze(2).to_broadcast([P, GROUPS, EPG])
                link(v.tensor_tensor(v4, e4[:, h], s4, ALU.mult))
                link(v.tensor_scalar(R("t4"), gs4[:, h, :], -1.0, -NEG, ALU.add, ALU.mult))
                link(v.tensor_tensor(v4, v4, R("t4").unsqueeze(2).to_broadcast([P, GROUPS, EPG]), ALU.add))
            first_max(R("one"), val, EXPERTS, R("m1"))
            link(v.scalar_tensor_tensor(out=R("val2"), in0=R("one"), scalar=1.1 * NEG, in1=val,
                                        op0=ALU.mult, op1=ALU.add))
            first_max(R("two"), R("val2"), EXPERTS, R("m2"))
            v.tensor_tensor(R("pexp"), R("m2"), R("m1"), ALU.subtract).then_inc(pexp_in, 1)
            link(v.tensor_tensor(R("choice"), R("one"), R("two"), ALU.add))
            v.tensor_copy(R("t2"), R("m1")).then_inc(choice_ready, 1)
            dve.wait_ge(pexp_ready, 1)
            link(v.tensor_scalar(R("p1"), R("pexp"), 1.0, None, ALU.add))
            link(v.reciprocal(R("p1"), R("p1")))
            link(v.tensor_tensor(R("p1"), R("p1"), R("pgr"), ALU.mult))
            link(v.tensor_tensor(R("p2"), R("p1"), R("pexp"), ALU.mult))
            link(v.tensor_tensor(R("val"), R("one"), wide(R("p1").rearrange("p (h o) -> p h o", o=1), EXPERTS),
                                 ALU.mult))
            link(v.tensor_tensor(R("val2"), R("two"), wide(R("p2").rearrange("p (h o) -> p h o", o=1), EXPERTS),
                                 ALU.mult))
            link(v.tensor_tensor(cwc[:, :, 1:1 + EXPERTS], R("val"), R("val2"), ALU.add))
            filled(dve, "A1", "route")
            rk = cols[:, :, 1:1 + EXPERTS]
            link(v.scalar_tensor_tensor(out=rk, in0=bank["A1"][:, 0:64].rearrange("p (h e) -> p h e", h=2),
                                        scalar=1000.0, in1=R("choice"), op0=ALU.add, op1=ALU.mult))
            link(v.tensor_scalar(rk, rk, -1000.0, None, ALU.add))
            gather_mask(0)
            dve.sem_inc(add_done, 2)
            cnt = bank["A1"][:, 64:96]
            link(v.tensor_scalar(R("ov"), cnt, float(TILE), None, ALU.is_gt))
            for b in range(2, S // TILE):
                ins = v.scalar_tensor_tensor(out=R("ov"), in0=cnt, scalar=float(b * TILE), in1=R("ov"),
                                             op0=ALU.is_gt, op1=ALU.add)
                if b < S // TILE - 1:
                    link(ins)
                else:
                    ins.then_inc(free["A1"], 1)
                    dve.wait_ge(free["A1"], before("A1", "expert") + 1)
            link(v.tensor_tensor_scan(R("incl"), ones[:, 0:EXPERTS], R("ov"), 0.0, ALU.mult, ALU.add))
            link(v.tensor_tensor(R("excl"), R("incl"), R("ov"), ALU.subtract))
            o7 = eidx[:, 0:OVER].unsqueeze(2).to_broadcast([P, OVER, EXPERTS])
            in7 = R("incl").unsqueeze(1).to_broadcast([P, OVER, EXPERTS])
            ex7 = R("excl").unsqueeze(1).to_broadcast([P, OVER, EXPERTS])
            own, first, tmp7 = R("own"), R("first"), R("tmp7")
            link(v.tensor_tensor(own, in7, o7, ALU.is_gt))
            link(v.tensor_tensor(first, ex7, o7, ALU.is_le))
            link(v.tensor_tensor(own, own, first, ALU.mult))
            link(v.tensor_tensor(first, o7, ex7, ALU.subtract))
            link(v.tensor_scalar(first, first, 1.0, float(TILE), ALU.add, ALU.mult))
            for h in range(HALVES):
                rk7 = cols[:, h, 1:1 + EXPERTS].unsqueeze(1).to_broadcast([P, OVER, EXPERTS])
                cw7 = cwc[:, h, 1:1 + EXPERTS].unsqueeze(1).to_broadcast([P, OVER, EXPERTS])
                link(v.tensor_tensor(tmp7, rk7, first, ALU.subtract))
                link(v.tensor_tensor(tmp7, tmp7, own, ALU.mult))
                link(v.tensor_reduce(cols[:, h, 1 + EXPERTS:1 + EXPERTS + OVER], tmp7, AX, ALU.add))
                link(v.tensor_tensor(tmp7, cw7, own, ALU.mult))
                link(v.tensor_reduce(cwc[:, h, 1 + EXPERTS:1 + EXPERTS + OVER], tmp7, AX, ALU.add))
            link(v.tensor_tensor(tmp7, own, eidx[:, 0:EXPERTS].unsqueeze(1).to_broadcast([P, OVER, EXPERTS]),
                                 ALU.mult))
            link(v.tensor_reduce(R("eid"), tmp7, AX, ALU.add))
            link(v.tensor_copy(plan_i[0:1, 0:OVER], R("eid")[0:1, :]))
            v.tensor_copy(plan_i[0:1, 8:9], R("incl")[0:1, EXPERTS - 1:EXPERTS]).then_inc(plan_ready, 1)
            leave("route")

            def adds(t, turns=range(8)):
                if 0 in turns:
                    dve.wait_ge(add_done, t * 8 + 2)
                for n in turns:
                    dve.wait_ge(cmb_done, t * 8 + n + 1)
                    h, q = n // 4, n % 4
                    o = xr[:, h, q * 512:(q + 1) * 512]
                    v.tensor_tensor(o, o, bank["OM"[n % 2]], ALU.add).then_inc(add_done, 1)

            def tile(t):
                dve.wait_ge(gather_done, t + 1)
                gather_mask(t + 1)
                dve.wait_ge(ptr_done, t + 1)
                for h in range(HALVES):
                    last = v.tensor_scalar(pw[:, h, :].rearrange("p (a s) -> p a s", a=2),
                                           iota[:, :].unsqueeze(1).to_broadcast([P, 2, TILE]),
                                           cols[:, h, bass.ds(t + 1, 1)], cwc[:, h, bass.ds(t + 1, 1)],
                                           ALU.is_equal, ALU.mult)
                last.then_inc(pw_ready, 1)
                adds(t, range(0, 2))
                dve.wait_ge(sil_ready, t + 1)
                v.tensor_tensor(actT, sil, bank["A1"].rearrange("p (j s) -> p j s", j=FC)[:, :, TILE:], ALU.mult)\
                    .then_inc(act_ready, 1)
                adds(t, range(2, 8))
                dve.wait_ge(slot_free["w5"], before("w5", "expert", t) + 2)
                v.tensor_tensor(ysb, pairT[:, :], g2s, ALU.mult).then_inc(y_ready, 1)

            with dve.Fori(0, EXPERTS) as e:
                tile(e)
            dve.wait_ge(plan_ready, 1)
            n_over = dve.value_load(plan_i[0:1, 8:9], min_val=0, max_val=OVER)
            with dve.Fori(0, OVER) as o:
                with dve.If(o < n_over):
                    tile(o + EXPERTS)
            adds(n_over + EXPERTS)

            dve.wait_ge(fin_ssq, 2)
            enter("last")
            inverse_root(0, fin_ms, fin_root, 1)
            leave("last")
            dve.wait_ge(gain_in, 16)
            for n in range(4):
                h, c = n // 2, slice(n % 2 * (D // 2), (n % 2 + 1) * (D // 2))
                v.scalar_tensor_tensor(out=xr[:, h, c], in0=xr[:, h, c], scalar=st[:, 6 + h:7 + h], in1=gfin[:, c],
                                       op0=ALU.mult, op1=ALU.mult).then_inc(fin_ready, 1)


NAMES = ["x", "c", "w_ada", "b_ada", "g_norm_mix", "w_in", "conv_w", "w_a_up", "w_b_out", "w_o", "g_norm_ffn",
         "w_rg", "b_rg", "w_re", "b_re", "w_e_gate", "w_e_up", "w_e_down", "g_norm_final"]


def kernel(**inputs):
    import numpy as np
    import concourse.bacc as bacc
    from concourse.bass_utils import run_bass_kernel_spmd

    nc = bacc.Bacc("TRN2", target_bir_lowering=False, num_devices=1)
    arrays, args = {}, []
    for name in NAMES:
        a = np.ascontiguousarray(inputs[name])
        arrays[f"in_{name}"] = a
        args.append(nc.dram_tensor(f"in_{name}", a.shape, mybir.dt.from_np(a.dtype), kind="ExternalInput").ap())
    args.append(nc.dram_tensor("out_x", (1, S, D), F32, kind="ExternalOutput").ap())
    block_kernel(nc, *args)
    r = run_bass_kernel_spmd(nc, [arrays], core_ids=[0])
    return r.results[0]["out_x"]
```
